# Optimizing a Trainium2 kernel written in Bass

```python
import jax, jax.numpy as jnp
from jax import lax
import numpy as np

D_MODEL = 1024
BATCH = 1
SEQ = 256
DEPTH = 2

D_MIX = D_MODEL
RET_HEADS = 4
RET_HEAD_DIM = 128
RET_WIDTH = RET_HEADS * RET_HEAD_DIM
RET_CHUNK = 128
GDN_HEADS = 4
GDN_HEAD_DIM = 128
GDN_WIDTH = GDN_HEADS * GDN_HEAD_DIM
GDN_CHUNK = 64
CONV_K = 5
D_FF = 2816
MEM_LEN = 256
XATTN_HEADS = 4
XATTN_HEAD_DIM = D_MODEL // XATTN_HEADS
ROPE_BASE = 10000.0
NORM_EPS = 1e-6
N_SUBLAYERS = 4
IN_COLS = 4 * RET_WIDTH + 4 * GDN_WIDTH + 4 * GDN_HEADS
IN_SPLITS = (RET_WIDTH, 2 * RET_WIDTH, 3 * RET_WIDTH, 4 * RET_WIDTH,
             4 * RET_WIDTH + 3 * GDN_WIDTH, 4 * RET_WIDTH + 4 * GDN_WIDTH,
             4 * RET_WIDTH + 4 * GDN_WIDTH + 2 * GDN_HEADS)


def rms_norm(x, w):
    xf = x.astype(jnp.float32)
    y = xf * lax.rsqrt(jnp.mean(xf * xf, axis=-1, keepdims=True) + NORM_EPS)
    return (y * w.astype(jnp.float32)).astype(x.dtype)

def swiglu(u, w_gate, w_up, w_down):
    return (jax.nn.silu(u @ w_gate) * (u @ w_up)) @ w_down

def rotary_tables(positions):
    inv_freq = ROPE_BASE ** (-jnp.arange(0, RET_HEAD_DIM, 2, dtype=jnp.float32) / RET_HEAD_DIM)
    ang = positions.astype(jnp.float32)[..., None] * inv_freq
    return jnp.cos(ang)[:, :, None, :], jnp.sin(ang)[:, :, None, :]

def rotary(x, cos, sin):
    half = x.shape[-1] // 2
    x1, x2 = x[..., :half], x[..., half:]
    return jnp.concatenate([x1 * cos - x2 * sin, x1 * sin + x2 * cos], axis=-1)

def flip_seq(t):
    return jnp.flip(t, axis=2)

def retention_direction(q, k, v, log_gamma, strict):
    b, h, s, d = q.shape
    n = s // RET_CHUNK
    q, k, v = (t.reshape(b, h, n, RET_CHUNK, d) for t in (q, k, v))
    pos = jnp.arange(RET_CHUNK, dtype=jnp.float32)
    rel = pos[:, None] - pos[None, :]
    mask = rel > 0 if strict else rel >= 0
    lg = log_gamma[:, None, None]
    dmat = jnp.where(mask, jnp.exp(jnp.where(mask, rel, 0.0) * lg), 0.0)
    scores = jnp.einsum('bhnid,bhnjd->bhnij', q, k) * dmat[:, None]
    o_intra = jnp.einsum('bhnij,bhnje->bhnie', scores, v)
    lgv = log_gamma[:, None]
    k_dec = k * jnp.exp((RET_CHUNK - 1.0 - pos) * lgv)[:, None, :, None]
    chunk_kv = jnp.einsum('bhncd,bhnce->bhnde', k_dec, v)
    chunk_decay = jnp.exp(RET_CHUNK * log_gamma)[None, :, None, None]

    def step(state, kv_c):
        return state * chunk_decay + kv_c, state

    _, prev = lax.scan(step, jnp.zeros((b, h, d, d), q.dtype), jnp.moveaxis(chunk_kv, 2, 0))
    prev = jnp.moveaxis(prev, 0, 2)
    q_dec = q * jnp.exp((pos + 1.0) * lgv)[:, None, :, None]
    o_inter = jnp.einsum('bhncd,bhnde->bhnce', q_dec, prev)
    return (o_intra + o_inter).reshape(b, h, s, d)

def retention_group(rq, rk, rv, rg, cos, sin, log_gamma):
    b, s, _ = rq.shape
    heads = lambda t: t.reshape(b, s, RET_HEADS, RET_HEAD_DIM)
    q = rotary(heads(rq), cos, sin)
    k = rotary(heads(rk), cos, sin) * RET_HEAD_DIM ** -0.5
    v = heads(rv)
    q, k, v = (jnp.swapaxes(t, 1, 2).astype(jnp.float32) for t in (q, k, v))
    lgam = log_gamma.astype(jnp.float32)
    fwd = retention_direction(q, k, v, lgam[0], strict=False)
    bwd = retention_direction(flip_seq(q), flip_seq(k), flip_seq(v), lgam[1], strict=True)
    o = fwd + flip_seq(bwd)
    mu = jnp.mean(o, axis=-1, keepdims=True)
    var = jnp.mean(jnp.square(o - mu), axis=-1, keepdims=True)
    o = (o - mu) * lax.rsqrt(var + NORM_EPS)
    o = jnp.swapaxes(o, 1, 2).reshape(b, s, RET_WIDTH).astype(rg.dtype)
    return jax.nn.silu(rg) * o

def gdn_direction(q, k, v, g, beta):
    b, h, s, dk = q.shape
    dv = v.shape[-1]
    n = s // GDN_CHUNK
    c = GDN_CHUNK
    q, k, v = (t.reshape(b, h, n, c, t.shape[-1]) for t in (q, k, v))
    g = jnp.cumsum(g.reshape(b, h, n, c), axis=-1)
    beta = beta.reshape(b, h, n, c)
    tril = jnp.tril(jnp.ones((c, c), bool))
    strict = jnp.tril(jnp.ones((c, c), bool), -1)
    decay = jnp.exp(jnp.where(tril, g[..., :, None] - g[..., None, :], -jnp.inf))
    k_beta = k * beta[..., None]
    lower = jnp.where(strict, jnp.einsum('bhnid,bhnjd->bhnij', k_beta, k) * decay, 0.0)
    rhs = jnp.concatenate([v * beta[..., None], k_beta * jnp.exp(g)[..., None]], axis=-1)
    sol = lax.linalg.triangular_solve(lower, rhs, left_side=True, lower=True, unit_diagonal=True)
    u, w = sol[..., :dv], sol[..., dv:]
    qk = jnp.einsum('bhnid,bhnjd->bhnij', q, k) * decay
    q_g = q * jnp.exp(g)[..., None]
    k_tail = k * jnp.exp(g[..., -1:] - g)[..., None]
    g_last = jnp.exp(g[..., -1])

    def step(state, xs):
        u_c, w_c, qk_c, qg_c, kt_c, gl_c = xs
        v_new = u_c - w_c @ state
        o_c = qg_c @ state + qk_c @ v_new
        state = state * gl_c[..., None, None] + jnp.swapaxes(kt_c, -1, -2) @ v_new
        return state, o_c

    xs = tuple(jnp.moveaxis(t, 2, 0) for t in (u, w, qk, q_g, k_tail, g_last))
    _, o = lax.scan(step, jnp.zeros((b, h, dk, dv), jnp.float32), xs)
    return jnp.moveaxis(o, 0, 2).reshape(b, h, s, dv)

def centred_depthwise_conv(x, w):
    return lax.conv_general_dilated(
        x, w[:, None, :], window_strides=(1,),
        padding=[((CONV_K - 1) // 2, CONV_K // 2)],
        dimension_numbers=('NWC', 'WIO', 'NWC'),
        feature_group_count=x.shape[-1])

def gdn_group(qkv, z, a, bl, conv_w, a_log, dt_bias, norm_w):
    b, s, _ = qkv.shape
    qkv = jax.nn.silu(centred_depthwise_conv(qkv, conv_w))
    q, k, v = jnp.split(qkv, 3, axis=-1)
    heads = lambda t: jnp.swapaxes(t.reshape(b, s, GDN_HEADS, GDN_HEAD_DIM), 1, 2).astype(jnp.float32)
    q, k, v = heads(q), heads(k), heads(v)
    l2n = lambda t: t * lax.rsqrt(jnp.sum(t * t, axis=-1, keepdims=True) + NORM_EPS)
    q = l2n(q) * GDN_HEAD_DIM ** -0.5
    k = l2n(k)
    dir_heads = lambda t: jnp.transpose(t.reshape(b, s, 2, GDN_HEADS), (2, 0, 3, 1)).astype(jnp.float32)
    a, bl = dir_heads(a), dir_heads(bl)
    g = -jnp.exp(a_log.astype(jnp.float32))[:, None, :, None] * jax.nn.softplus(
        a + dt_bias.astype(jnp.float32)[:, None, :, None])
    beta = jax.nn.sigmoid(bl)
    fwd = gdn_direction(q, k, v, g[0], beta[0])
    bwd = gdn_direction(flip_seq(q), flip_seq(k), flip_seq(v), flip_seq(g[1]), flip_seq(beta[1]))
    o = fwd + flip_seq(bwd)
    o = o * lax.rsqrt(jnp.mean(o * o, axis=-1, keepdims=True) + NORM_EPS) * norm_w.astype(jnp.float32)
    o = jnp.swapaxes(o, 1, 2).reshape(b, s, GDN_WIDTH).astype(z.dtype)
    return o * jax.nn.silu(z)

def parallel_head_groups(u, cos, sin, w_in, conv_w, ret_log_gamma, a_log, dt_bias, gdn_norm_w, w_out):
    proj = u @ w_in
    rq, rk, rv, rg, qkv, z, a, bl = jnp.split(proj, IN_SPLITS, axis=-1)
    o_ret = retention_group(rq, rk, rv, rg, cos, sin, ret_log_gamma)
    o_gdn = gdn_group(qkv, z, a, bl, conv_w, a_log, dt_bias, gdn_norm_w)
    return jnp.concatenate([o_ret, o_gdn], axis=-1) @ w_out

def memory_cross_attention(u, mem_n, wq, wk, wv, wo):
    b, s, _ = u.shape
    m = mem_n.shape[1]
    q = (u @ wq).reshape(b, s, XATTN_HEADS, XATTN_HEAD_DIM)
    k = (mem_n @ wk).reshape(b, m, XATTN_HEADS, XATTN_HEAD_DIM)
    v = (mem_n @ wv).reshape(b, m, XATTN_HEADS, XATTN_HEAD_DIM)
    scores = jnp.einsum('bshd,bmhd->bhsm', q, k).astype(jnp.float32) * XATTN_HEAD_DIM ** -0.5
    p = jax.nn.softmax(scores, axis=-1).astype(v.dtype)
    o = jnp.einsum('bhsm,bmhd->bshd', p, v).reshape(b, s, D_MODEL)
    return o @ wo

def first_inputs(seed: int = 0) -> dict:
    key = jax.random.key(seed)
    ks = jax.random.split(key, 24)
    nrm = lambda k, shape: jax.random.normal(k, shape, jnp.float32)
    dense = lambda k, shape, fan_in: nrm(k, shape) * fan_in ** -0.5
    gain = lambda k, shape: 1.0 + 0.02 * nrm(k, shape)
    x = nrm(ks[0], (BATCH, SEQ, D_MODEL))
    mem = nrm(ks[1], (BATCH, MEM_LEN, D_MODEL))
    positions = jnp.broadcast_to(jnp.arange(SEQ, dtype=jnp.int32)[None, :], (BATCH, SEQ))
    base = jnp.log1p(-(2.0 ** (-5.0 - jnp.arange(RET_HEADS, dtype=jnp.float32))))
    ret_log_gamma = base * (1.0 + 0.05 * nrm(ks[10], (DEPTH, 2, RET_HEADS)))
    gdn_a_log = jnp.log(jax.random.uniform(ks[11], (DEPTH, 2, GDN_HEADS), jnp.float32, 1.0, 16.0))
    dt = jnp.exp(jax.random.uniform(ks[12], (DEPTH, 2, GDN_HEADS), jnp.float32,
                                    float(np.log(1e-3)), float(np.log(1e-1))))
    gdn_dt_bias = dt + jnp.log(-jnp.expm1(-dt))
    return {
        "x": x,
        "mem": mem,
        "positions": positions,
        "norm_pre": gain(ks[2], (DEPTH, N_SUBLAYERS, D_MODEL)),
        "norm_post": gain(ks[3], (DEPTH, N_SUBLAYERS, D_MODEL)),
        "mem_norm": gain(ks[4], (DEPTH, D_MODEL)),
        "ffn1_gate": dense(ks[5], (DEPTH, D_MODEL, D_FF), D_MODEL),
        "ffn1_up": dense(ks[6], (DEPTH, D_MODEL, D_FF), D_MODEL),
        "ffn1_down": dense(ks[7], (DEPTH, D_FF, D_MODEL), D_FF),
        "w_in": dense(ks[8], (DEPTH, D_MODEL, IN_COLS), D_MODEL),
        "gdn_conv": dense(ks[9], (DEPTH, CONV_K, 3 * GDN_WIDTH), CONV_K),
        "ret_log_gamma": ret_log_gamma,
        "gdn_a_log": gdn_a_log,
        "gdn_dt_bias": gdn_dt_bias,
        "gdn_norm": gain(ks[13], (DEPTH, GDN_HEAD_DIM)),
        "w_out": dense(ks[14], (DEPTH, D_MIX, D_MODEL), D_MIX),
        "xattn_q": dense(ks[15], (DEPTH, D_MODEL, D_MODEL), D_MODEL),
        "xattn_k": dense(ks[16], (DEPTH, D_MODEL, D_MODEL), D_MODEL),
        "xattn_v": dense(ks[17], (DEPTH, D_MODEL, D_MODEL), D_MODEL),
        "xattn_o": dense(ks[18], (DEPTH, D_MODEL, D_MODEL), D_MODEL),
        "ffn2_gate": dense(ks[19], (DEPTH, D_MODEL, D_FF), D_MODEL),
        "ffn2_up": dense(ks[20], (DEPTH, D_MODEL, D_FF), D_MODEL),
        "ffn2_down": dense(ks[21], (DEPTH, D_FF, D_MODEL), D_FF),
    }

def first_block(x, mem, positions, norm_pre, norm_post, mem_norm, ffn1_gate, ffn1_up, ffn1_down,
              w_in, gdn_conv, ret_log_gamma, gdn_a_log, gdn_dt_bias, gdn_norm, w_out,
              xattn_q, xattn_k, xattn_v, xattn_o, ffn2_gate, ffn2_up, ffn2_down):
    cos, sin = rotary_tables(positions)
    for l in range(DEPTH):
        h = swiglu(rms_norm(x, norm_pre[l, 0]), ffn1_gate[l], ffn1_up[l], ffn1_down[l])
        x = x + 0.5 * rms_norm(h, norm_post[l, 0])
        h = parallel_head_groups(rms_norm(x, norm_pre[l, 1]), cos, sin, w_in[l], gdn_conv[l],
                                 ret_log_gamma[l], gdn_a_log[l], gdn_dt_bias[l], gdn_norm[l], w_out[l])
        x = x + rms_norm(h, norm_post[l, 1])
        h = memory_cross_attention(rms_norm(x, norm_pre[l, 2]), rms_norm(mem, mem_norm[l]),
                                   xattn_q[l], xattn_k[l], xattn_v[l], xattn_o[l])
        x = x + rms_norm(h, norm_post[l, 2])
        h = swiglu(rms_norm(x, norm_pre[l, 3]), ffn2_gate[l], ffn2_up[l], ffn2_down[l])
        x = x + 0.5 * rms_norm(h, norm_post[l, 3])
    return x


DEPTH_2 = 1

CHUNK = 64
D_MIX_2 = D_MODEL
N_GROUPS = 4
GW = D_MIX_2 // N_GROUPS
HEAD_DIM = 64
N_HEADS_GROUP = GW // HEAD_DIM
ATTN_LEFT_CHUNKS = 8
N_BAND = ATTN_LEFT_CHUNKS + 1
REL_CLIP = 256
ATTN_SCALE = HEAD_DIM ** -0.5
NEG_INF = -1e30
RWKV_W_RANK = 32
RWKV_A_RANK = 32
RWKV_G_RANK = 64
RWKV_GN_EPS = HEAD_DIM * 1e-5
LRU_CONV = 4
LRU_C = 8.0
LRU_BLOCKS = N_HEADS_GROUP
LRU_BLOCK_DIM = GW // LRU_BLOCKS
ATTN_COLS = 3 * GW
HGRN_COLS = 4 * GW
RWKV_COLS = 3 * GW + RWKV_W_RANK + RWKV_A_RANK + RWKV_G_RANK
LRU_COLS = 2 * GW
D_IN = ATTN_COLS + HGRN_COLS + RWKV_COLS + LRU_COLS
MLP_HIDDEN = 4 * D_MODEL
RMS_EPS = 1e-6


def split_cols(t, sizes):
    offs = np.cumsum(sizes)[:-1].tolist()
    return jnp.split(t, offs, axis=-1)

def rms_norm_2(x, gain):
    xf = x.astype(jnp.float32)
    y = xf * lax.rsqrt(jnp.mean(xf * xf, axis=-1, keepdims=True) + RMS_EPS)
    return (y * gain.astype(jnp.float32)).astype(x.dtype)

def to_heads(t):
    return t.reshape(t.shape[0], t.shape[1], N_HEADS_GROUP, HEAD_DIM)

def to_chunks(t):
    b, s, _ = t.shape
    return t.reshape(b, s // CHUNK, CHUNK, N_HEADS_GROUP, HEAD_DIM).transpose(1, 0, 3, 2, 4)

def from_chunks(t):
    nc, b = t.shape[0], t.shape[1]
    return t.transpose(1, 0, 3, 2, 4).reshape(b, nc * CHUNK, GW)

def chunk_attention(q, k, v, rel_bias):
    b, s, _ = q.shape
    nc = s // CHUNK
    shp = (b, nc, CHUNK, N_HEADS_GROUP, HEAD_DIM)
    qc, kc, vc = q.reshape(shp), k.reshape(shp), v.reshape(shp)
    pad = ((0, 0), (ATTN_LEFT_CHUNKS, 0), (0, 0), (0, 0), (0, 0))
    band = jnp.arange(nc)[:, None] + jnp.arange(N_BAND)[None, :]
    kb = jnp.pad(kc, pad)[:, band].reshape(b, nc, N_BAND * CHUNK, N_HEADS_GROUP, HEAD_DIM)
    vb = jnp.pad(vc, pad)[:, band].reshape(b, nc, N_BAND * CHUNK, N_HEADS_GROUP, HEAD_DIM)
    scores = jnp.einsum('bcqhd,bckhd->bchqk', qc, kb) * ATTN_SCALE
    key_off = ((jnp.arange(N_BAND) - ATTN_LEFT_CHUNKS)[:, None] * CHUNK
               + jnp.arange(CHUNK)[None, :]).reshape(-1)
    rel = key_off[None, :] - jnp.arange(CHUNK)[:, None]
    bias = rel_bias.astype(jnp.float32)[:, jnp.clip(rel, -REL_CLIP, REL_CLIP) + REL_CLIP]
    valid = jnp.repeat(band >= ATTN_LEFT_CHUNKS, CHUNK, axis=1)
    scores = jnp.where(valid[None, :, None, None, :], scores + bias[None, None], NEG_INF)
    probs = jax.nn.softmax(scores, axis=-1)
    out = jnp.einsum('bchqk,bckhd->bcqhd', probs, vb)
    return out.reshape(b, s, GW)

def hgrn2(q_raw, f_raw, i_raw, g_raw, lb, norm_gain):
    b = q_raw.shape[0]
    log_f = jnp.logaddexp(jnp.log(lb), jnp.log1p(-lb) + jax.nn.log_sigmoid(f_raw))
    key = (1.0 - lb) * jax.nn.sigmoid(-f_raw)
    q = jax.nn.silu(q_raw)
    tri = jnp.tril(jnp.ones((CHUNK, CHUNK), dtype=bool))

    def step(state, inp):
        qc, kc, vc, gc = inp
        cum = jnp.cumsum(gc, axis=2)
        last = cum[:, :, -1:, :]
        o_inter = jnp.einsum('bhtk,bhkv->bhtv', qc * jnp.exp(cum), state)
        diff = cum[:, :, :, None, :] - cum[:, :, None, :, :]
        decay = jnp.exp(jnp.where(tri[None, None, :, :, None], diff, -jnp.inf))
        att = jnp.einsum('bhtk,bhsk,bhtsk->bhts', qc, kc, decay)
        o_intra = jnp.einsum('bhts,bhsv->bhtv', att, vc)
        new_state = (jnp.exp(last).transpose(0, 1, 3, 2) * state
                     + jnp.einsum('bhsk,bhsv->bhkv', kc * jnp.exp(last - cum), vc))
        return new_state, o_inter + o_intra

    state0 = jnp.zeros((b, N_HEADS_GROUP, HEAD_DIM, HEAD_DIM), jnp.float32)
    _, o = lax.scan(step, state0, (to_chunks(q), to_chunks(key), to_chunks(i_raw), to_chunks(log_f)))
    o = to_heads(from_chunks(o))
    o = o * lax.rsqrt(jnp.mean(o * o, axis=-1, keepdims=True) + RMS_EPS)
    return o.reshape(g_raw.shape) * norm_gain * jax.nn.silu(g_raw)

def rwkv7(pc, mu, w0, w2, a0, a2, g2, k_k, k_a, r_k, ln_w, ln_b):
    b, s, _ = pc.shape
    prev = jnp.pad(pc, ((0, 0), (1, 0), (0, 0)))[:, :-1]
    xs = pc + mu * (prev - pc)
    r, k, v, w_lo, a_lo, g_lo = split_cols(xs, [GW, GW, GW, RWKV_W_RANK, RWKV_A_RANK, RWKV_G_RANK])
    w_pre = -jax.nn.softplus(-(w0 + jnp.tanh(w_lo) @ w2)) - 0.5
    decay = jnp.exp(-jnp.exp(w_pre))
    a = jax.nn.sigmoid(a0 + a_lo @ a2)
    g = jax.nn.sigmoid(g_lo) @ g2
    kk = to_heads(k * k_k)
    kk = kk / jnp.maximum(jnp.sqrt(jnp.sum(kk * kk, axis=-1, keepdims=True)), 1e-12)
    k = k * (1.0 + (a - 1.0) * k_a)
    r_h, w_h, k_h, v_h, a_h = to_heads(r), to_heads(decay), to_heads(k), to_heads(v), to_heads(a)

    def step(state, inp):
        rt, wt, kt, vt, kkt, at = inp
        sa = jnp.einsum('bhvk,bhk->bhv', state, -kkt)
        state = (state * wt[:, :, None, :] + sa[..., None] * (kkt * at)[:, :, None, :]
                 + vt[..., None] * kt[:, :, None, :])
        return state, jnp.einsum('bhvk,bhk->bhv', state, rt)

    seq_first = lambda t: t.transpose(1, 0, 2, 3)
    state0 = jnp.zeros((b, N_HEADS_GROUP, HEAD_DIM, HEAD_DIM), jnp.float32)
    _, y = lax.scan(step, state0, (seq_first(r_h), seq_first(w_h), seq_first(k_h),
                                   seq_first(v_h), seq_first(kk), seq_first(a_h)))
    y = seq_first(y)
    mean = jnp.mean(y, axis=-1, keepdims=True)
    var = jnp.mean(jnp.square(y - mean), axis=-1, keepdims=True)
    y = ((y - mean) * lax.rsqrt(var + RWKV_GN_EPS)).reshape(b, s, GW) * ln_w + ln_b
    bonus = (jnp.sum(r_h * k_h * r_k, axis=-1, keepdims=True) * v_h).reshape(b, s, GW)
    return (y + bonus) * g

def rglru(xb, gb, conv_w, conv_b, wa, ba, wx, bx, lam):
    b, s, _ = xb.shape
    conv = lax.conv_general_dilated(xb, conv_w.astype(xb.dtype)[:, None, :], window_strides=(1,),
                                    padding=[(LRU_CONV - 1, 0)],
                                    dimension_numbers=('NWC', 'WIO', 'NWC'),
                                    feature_group_count=GW) + conv_b
    xh = conv.reshape(b, s, LRU_BLOCKS, LRU_BLOCK_DIM)
    gate_r = jax.nn.sigmoid(jnp.einsum('bsnd,nde->bsne', xh, wa).reshape(b, s, GW) + ba)
    gate_i = jax.nn.sigmoid(jnp.einsum('bsnd,nde->bsne', xh, wx).reshape(b, s, GW) + bx)
    log_a = -LRU_C * gate_r * jax.nn.softplus(-lam)
    a = jnp.exp(log_a)
    inp = jnp.sqrt(-jnp.expm1(2.0 * log_a)) * (gate_i * conv)

    def combine(c1, c2):
        a1, b1 = c1
        a2, b2 = c2
        return a1 * a2, a2 * b1 + b2

    _, h = lax.associative_scan(combine, (a, inp), axis=1)
    return h * jax.nn.gelu(gb)

def second_inputs(seed: int = 0) -> dict:
    key = jax.random.key(seed)
    ks = jax.random.split(key, 32)
    L = DEPTH_2

    def nrm(k, shape, scale):
        return jax.random.normal(k, shape, jnp.float32) * scale

    u = jax.random.uniform(ks[27], (L, GW), jnp.float32, 0.9, 0.999)
    a_root = u ** (1.0 / LRU_C)
    lam = jnp.log(a_root) - jnp.log1p(-a_root)
    return {
        'x': nrm(ks[0], (BATCH, SEQ, D_MODEL), 1.0),
        'norm_mix_pre': 1.0 + nrm(ks[1], (L, D_MODEL), 0.05),
        'norm_mix_post': 1.0 + nrm(ks[2], (L, D_MODEL), 0.05),
        'norm_mlp_pre': 1.0 + nrm(ks[3], (L, D_MODEL), 0.05),
        'norm_mlp_post': 1.0 + nrm(ks[4], (L, D_MODEL), 0.05),
        'w_in': nrm(ks[5], (L, D_MODEL, D_IN), D_MODEL ** -0.5),
        'w_out': nrm(ks[6], (L, D_MIX_2, D_MODEL), D_MIX_2 ** -0.5),
        'attn_rel_bias': nrm(ks[7], (L, N_HEADS_GROUP, 2 * REL_CLIP + 1), 0.2),
        'hgrn_lb_logits': nrm(ks[8], (L, GW), 0.5),
        'hgrn_norm': 1.0 + nrm(ks[9], (L, GW), 0.05),
        'rwkv_mu': jax.random.uniform(ks[10], (L, RWKV_COLS), jnp.float32, 0.2, 0.8),
        'rwkv_w0': jax.random.uniform(ks[11], (L, GW), jnp.float32, -6.0, 1.0),
        'rwkv_w2': nrm(ks[12], (L, RWKV_W_RANK, GW), 0.5 * RWKV_W_RANK ** -0.5),
        'rwkv_a0': nrm(ks[13], (L, GW), 0.1),
        'rwkv_a2': nrm(ks[14], (L, RWKV_A_RANK, GW), 0.5 * RWKV_A_RANK ** -0.5),
        'rwkv_g2': nrm(ks[15], (L, RWKV_G_RANK, GW), RWKV_G_RANK ** -0.5),
        'rwkv_k_k': 0.85 + nrm(ks[16], (L, GW), 0.05),
        'rwkv_k_a': 1.0 + nrm(ks[17], (L, GW), 0.05),
        'rwkv_r_k': nrm(ks[18], (L, N_HEADS_GROUP, HEAD_DIM), 0.1),
        'rwkv_ln_w': 1.0 + nrm(ks[19], (L, GW), 0.05),
        'rwkv_ln_b': nrm(ks[20], (L, GW), 0.02),
        'lru_conv_w': nrm(ks[21], (L, LRU_CONV, GW), 0.5 * LRU_CONV ** -0.5),
        'lru_conv_b': nrm(ks[22], (L, GW), 0.02),
        'lru_wa': nrm(ks[23], (L, LRU_BLOCKS, LRU_BLOCK_DIM, LRU_BLOCK_DIM), LRU_BLOCK_DIM ** -0.5),
        'lru_ba': nrm(ks[24], (L, GW), 0.02),
        'lru_wx': nrm(ks[25], (L, LRU_BLOCKS, LRU_BLOCK_DIM, LRU_BLOCK_DIM), LRU_BLOCK_DIM ** -0.5),
        'lru_bx': nrm(ks[26], (L, GW), 0.02),
        'lru_lambda': lam,
        'mlp_w1': nrm(ks[28], (L, D_MODEL, MLP_HIDDEN), D_MODEL ** -0.5),
        'mlp_w2': nrm(ks[29], (L, MLP_HIDDEN, D_MODEL), MLP_HIDDEN ** -0.5),
    }

def second_block(x, norm_mix_pre, norm_mix_post, norm_mlp_pre, norm_mlp_post, w_in, w_out,
              attn_rel_bias, hgrn_lb_logits, hgrn_norm, rwkv_mu, rwkv_w0, rwkv_w2, rwkv_a0, rwkv_a2,
              rwkv_g2, rwkv_k_k, rwkv_k_a, rwkv_r_k, rwkv_ln_w, rwkv_ln_b, lru_conv_w, lru_conv_b,
              lru_wa, lru_ba, lru_wx, lru_bx, lru_lambda, mlp_w1, mlp_w2):
    dt = x.dtype
    f32 = jnp.float32
    lb_sm = jax.nn.softmax(hgrn_lb_logits.astype(f32), axis=0)
    lb_all = jnp.maximum(jnp.cumsum(lb_sm, axis=0) - lb_sm[0:1], 0.0)
    for l in range(DEPTH_2):
        h = rms_norm_2(x, norm_mix_pre[l])
        proj = (h @ w_in[l]).astype(f32)
        pa, pb, pc, pd = split_cols(proj, [ATTN_COLS, HGRN_COLS, RWKV_COLS, LRU_COLS])
        qa, ka, va = split_cols(pa, [GW, GW, GW])
        ya = chunk_attention(qa, ka, va, attn_rel_bias[l])
        qb, fb, ib, gb = split_cols(pb, [GW, GW, GW, GW])
        yb = hgrn2(qb, fb, ib, gb, lb_all[l], hgrn_norm[l].astype(f32))
        yc = rwkv7(pc, rwkv_mu[l].astype(f32), rwkv_w0[l].astype(f32), rwkv_w2[l].astype(f32),
                   rwkv_a0[l].astype(f32), rwkv_a2[l].astype(f32), rwkv_g2[l].astype(f32),
                   rwkv_k_k[l].astype(f32), rwkv_k_a[l].astype(f32), rwkv_r_k[l].astype(f32),
                   rwkv_ln_w[l].astype(f32), rwkv_ln_b[l].astype(f32))
        xd, gd = split_cols(pd, [GW, GW])
        yd = rglru(xd, gd, lru_conv_w[l].astype(f32), lru_conv_b[l].astype(f32), lru_wa[l].astype(f32),
                   lru_ba[l].astype(f32), lru_wx[l].astype(f32), lru_bx[l].astype(f32),
                   lru_lambda[l].astype(f32))
        mix = jnp.concatenate([ya, yb, yc, yd], axis=-1).astype(dt)
        x = x + rms_norm_2(mix @ w_out[l], norm_mix_post[l])
        h = rms_norm_2(x, norm_mlp_pre[l])
        ff = jnp.square(jax.nn.relu(h @ mlp_w1[l])) @ mlp_w2[l]
        x = x + rms_norm_2(ff, norm_mlp_post[l])
    return x


def setup_inputs(seed=0):
    out = dict(first_inputs(seed))
    for name, value in second_inputs(seed + 1).items():
        if name != "x":
            out[name + "_2"] = value
    return out


def reference(
    x, mem, positions, norm_pre, norm_post, mem_norm, ffn1_gate, ffn1_up, ffn1_down, w_in,
    gdn_conv, ret_log_gamma, gdn_a_log, gdn_dt_bias, gdn_norm, w_out, xattn_q, xattn_k, xattn_v,
    xattn_o, ffn2_gate, ffn2_up, ffn2_down, norm_mix_pre_2, norm_mix_post_2, norm_mlp_pre_2,
    norm_mlp_post_2, w_in_2, w_out_2, attn_rel_bias_2, hgrn_lb_logits_2, hgrn_norm_2, rwkv_mu_2,
    rwkv_w0_2, rwkv_w2_2, rwkv_a0_2, rwkv_a2_2, rwkv_g2_2, rwkv_k_k_2, rwkv_k_a_2, rwkv_r_k_2,
    rwkv_ln_w_2, rwkv_ln_b_2, lru_conv_w_2, lru_conv_b_2, lru_wa_2, lru_ba_2, lru_wx_2,
    lru_bx_2, lru_lambda_2, mlp_w1_2, mlp_w2_2,
):
    x = first_block(
        x, mem, positions, norm_pre, norm_post, mem_norm, ffn1_gate, ffn1_up, ffn1_down, w_in,
        gdn_conv, ret_log_gamma, gdn_a_log, gdn_dt_bias, gdn_norm, w_out, xattn_q, xattn_k,
        xattn_v, xattn_o, ffn2_gate, ffn2_up, ffn2_down,
    )
    return second_block(
        x, norm_mix_pre_2, norm_mix_post_2, norm_mlp_pre_2, norm_mlp_post_2, w_in_2, w_out_2,
        attn_rel_bias_2, hgrn_lb_logits_2, hgrn_norm_2, rwkv_mu_2, rwkv_w0_2, rwkv_w2_2,
        rwkv_a0_2, rwkv_a2_2, rwkv_g2_2, rwkv_k_k_2, rwkv_k_a_2, rwkv_r_k_2, rwkv_ln_w_2,
        rwkv_ln_b_2, lru_conv_w_2, lru_conv_b_2, lru_wa_2, lru_ba_2, lru_wx_2, lru_bx_2,
        lru_lambda_2, mlp_w1_2, mlp_w2_2,
    )


_drawn_inputs = setup_inputs


def setup_inputs(seed=0):
    import zlib

    import numpy as np

    out = dict(_drawn_inputs(seed))
    spreads = {}
    factors = {'gdn_norm': 3.545,
     'norm_mix_post_2': 2.952,
     'norm_mlp_pre_2': 2.791,
     'norm_mlp_post_2': 3.252,
     'attn_rel_bias_2': 5.705,
     'hgrn_norm_2': 5.191,
     'rwkv_w2_2': 4.658,
     'rwkv_a0_2': 5.795,
     'rwkv_ln_w_2': 5.56,
     'rwkv_ln_b_2': 25.096,
     'lru_conv_b_2': 28.24,
     'lru_wa_2': 139.944,
     'lru_ba_2': 200.0,
     'lru_bx_2': 200.0,
     'lru_wx_2': 34.208,
     'lru_lambda_2': 25.224,
     'lru_conv_w_2': 8.0}
    for name, (base, spread) in spreads.items():
        noise = np.random.default_rng([zlib.crc32(name.encode()), seed]).standard_normal(out[name].shape)
        drawn = base * np.exp(spread * noise) if base else spread * noise
        out[name] = __import__('jax').numpy.asarray(drawn.astype(out[name].dtype))
    for name, factor in factors.items():
        out[name] = (out[name] * factor).astype(out[name].dtype)
    return out
```

```python
from contextlib import ExitStack

import numpy as np

import concourse.bass as bass
from concourse import mybir

F32 = mybir.dt.float32
F32R = mybir.dt.float32r
I32 = mybir.dt.int32
ALU = mybir.AluOpType
ACT = mybir.ActivationFunctionType
AXX = mybir.AxisListType.X
MUL, ADD, SUB, MAX, MIN = ALU.mult, ALU.add, ALU.subtract, ALU.max, ALU.min

P = 128
TOK = 256
NT = TOK // P
D = 1024
KD = D // P
DEPTH = 2
D_FF = 2816
HEADS = 4
HD = 128
MLP = 4096
EPS = 1e-6
SLAB = 2048
NSLOT = 5
LEVELS = (1, 2, 4, 8, 16, 32, 64)


class Queue:

    def __init__(self, sem):
        self.sem, self.count, self.steps, self.seen = sem, 0, [], {}

    def wait(self, marks):
        for sem, value in marks:
            if self.seen.get(sem.name, 0) < value:
                self.seen[sem.name] = value
                self.steps.append(lambda e, s=sem, v=value: e.wait_ge(s, v))

    def do(self, after, *instructions):
        self.wait(after)
        self.steps += [lambda e, f=f: f() for f in instructions[:-1]]
        self.steps.append(lambda e, f=instructions[-1]: f().then_inc(self.sem, 1))
        self.count += 1
        return (self.sem, self.count)

    def last(self):
        return [(self.sem, self.count)] if self.count else []

    def dma(self, after, sem, total, dst, src):
        self.wait(after)
        self.steps.append(lambda e: e.dma_start(dst, src).then_inc(sem, 16))
        return (sem, total)

    def play(self, engine):
        for s in self.steps:
            s(engine)


def shape_constants():
    i = np.arange(P)[:, None]
    j = np.arange(P)[None, :]
    f = lambda a: np.asarray(a, np.float32)
    parts = {"ident": f(i == j), "upto": f(i <= j), "from": f(i >= j), "before": f(i < j)}
    parts["ones"] = np.ones((P, P), np.float32)
    for name in ("fwd", "bwd"):
        masks = []
        for b in LEVELS:
            m = (i // (2 * b) == j // (2 * b)) & (i % (2 * b) >= b) & (j % (2 * b) < b)
            masks.append(f(m if name == "fwd" else m.T))
        parts[name] = np.concatenate(masks, 1)
    n = np.arange(TOK)[None, None, :]
    m = np.arange(NT)[None, :, None] * P + np.arange(P)[:, None, None]
    parts["ahead"] = f(np.maximum(n - m, 0)).reshape(P, -1)
    parts["behind"] = f(np.maximum(m - n, 0)).reshape(P, -1)
    parts["rotate"] = f(i == j - 64) - f(i == j + 64)
    parts["flip"] = f(i + j == P - 1)
    parts["half"] = f(i // 64 == j // 64)
    parts["resets"] = np.broadcast_to(f(np.arange(TOK) % 64 != 0), (P, TOK))
    parts["headcol"] = f(i // 64 == np.arange(2)[None, :])
    inv = np.float32(10000.0) ** (-np.arange(0, HD, 2, dtype=np.float32) / np.float32(HD))
    parts["freq"] = f(np.concatenate([inv, inv])[:, None])
    barred = np.zeros((P, 64), np.float32)
    barred[:64] = -1e30
    parts["barred"] = barred
    at, where = 0, {}
    for k, v in parts.items():
        where[k] = (at, at + v.shape[1])
        at += v.shape[1]
    return np.ascontiguousarray(np.concatenate(list(parts.values()), 1)), where


def build(nc, a, out, dbg=None):
    _, const_at = shape_constants()
    with ExitStack() as ctx:
        def sb(name, shape, dt=F32):
            return ctx.enter_context(nc.sbuf_tensor(name, shape, dt))

        def sem(name):
            return ctx.enter_context(nc.semaphore(name))

        pe, dve, act, pool, sp = (Queue(sem(f"{n}_steps")) for n in ("pe", "dve", "act", "pool", "sp"))
        V, S, G, T = nc.vector, nc.scalar, nc.gpsimd, nc.tensor

        psum = ctx.enter_context(nc.psum_tensor("psum", [P, 8, 512], F32))
        ring = sb("weight_ring", [P, NSLOT, SLAB])
        slot_landed = [sem(f"slab_landed{s}") for s in range(NSLOT)]
        slot_loads = [0] * NSLOT
        slot_free = [[] for _ in range(NSLOT)]
        x = sb("x", [P, NT, D])
        xnT = sb("xnT", [P, KD, TOK])
        memkT = sb("memkT", [P, KD, TOK])
        memv = sb("memv", [P, NT, D])
        mixT = xnT
        consts = sb("consts", [P, max(e for _, e in const_at.values())])
        gains = sb("gains", [P, 96])
        taps = sb("taps", [P, 120])
        vecs = sb("vecs", [P, 48])
        post_w = sb("post_w", [P, 1, D])
        cosT = sb("cosT", [P, TOK])
        sinT = sb("sinT", [P, TOK])
        ssq = sb("ssq", [P, 4])
        inv_rms = sb("inv_rms", [P, 4])
        softmax_s = sb("softmax_s", [P, 16])
        minus_half = sb("minus_half", [P, 16])
        ARENA = 26624
        arena_base = (nc.sbuf_usable_end - 4 * ARENA) // 32 * 32
        arena = nc.alloc_sbuf_tensor_at("arena", [P, ARENA], F32, offset=arena_base)
        NHL = 4
        w_hl = nc.alloc_sbuf_tensor_at("w_hi_lo", [P, NHL, 2, SLAB], F32R, offset=arena_base + 4 * (ARENA - 4096 * NHL))
        x_hl = nc.alloc_sbuf_tensor_at("x_hi_lo", [P, 2, KD, TOK], F32R, offset=arena_base + 4 * (ARENA - 4096 * NHL - 4096))
        NH = 3
        h_hl = nc.alloc_sbuf_tensor_at("h_hi_lo", [P, NH, 2, 2, TOK], F32R, offset=arena_base + 4 * (ARENA - 4096 * NHL - 4096 - 1024 * NH))
        hl_free = [[] for _ in range(NHL)]
        arena_at, keep_tail = [0], [False]
        tail_2k = arena[:, ARENA - 2048:ARENA]
        memT = tail_2k.rearrange("p (k t) -> p k t", k=KD)

        def carve(*shape):
            n = int(np.prod(shape))
            assert arena_at[0] + n <= ARENA, (arena_at, n)
            v = arena[:, arena_at[0]:arena_at[0] + n]
            arena_at[0] += n
            assert arena_at[0] <= ARENA - (2048 if keep_tail[0] else 0), arena_at
            names = "abcd"[:len(shape)]
            if len(shape) == 1:
                return v
            return v.rearrange(f"p ({' '.join(names)}) -> p {' '.join(names)}",
                               **{names[k]: shape[k] for k in range(1, len(shape))})

        def C(name):
            lo, hi = const_at[name]
            return consts[:, lo:hi]

        ident = C("ident")

        def stage_start():
            marks = pe.last() + dve.last() + act.last() + pool.last()
            for q in (pe, dve, act, pool, sp):
                q.wait(marks)
            arena_at[0] = 0
            for k in range(NHL):
                hl_free[k] = []

        def V_(after, *f):
            return dve.do(after, *f)

        load_sems = {}

        def load(dst, src, after=(), group="setup"):
            if group not in load_sems:
                load_sems[group] = [sem(f"{group}_landed"), 0]
            g = load_sems[group]
            g[1] += 16
            return sp.dma(after, g[0], g[1], dst, src)

        bank_free = [[] for _ in range(8)]
        turn = [0]

        def take(banks=(4, 5, 6, 7)):
            b = banks[turn[0] % len(banks)]
            turn[0] += 1
            return b, bank_free[b]

        slab_no = [0]

        def slab(src, rows, cols):
            s = slab_no[0] % NSLOT
            slab_no[0] += 1
            slot_loads[s] += 16
            view = ring[:, s, 0:rows * cols].rearrange("p (k n) -> p k n", n=cols)
            mark = sp.dma(slot_free[s], slot_landed[s], slot_loads[s], view, src)
            return s, view, mark

        def columns(w, c0, n=256):
            return w[:, c0:c0 + n].rearrange("(k p) n -> p k n", p=P), w.shape[0] // P, n

        def rows(w, r0, n=2):
            return w[r0 * P:(r0 + n) * P, :].rearrange("(k p) n -> p k n", p=P), n, w.shape[1]

        def mm(o, l, r, start=True, stop=True):
            return lambda: T.matmul(o, l, r, start=start, stop=stop)

        def tr(o, i):
            k = i.partition_size()
            b = i.base_partition()
            return lambda: T.transpose(o, i, ident[b:b + k, 0:k])

        def project_T(w, c0, srcT, after, banks=(4, 5, 6, 7)):
            s, wv, landed = slab(*columns(w, c0))
            b, free = take(banks)
            ops = [mm(psum[:, b, 256 * j:256 * j + 256], wv[:, k, P * j:P * j + P], srcT[:, k, :],
                      k == 0, k == KD - 1) for j in range(2) for k in range(KD)]
            m = pe.do([landed] + free + after, *ops)
            slot_free[s] = [m]
            return b, psum[:, b, :].rearrange("p (j t) -> p j t", j=2), m

        def project_N(w, c0, srcT, after, n=256, banks=(4, 5, 6, 7)):
            s, wv, landed = slab(*columns(w, c0, n))
            b, free = take(banks)
            ops = [mm(psum[:, b, n * t:n * t + n], srcT[:, k, P * t:P * t + P], wv[:, k, :],
                      k == 0, k == KD - 1) for t in range(NT) for k in range(KD)]
            m = pe.do([landed] + free + after, *ops)
            slot_free[s] = [m]
            return b, psum[:, b, 0:2 * n].rearrange("p (t n) -> p t n", t=2), m

        def project_out(w, r0, nrows, srcT, total, after):
            s, wv, landed = slab(*rows(w, r0, nrows))
            ops = [mm(psum[:, 2 * t + n, :], srcT[:, r0 + j, P * t:P * t + P], wv[:, j, 512 * n:512 * n + 512],
                      r0 + j == 0, r0 + j == total - 1)
                   for j in range(nrows) for t in range(NT) for n in range(2)]
            free = [] if r0 else [m for b in range(4) for m in bank_free[b]]
            m = pe.do([landed] + free + after, *ops)
            slot_free[s] = [m]
            return m

        def split(src, hi, lo, after):
            mh = act.do(after, lambda: S.copy(hi, src))
            return V_([mh], lambda: V.tensor_tensor(lo, src, hi.bitcast(F32), SUB))

        class SplitStream:

            def __init__(self, sources):
                self.sources, self.cut, self.used = sources, [], 0

            def ahead(self, n):
                while len(self.cut) < min(self.used + n, len(self.sources)):
                    s, view, landed = slab(*self.sources[len(self.cut)])
                    k = len(self.cut) % NHL
                    m = split(ring[:, s, :], w_hl[:, k, 0, :], w_hl[:, k, 1, :], [landed] + hl_free[k])
                    slot_free[s] = [m]
                    n_cols = self.sources[len(self.cut)][2]
                    self.cut.append((k, [w_hl[:, k, i, :].rearrange("p (k n) -> p k n", n=n_cols) for i in range(2)], m))

            def next(self):
                self.used += 1
                return self.cut[self.used - 1]

        def three(o, l, r, start, stop):
            return [mm(o, l[0], r[0], start, False), mm(o, l[0], r[1], False, False), mm(o, l[1], r[0], False, stop)]

        def split_project_T(stream, after):
            k_, w, m = stream.next()
            b, free = take()
            ops = [op for j in range(2) for k in range(KD) for op in
                   three(psum[:, b, 256 * j:256 * j + 256], [w[i][:, k, P * j:P * j + P] for i in range(2)],
                         [x_hl[:, i, k, :] for i in range(2)], k == 0, k == KD - 1)]
            m = pe.do([m] + free + after, *ops)
            hl_free[k_] = [m]
            return b, psum[:, b, :].rearrange("p (j t) -> p j t", j=2), m

        def split_out(stream, lhs, first, last, after):
            k_, w, m = stream.next()
            free = [m_ for b in range(4) for m_ in bank_free[b]] if first else []
            ops = [op for j in range(2) for t in range(NT) for n in range(2) for op in
                   three(psum[:, 2 * t + n, :], [lhs(i, j)[:, P * t:P * t + P] for i in range(2)],
                         [w[i][:, j, 512 * n:512 * n + 512] for i in range(2)], first and j == 0, last and j == 1)]
            m = pe.do([m] + free + after, *ops)
            hl_free[k_] = [m]
            return m

        def split_xn(marks):
            out_ = []
            for i in range(4):
                t, g = i // 2, i % 2
                at = (slice(None), slice(4 * g, 4 * g + 4), slice(P * t, P * t + P))
                out_.append(split(xnT[at], x_hl[:, 0][at], x_hl[:, 1][at], [marks[i]]))
            return out_

        const_mark = load(consts[:, :], a["consts"])
        staging = carve(3, P)
        lo = []
        r = 0
        for name in ("norm_pre", "mem_norm", "norm_mix_pre_2", "norm_mlp_pre_2"):
            v = a[name].rearrange("a b c -> (a b c)") if len(a[name].shape) == 3 else a[name].rearrange("a b -> (a b)")
            n = v.shape[0] // P
            load(staging[r:r + n, 0, :], v.rearrange("(r c) -> r c", c=P))
            r += n
        load(staging[0:120, 1, :], a["gdn_conv"].rearrange("l j (r c) -> (l j r) c", c=P))
        vec_at = {}
        r = 0
        for name in ("rwkv_mu_2", "rwkv_w0_2", "rwkv_a0_2", "rwkv_k_k_2", "rwkv_k_a_2", "rwkv_r_k_2",
                     "rwkv_ln_w_2", "rwkv_ln_b_2", "lru_conv_w_2", "lru_conv_b_2", "lru_ba_2",
                     "lru_bx_2", "lru_lambda_2", "hgrn_lb_logits_2"):
            v = a[name]
            v = v.rearrange("a b c -> (a b c)") if len(v.shape) == 3 else v.rearrange("a b -> (a b)")
            n = v.shape[0] // P
            load(staging[r:r + n, 2, :], v.rearrange("(r c) -> r c", c=P))
            vec_at[name] = r
            r += n
        nvec = r
        load(x[:, :, :], a["x"][0].rearrange("(t p) d -> p t d", p=P))
        posi = sb("posi", [P, TOK], I32)
        load(posi[:, :], a["positions"].partition_broadcast(P))
        lg = sb("lg", [P, 16])
        load(lg[:, :], a["ret_log_gamma"].rearrange("l d h -> (l d h)").partition_broadcast(P))
        alog = sb("alog", [P, 16])
        load(alog[:, :], a["gdn_a_log"].rearrange("l d h -> (l d h)").partition_broadcast(P))
        dtb = sb("dtb", [P, 16])
        load(dtb[:, :], a["gdn_dt_bias"].rearrange("l d h -> (l d h)").partition_broadcast(P))
        gnw = sb("gnw", [P, 2 * P])
        load(gnw[:, :], a["gdn_norm"].rearrange("l d -> (l d)").partition_broadcast(P))
        hgn = sb("hgn", [P, 256])
        setup = [load(hgn[:, :], a["hgrn_norm_2"].rearrange("l d -> (l d)").partition_broadcast(P))]
        half_set = pool.do([], lambda: G.memset(minus_half[:, :], -0.5))
        for q in (pe, dve, act, pool):
            q.wait(setup)

        t0 = pe.do([], tr(psum[:, 4, 0:96], staging[0:96, 0, :]), tr(psum[:, 4, 128:248], staging[0:120, 1, :]),
                   tr(psum[:, 4, 256:256 + nvec], staging[0:nvec, 2, :]))
        v0 = dve.do([t0], lambda: V.tensor_copy(gains[:, :], psum[:, 4, 0:96]),
                    lambda: V.tensor_copy(taps[:, :], psum[:, 4, 128:248]),
                    lambda: V.tensor_copy(vecs[:, 0:nvec], psum[:, 4, 256:256 + nvec]))
        bank_free[4] = [v0]
        for q in (pe, act, pool, dve):
            q.wait([v0, half_set])

        def vec(name, k=0):
            c = vec_at[name] + k
            return vecs[:, c:c + 1]

        ang, turns, red = carve(TOK), carve(TOK), carve(TOK)
        TWO_PI = (6.28125, 0.0019350051879882812, float(2 * np.pi - 6.28125 - 0.0019350051879882812))
        MAGIC = 12582912.0
        m = V_([], lambda: V.tensor_copy(ang, posi[:, :]))
        m = V_([m], lambda: V.tensor_scalar(ang, ang, C("freq"), None, MUL))
        for table, shift in ((sinT, 0.0), (cosT, 0.25)):
            m = V_([m], lambda s=shift: V.tensor_scalar(turns, ang, float(1 / (2 * np.pi)), s, MUL, ADD))
            m = V_([m], lambda: V.tensor_scalar(turns, turns, MAGIC, MAGIC, ADD, SUB))
            m = V_([m] + act.last(), lambda: V.scalar_tensor_tensor(red, turns, -TWO_PI[0], ang, MUL, ADD))
            m = V_([m], lambda: V.scalar_tensor_tensor(red, turns, -TWO_PI[1], red, MUL, ADD))
            m = V_([m], lambda: V.scalar_tensor_tensor(red, turns, -TWO_PI[2], red, MUL, ADD))
            m = V_([m], lambda s=shift: V.tensor_scalar(red, red, float(2 * np.pi * s), 3.1415925, ADD, MIN))
            m = V_([m], lambda: V.tensor_scalar(red, red, -3.1415925, None, MAX))
            act.do([m], lambda tb=table: S.activation(tb[:, :], red, ACT.Sin))

        def inverse_root(dst, src, after, scale, eps=EPS, n=None, gain=1.0):
            n = dst.shape[1]
            p = dst.shape[0]
            m = V_(after, lambda: V.tensor_scalar(dst, src, scale, eps, MUL, ADD))
            m = pool.do([m], lambda: G.tensor_tensor(dst, dst, minus_half[0:p, 0:n], ALU.pow))
            if gain != 1.0:
                m = V_([m], lambda: V.tensor_scalar(dst, dst, gain, None, MUL))
            return m

        def norm_T(src, dstT, gain_at, scaled, after):
            marks = []
            for t in range(NT):
                m = act.do(after, lambda t=t: S.activation(scaled[:, t, :], src[:, t, :], ACT.Square,
                                                           accum_out=ssq[:, t:t + 1]))
                m = inverse_root(inv_rms[:, t:t + 1], ssq[:, t:t + 1], [m], 1.0 / D)
                m = V_([m], lambda t=t: V.tensor_scalar(scaled[:, t, :], src[:, t, :], inv_rms[:, t:t + 1], None, MUL))
                for g in range(2):
                    b, free = take()
                    mt = pe.do([m] + free, *[tr(psum[:, b, P * j:P * j + P],
                                                scaled[:, t, P * (4 * g + j):P * (4 * g + j + 1)]) for j in range(4)])
                    c = gain_at + 4 * g
                    mv = V_([mt], lambda b=b, g=g, t=t, c=c: V.tensor_tensor(
                        dstT[:, 4 * g:4 * g + 4, P * t:P * t + P],
                        psum[:, b, :].rearrange("p (j n) -> p j n", j=4),
                        gains[:, c:c + 4].unsqueeze(2).to_broadcast([P, 4, P]), MUL))
                    bank_free[b] = [mv]
                    marks.append(mv)
            return marks

        def load_post(src, k):
            return load(post_w[:, k, :], src.partition_broadcast(P), group="post_gain")

        def residual(done, wrow, wmark, scratch, half):
            for t in range(NT):
                h = psum[:, 2 * t:2 * t + 2, :]
                sc = scratch[:, t, :].rearrange("p (n c) -> p n c", n=2)
                m = act.do(done, lambda h=h, sc=sc, t=t: S.activation(sc, h, ACT.Square, accum_out=ssq[:, t:t + 1]))
                m = inverse_root(inv_rms[:, t:t + 1], ssq[:, t:t + 1], [m], 1.0 / D, gain=half)
                w = wrow.rearrange("p (n c) -> p n c", n=2)
                m = V_([m, wmark], lambda h=h, sc=sc, t=t, w=w: V.scalar_tensor_tensor(
                    sc, h, inv_rms[:, t:t + 1], w, MUL, MUL))
                bank_free[2 * t] = bank_free[2 * t + 1] = [m]
                m = V_([m], lambda t=t: V.tensor_tensor(x[:, t, :], x[:, t, :], scratch[:, t, :], ADD))
            return [m]

        def dump(name, tile, marks):
            if dbg and name in dbg:
                load(dbg[name], tile, marks + dve.last() + act.last() + pool.last() + pe.last(), group="dump")

        def ffn(wg, wu, wd, gain_at, post_src):
            stage_start()
            wmark = load_post(post_src, 0)
            scaled = carve(NT, D)
            silu, h32 = carve(2, TOK), carve(2, TOK)
            n_groups = D_FF // 256
            sources = []
            for i in range(n_groups + 1):
                if i < n_groups:
                    sources += [columns(wg, 256 * i), columns(wu, 256 * i)]
                if i:
                    sources.append(rows(wd, 2 * (i - 1)))
            stream = SplitStream(sources)
            stream.ahead(2)
            ready = split_xn(norm_T(x, xnT, gain_at, scaled, []))
            stream.ahead(4)
            h_ready, h_read, h32_read = [None] * n_groups, [[] for _ in range(NH)], [[], []]
            for i in range(n_groups + 1):
                if i < n_groups:
                    kg, gv, gland = stream.next()
                    ku, uv, uland = stream.next()
                    evac = []
                    for j in range(2):
                        b, free = take()
                        m = pe.do([gland, uland] + free + ready,
                                  *[op for o, wv in ((0, gv), (1, uv)) for k in range(KD) for op in
                                    three(psum[:, b, 256 * o:256 * o + 256], [wv[h][:, k, P * j:P * j + P] for h in range(2)],
                                          [x_hl[:, h, k, :] for h in range(2)], k == 0, k == KD - 1)])
                        evac.append((b, m))
                    hl_free[kg] = hl_free[ku] = [m]
                    for j, (b, m) in enumerate(evac):
                        ma = act.do([m] + h32_read[j], lambda b=b, j=j: S.activation(silu[:, j, :], psum[:, b, 0:256], ACT.Silu))
                        mv = V_([ma] + h32_read[j], lambda b=b, j=j: V.tensor_tensor(h32[:, j, :], silu[:, j, :], psum[:, b, 256:512], MUL))
                        bank_free[b] = [mv]
                        h_ready[i] = split(h32[:, j, :], h_hl[:, i % NH, 0, j, :], h_hl[:, i % NH, 1, j, :], [mv] + h_read[i % NH])
                        h32_read[j] = [h_ready[i]]
                    stream.ahead(3)
                if i:
                    g = (i - 1) % NH
                    done = split_out(stream, lambda h, j, g=g: h_hl[:, g, h, j, :], i == 1, i == n_groups, [h_ready[i - 1]])
                    h_read[g] = [done]
                    stream.ahead(4)
            residual([done], post_w[:, 0, :], wmark, scaled, 0.5)

        def inverses(systems, size, per, masks, levels, fill, LM, W, taken):
            p = size
            state = []
            for s, (L, X, XT, lm) in enumerate(systems):
                state.append(dict(L=L, X=X, XT=XT, lm=lm, x=[], xt=[]))
            lm_read = [list(taken) for _ in systems]
            eye = ident[0:p, 0:p].unsqueeze(1).to_broadcast([p, per, size])
            for n, b_size in enumerate(levels):
                for s, st in enumerate(state):
                    mk = C(masks[s])[0:p, P * n:P * n + size].unsqueeze(1).to_broadcast([p, per, size])
                    lmm = pool.do(st["lm"] + lm_read[s], lambda s=s, st=st, mk=mk: G.tensor_tensor(
                        LM[0:p, s], st["L"], mk, MUL))
                    b, free = take(range(8))
                    bv = psum[0:p, b, :].rearrange("p (h n) -> p h n", h=per)
                    if n == 0:
                        m = pe.do([lmm] + free, *[mm(bv[:, h, :], LM[0:p, s, h, :], ident[0:p, 0:p]) for h in range(per)])
                        st["x"] = [V_([lmm], lambda s=s, st=st: V.tensor_tensor(st["X"], eye, LM[0:p, s], SUB))]
                        st["xt"] = [V_([m], lambda st=st, bv=bv: V.tensor_tensor(st["XT"], eye, bv, SUB))]
                        bank_free[b] = st["xt"]
                        lm_read[s] = st["x"] + [m]
                        continue
                    m = pe.do([lmm] + free + st["xt"], *[mm(bv[:, h, :], LM[0:p, s, h, :], st["XT"][:, h, :])
                                                        for h in range(per)])
                    lm_read[s] = [m]
                    mw = act.do([m], lambda s=s, bv=bv: S.copy(W[0:p, s], bv))
                    bank_free[b] = [mw]
                    last = n == len(levels) - 1
                    b2, free2 = take(range(8))
                    b2v = psum[0:p, b2, :].rearrange("p (h n) -> p h n", h=per)
                    m2 = pe.do([mw] + free2 + st["x"], *[mm(b2v[:, h, :], st["X"][:, h, :], W[0:p, s, h, :]) for h in range(per)])
                    if not last:
                        b1, free1 = take(range(8))
                        b1v = psum[0:p, b1, :].rearrange("p (h n) -> p h n", h=per)
                        m1 = pe.do([mw] + free1 + st["x"], *[mm(b1v[:, h, :], W[0:p, s, h, :], st["X"][:, h, :]) for h in range(per)])
                    else:
                        m1 = m2
                    st["xt"] = [V_([m2, m1], lambda st=st, b2v=b2v: V.tensor_tensor(st["XT"], st["XT"], b2v, SUB))]
                    bank_free[b2] = st["xt"]
                    if not last:
                        st["x"] = [V_([m1], lambda st=st, b1v=b1v: V.tensor_tensor(st["X"], st["X"], b1v, SUB))]
                        bank_free[b1] = st["x"]
                    lm_read[s] = [m]
                fill(n)
            return [st["xt"] for st in state]

        def softplus(dst, src, scratch, after):
            m = act.do(after, lambda: S.activation(scratch, src, ACT.Abs))
            m = act.do([m], lambda: S.activation(scratch, scratch, ACT.Exp, scale=-1.0))
            m = act.do([m], lambda: S.activation(scratch, scratch, ACT.Ln, bias=1.0))
            return V_([m], lambda: V.scalar_tensor_tensor(dst, src, 0.0, scratch, MAX, ADD))

        WORK8 = tuple(range(8))

        def mixer(l):
            stage_start()
            wmark = load_post(a["norm_post"][l, 1], 0)
            w = a["w_in"][l]
            W = 512
            mix = carve(NT, D)
            scaled = mix
            ready = norm_T(x, xnT, 32 * l + 8, scaled, [])
            colN = lambda c0, n=256: project_N(w, c0, xnT, ready, n, banks=WORK8)
            colT = lambda c0: project_T(w, c0, xnT, ready, banks=WORK8)

            ab = carve(NT, 16)
            g_a, sp_s, g, beta, ea = carve(NT, 8), carve(NT, 8), carve(NT, 8), carve(NT, 8), carve(8)
            b, pv, m = colN(8 * W, 16)
            m = V_([m], lambda pv=pv: V.tensor_copy(ab, pv))
            bank_free[b] = [m]
            mb = act.do([m], lambda: S.activation(beta, ab[:, :, 8:16], ACT.Sigmoid))
            mea = act.do([], lambda: S.activation(ea, alog[:, 8 * l:8 * l + 8], ACT.Exp))
            m = V_([m], lambda: V.tensor_tensor(g_a, ab[:, :, 0:8], dtb[:, 8 * l:8 * l + 8].unsqueeze(1).to_broadcast([P, NT, 8]), ADD))
            m = softplus(g, g_a, sp_s, [m])
            gm = V_([m, mea], lambda: V.scalar_tensor_tensor(g, g, -1.0, ea.unsqueeze(1).to_broadcast([P, NT, 8]), MUL, MUL))

            raw = carve(12, TOK + 4)
            qkv = carve(12, TOK)
            zero = pool.do([], lambda: G.memset(raw[:, :, 0:2], 0.0), lambda: G.memset(raw[:, :, TOK + 2:TOK + 4], 0.0))
            silu_done = []
            for i in range(6):
                b, pv, m = colT(4 * W + 256 * i)
                m = act.do([m, zero], lambda i=i, pv=pv: S.copy(raw[:, 2 * i:2 * i + 2, 2:TOK + 2], pv))
                bank_free[b] = [m]
                for c in (2 * i, 2 * i + 1):
                    tap = lambda j, c=c: taps[:, 60 * l + 12 * j + c:60 * l + 12 * j + c + 1]
                    mc = V_([m, zero], lambda c=c, tap=tap: V.tensor_scalar(qkv[:, c, :], raw[:, c, 0:TOK], tap(0), None, MUL))
                    for j in range(1, 5):
                        mc = V_([mc], lambda c=c, j=j, tap=tap: V.scalar_tensor_tensor(
                            qkv[:, c, :], raw[:, c, j:j + TOK], tap(j), qkv[:, c, :], MUL, ADD))
                silu_done.append(act.do([mc], lambda i=i: S.activation(qkv[:, 2 * i:2 * i + 2, :], qkv[:, 2 * i:2 * i + 2, :], ACT.Silu)))
            qT, kT, vT = qkv[:, 0:4, :], qkv[:, 4:8, :], qkv[:, 8:12, :]

            norm_s = carve(2, TOK)
            qk_done = [None] * 4
            nfree = []
            for i in range(4):
                sl = qkv[:, 2 * i:2 * i + 2, :]
                m = pool.do([silu_done[i]] + nfree, lambda sl=sl: G.tensor_tensor(norm_s, sl, sl, MUL))
                b, free = take(WORK8)
                m = pe.do([m] + free, mm(psum[:, b, :], C("ones"), norm_s.rearrange("p a b -> p (a b)")))
                pv = psum[:, b, :].rearrange("p (a b) -> p a b", a=2)
                m = V_([m], lambda pv=pv: V.tensor_scalar(norm_s, pv, EPS, None, ADD))
                bank_free[b] = [m]
                m = act.do([m], lambda: S.activation(norm_s, norm_s, ACT.Sqrt))
                m = V_([m], lambda: V.reciprocal(norm_s, norm_s))
                sc = HD ** -0.5 if i < 2 else 1.0
                m = V_([m], lambda sl=sl, sc=sc: V.scalar_tensor_tensor(sl, sl, sc, norm_s, MUL, MUL))
                qk_done[i] = m
                nfree = [m]
            dump("qkv", qkv, nfree)

            kN, vN = carve(NT, HEADS, HD), carve(NT, HEADS, HD)
            kv_nat = []
            for src, dst, dep in ((kT, kN, qk_done[2:]), (vT, vN, silu_done[4:])):
                for t in range(NT):
                    b, free = take(WORK8)
                    m = pe.do(list(dep) + free, *[tr(psum[:, b, P * h:P * h + P], src[:, h, P * t:P * t + P]) for h in range(4)])
                    m = act.do([m], lambda dst=dst, t=t, b=b: S.copy(dst[:, t], psum[:, b, :].rearrange("p (h d) -> p h d", h=4)))
                    bank_free[b] = [m]
                    kv_nat.append(m)

            combos = [(d, t) for d in range(2) for t in range(NT)]
            first = {0: 0, 1: 1}
            order = ("upto", "from")
            Gn, Gt = carve(4, 4), carve(4, 4)
            b, free = take(WORK8)
            ops = [mm(psum[:, b, 4 * c:4 * c + 4], C(order[d]), g[:, t, 4 * d:4 * d + 4]) for c, (d, t) in enumerate(combos)]
            ops += [mm(psum[:, b, 16 + 4 * c:20 + 4 * c], C("ones"), g[:, t, 4 * d:4 * d + 4]) for c, (d, t) in enumerate(combos)]
            m = pe.do([gm] + free, *ops)
            gn = V_([m], lambda b=b: V.tensor_copy(Gn, psum[:, b, 0:16].rearrange("p (c h) -> p c h", c=4)),
                    lambda b=b: V.tensor_copy(Gt, psum[:, b, 16:32].rearrange("p (c h) -> p c h", c=4)))
            bank_free[b] = [gn]
            tail, ebg = carve(4, 4), carve(4, 4)
            m = V_([gn], lambda: V.tensor_tensor(tail, Gt, Gn, SUB))
            mt_ = act.do([m], lambda: S.activation(tail, tail, ACT.Exp))
            m = act.do([gn], lambda: S.activation(ebg, Gn, ACT.Exp))
            me = V_([m, mb], *[lambda c=c, d=d, t=t: V.tensor_tensor(ebg[:, c], ebg[:, c], beta[:, t, 4 * d:4 * d + 4], MUL)
                               for c, (d, t) in enumerate(combos)])

            L, X, XT = carve(4, 4, P), carve(4, 4, P), carve(4, 4, P)
            QK = carve(4, 4, P)
            qg, vb, kbg, kt = carve(2, 4, P), carve(4, 4, P), carve(2, 4, P), carve(2, 4, P)
            dec = raw.rearrange("p a b -> p (a b)")[:, 0:1024].rearrange("p (a h n) -> p a h n", a=2, h=4)
            dec_read = [silu_done[-1]]
            lmarks, qkmarks, vbm, qgm, kbm, ktm = [], [], [], {}, {}, {}
            bc = lambda v: v.unsqueeze(2).to_broadcast([P, 4, P])
            for c, (d, t) in enumerate(combos):
                later = t != first[d]
                b, free = take(WORK8)
                bv = psum[:, b, :].rearrange("p (h n) -> p h n", h=4)
                m = pe.do([gm] + free, *[mm(bv[:, h, :], g[:, t, 4 * d + h:4 * d + h + 1].to_broadcast([P, P]), C(order[d])) for h in range(4)])
                m1 = V_([m, gn] + dec_read, *[lambda h=h, c=c, bv=bv: V.tensor_scalar(dec[:, 0, h, :], bv[:, h, :], Gn[:, c, h:h + 1], 0.0, SUB, MAX) for h in range(4)])
                m2 = V_([m1], *[lambda h=h, c=c, bv=bv: V.tensor_scalar(dec[:, 1, h, :], bv[:, h, :], Gn[:, c, h:h + 1], 0.0, SUB, MIN) for h in range(4)])
                fr = [m2]
                if later:
                    mq = act.do([m] + fr, lambda c=c, d=d, bv=bv: S.activation(qg[:, d], bv, ACT.Exp))
                    fr = fr + [mq]
                    qgm[d] = pool.do([mq] + qk_done[0:2], lambda d=d, t=t: G.tensor_tensor(qg[:, d], qg[:, d], qT[:, :, P * t:P * t + P], MUL))
                bank_free[b] = fr
                ma = act.do([m1], lambda: S.activation(dec[:, 0], dec[:, 0], ACT.Exp, scale=-1.0))
                mb2 = act.do([m2], lambda: S.activation(dec[:, 1], dec[:, 1], ACT.Exp))
                b1, free = take(WORK8)
                b1v = psum[:, b1, :].rearrange("p (h n) -> p h n", h=4)
                mk = pe.do(qk_done[2:] + free, *[mm(b1v[:, h, :], kT[:, h, P * t:P * t + P], kT[:, h, P * t:P * t + P]) for h in range(4)])
                ml = V_([mk, ma, mb], *[lambda h=h, c=c, d=d, t=t, b1v=b1v: V.scalar_tensor_tensor(
                    L[:, c, h, :], b1v[:, h, :], beta[:, t, 4 * d + h:4 * d + h + 1], dec[:, 0, h, :], MUL, MUL) for h in range(4)])
                bank_free[b1] = [ml]
                lmarks.append(ml)
                b2, free = take(WORK8)
                b2v = psum[:, b2, :].rearrange("p (h n) -> p h n", h=4)
                mk = pe.do(qk_done + free, *[mm(b2v[:, h, :], kT[:, h, P * t:P * t + P], qT[:, h, P * t:P * t + P]) for h in range(4)])
                mi = pool.do([mb2], lambda d=d: G.tensor_tensor(dec[:, 1], dec[:, 1], C(order[d]).unsqueeze(1).to_broadcast([P, 4, P]), MUL))
                mq = V_([mk, mi], lambda c=c, b2v=b2v: V.tensor_tensor(QK[:, c], b2v, dec[:, 1], MUL))
                bank_free[b2] = [mq]
                qkmarks.append(mq)
                dec_read = [mq, ml]
                vbm.append(pool.do(kv_nat[2:] + [mb], lambda c=c, d=d, t=t: G.tensor_tensor(vb[:, c], vN[:, t], bc(beta[:, t, 4 * d:4 * d + 4]), MUL)))
                if later:
                    kbm[d] = pool.do(kv_nat[:2] + [me], lambda c=c, d=d, t=t: G.tensor_tensor(kbg[:, d], kN[:, t], bc(ebg[:, c]), MUL))
                else:
                    ktm[d] = pool.do(kv_nat[:2] + [mt_], lambda c=c, d=d, t=t: G.tensor_tensor(kt[:, d], kN[:, t], bc(tail[:, c]), MUL))

            wk, wv_ = a["xattn_k"][l], a["xattn_v"][l]
            qr = raw.rearrange("p a b -> p (a b)")[:, 0:2048].rearrange("p (a b) -> p a b", a=8)
            rv = vN.rearrange("p t h d -> p t (h d)")
            rg, z = (tail_2k[:, 1024 * k:1024 * k + 1024].rearrange("p (t n) -> p t n", t=NT) for k in range(2))
            ret_in = []
            r_marks = {}

            def keep(b, pv, m, dst, key, fn=None):
                if fn is None:
                    m = act.do([m] + dec_read + vbm, lambda: S.copy(dst, pv))
                else:
                    m = act.do([m], lambda: S.activation(dst, pv, fn))
                bank_free[b] = [m]
                r_marks[key] = m

            fills = []
            for i in range(4):
                fills.append(lambda i=i: keep(*colT(256 * i), qr[:, 2 * i:2 * i + 2, :], ("r", i)))
            for i in range(2):
                fills.append(lambda i=i: keep(*colN(2 * W + 256 * i), rv[:, :, 256 * i:256 * i + 256], ("v", i)))
            for i in range(4):
                fills.append(lambda i=i: keep(*project_T(wk, 256 * i, memT, [], WORK8), memkT[:, 2 * i:2 * i + 2, :], ("mk", i)))
                fills.append(lambda i=i: keep(*project_N(wv_, 256 * i, memT, [], banks=WORK8), memv[:, :, 256 * i:256 * i + 256], ("mv", i)))
            for i in range(2):
                fills.append(lambda i=i: keep(*colN(3 * W + 256 * i), rg[:, :, 256 * i:256 * i + 256], ("g", i), ACT.Silu))
                fills.append(lambda i=i: keep(*colN(7 * W + 256 * i), z[:, :, 256 * i:256 * i + 256], ("z", i), ACT.Silu))

            def fill(n):
                for _ in range(3):
                    if fills:
                        fills.pop(0)()

            xts = inverses([(L[:, c], X[:, c], XT[:, c], [lmarks[c]]) for c in range(4)], P, 4,
                           ["fwd", "fwd", "bwd", "bwd"], LEVELS, fill,
                           mix.rearrange("p t (a h n) -> p (t a) h n", h=4, n=P),
                           qkv[:, 0:8, :].rearrange("p (c b) (h n) -> p c (b h) n", c=4, h=2),
                           qk_done + qkmarks + kv_nat + list(qgm.values()))
            while fills:
                fills.pop(0)()

            u = L
            wT = X
            um, wm = [], {}
            for c, (d, t) in enumerate(combos):
                b, free = take(WORK8)
                bv = psum[:, b, :].rearrange("p (h n) -> p h n", h=4)
                m = pe.do(xts[c] + [vbm[c]] + free, *[mm(bv[:, h, :], XT[:, c, h, :], vb[:, c, h, :]) for h in range(4)])
                m = V_([m], lambda c=c, bv=bv: V.tensor_copy(u[:, c], bv))
                bank_free[b] = [m]
                um.append(m)
                if t != first[d]:
                    b, free = take(WORK8)
                    bv2 = psum[:, b, :].rearrange("p (h n) -> p h n", h=4)
                    m = pe.do(xts[c] + [kbm[d]] + free, *[mm(bv2[:, h, :], kbg[:, d, h, :], XT[:, c, h, :]) for h in range(4)])
                    m = act.do([m], lambda c=c, bv2=bv2: S.copy(wT[:, c], bv2))
                    bank_free[b] = [m]
                    wm[d] = m
            state = kN
            stm = {}
            for d in range(2):
                c1 = combos.index((d, first[d]))
                c2 = combos.index((d, 1 - first[d]))
                b, free = take(WORK8)
                bv = psum[:, b, :].rearrange("p (h n) -> p h n", h=4)
                m = pe.do([um[c1], ktm[d]] + free, *[mm(bv[:, h, :], kt[:, d, h, :], u[:, c1, h, :]) for h in range(4)])
                m = act.do([m] + list(kbm.values()) + list(ktm.values()), lambda d=d, bv=bv: S.copy(state[:, d], bv))
                bank_free[b] = [m]
                stm[d] = m
                b, free = take(WORK8)
                bv2 = psum[:, b, :].rearrange("p (h n) -> p h n", h=4)
                m = pe.do([stm[d], wm[d]] + free, *[mm(bv2[:, h, :], wT[:, c2, h, :], state[:, d, h, :]) for h in range(4)])
                m = V_([m, um[c2]], lambda c2=c2, bv2=bv2: V.tensor_tensor(u[:, c2], u[:, c2], bv2, SUB))
                bank_free[b] = [m]
                um[c2] = m
            r4 = carve(4, 4)
            sq = kbg[:, 1]
            mix_marks = []
            for t in range(NT):
                b, free = take(WORK8)
                bv = psum[:, b, :].rearrange("p (h n) -> p h n", h=4)
                ops = []
                dl = t if first[0] != t else 1
                for h in range(4):
                    dlate = 0 if first[0] != t else 1
                    dearly = 1 - dlate
                    cl, ce = combos.index((dlate, t)), combos.index((dearly, t))
                    ops += [mm(bv[:, h, :], qg[:, dlate, h, :], state[:, dlate, h, :], True, False),
                            mm(bv[:, h, :], QK[:, cl, h, :], u[:, cl, h, :], False, False),
                            mm(bv[:, h, :], QK[:, ce, h, :], u[:, ce, h, :], False, True)]
                m = pe.do(um + qkmarks + [qgm[0], qgm[1], stm[0], stm[1]] + free, *ops)
                ms = act.do([m] + mix_marks + list(wm.values()), lambda bv=bv: S.activation(sq, bv, ACT.Square))
                mr = V_([ms], lambda t=t: V.tensor_reduce(r4[:, t], sq, AXX, ADD))
                mr = inverse_root(r4[:, t], r4[:, t], [mr], 1.0 / HD)
                o = mix[:, t, W:2 * W].rearrange("p (h n) -> p h n", h=4)
                mo = V_([mr], lambda t=t, o=o, bv=bv: V.tensor_tensor(o, bv, bc(r4[:, t]), MUL))
                bank_free[b] = [mo]
                mo = pool.do([mo], lambda o=o: G.tensor_tensor(o, o, gnw[:, P * l:P * l + P].unsqueeze(1).to_broadcast([P, 4, P]), MUL))
                mo = pool.do([mo, r_marks[("z", 0)], r_marks[("z", 1)]], lambda t=t: G.tensor_tensor(mix[:, t, W:2 * W], mix[:, t, W:2 * W], z[:, t, :], MUL))
                mix_marks = [mo]
            gdn_done = mix_marks
            dump("mix", mix, gdn_done)

            rT = qkv[:, 0:8, :]
            rot_s = kbg[:, 0].rearrange("p (a b) n -> p a (b n)", a=2)
            rr = []
            rfree = um
            for i in range(4):
                src = qr[:, 2 * i:2 * i + 2, :]
                b, free = take(WORK8)
                pv = psum[:, b, :].rearrange("p (a b) -> p a b", a=2)
                m = pe.do([r_marks[("r", i)]] + free, mm(psum[:, b, :], C("rotate"), src.rearrange("p a b -> p (a b)")))
                m = V_([m] + rfree, lambda pv=pv: V.tensor_tensor(rot_s, pv, sinT[:, :].unsqueeze(1).to_broadcast([P, 2, TOK]), MUL))
                bank_free[b] = [m]
                m2 = pool.do([r_marks[("r", i)]] + um, lambda i=i, src=src: G.tensor_tensor(rT[:, 2 * i:2 * i + 2, :], src, cosT[:, :].unsqueeze(1).to_broadcast([P, 2, TOK]), MUL))
                m = V_([m, m2], lambda i=i: V.tensor_tensor(rT[:, 2 * i:2 * i + 2, :], rT[:, 2 * i:2 * i + 2, :], rot_s, ADD))
                rfree = [m]
                rr.append(m)
            decay = vb.rearrange("p c h n -> p (c h n)").rearrange("p (h m) -> p h m", h=4)
            PT = QK.rearrange("p c h n -> p (c h n)").rearrange("p (h m) -> p h m", h=4)
            ptm = []
            for h in range(4):
                gf, gb = lg[:, 8 * l + h:8 * l + h + 1], lg[:, 8 * l + 4 + h:8 * l + 5 + h]
                m = V_(gdn_done + um, lambda h=h, gf=gf: V.tensor_scalar(decay[:, h, :], C("ahead"), gf, None, MUL))
                m = V_([m], lambda h=h, gb=gb: V.scalar_tensor_tensor(decay[:, h, :], C("behind"), gb, decay[:, h, :], MUL, ADD))
                md = act.do([m], lambda h=h: S.activation(decay[:, h, :], decay[:, h, :], ACT.Exp))
                b, free = take(WORK8)
                m = pe.do([rr[h // 2], rr[2 + h // 2]] + free, *[mm(psum[:, b, 256 * j:256 * j + 256], rT[:, 4 + h, P * j:P * j + P], rT[:, h, :]) for j in range(2)])
                m = V_([m, md], lambda h=h, b=b: V.scalar_tensor_tensor(PT[:, h, :], psum[:, b, :], HD ** -0.5, decay[:, h, :], MUL, MUL))
                bank_free[b] = [m]
                ptm.append(m)
            for t in range(NT):
                b, free = take(WORK8)
                bv = psum[:, b, :].rearrange("p (h n) -> p h n", h=4)
                m = pe.do(ptm + [r_marks[("v", 0)], r_marks[("v", 1)]] + free,
                          *[mm(bv[:, h, :], PT[:, h, 256 * j + P * t:256 * j + P * t + P], rv[:, j, HD * h:HD * h + HD], j == 0, j == 1)
                            for h in range(4) for j in range(2)])
                o = mix[:, t, 0:W].rearrange("p (h n) -> p h n", h=4)
                mu, var = r4[:, 2, :], r4[:, 3, :]
                mm_ = V_([m], lambda bv=bv: V.tensor_reduce(mu, bv, AXX, ADD))
                mm_ = V_([mm_], lambda: V.tensor_scalar(mu, mu, 1.0 / HD, None, MUL))
                mc = V_([mm_], lambda o=o, bv=bv: V.tensor_tensor(o, bv, bc(mu), SUB))
                bank_free[b] = [mc]
                ms = act.do([mc] + gdn_done, lambda o=o: S.activation(sq, o, ACT.Square))
                mr = V_([ms], lambda: V.tensor_reduce(var, sq, AXX, ADD))
                mr = inverse_root(var, var, [mr], 1.0 / HD)
                m = V_([mr], lambda o=o: V.tensor_tensor(o, o, bc(var), MUL))
                m = pool.do([m, r_marks[("g", 0)], r_marks[("g", 1)]], lambda t=t: G.tensor_tensor(mix[:, t, 0:W], mix[:, t, 0:W], rg[:, t, :], MUL))
                gdn_done = gdn_done + [m]
            dump("mix2", mix, gdn_done)
            mixed = to_T(mix, mixT, gdn_done)
            for i in range(4):
                done = project_out(a["w_out"][l], 2 * i, 2, mixT, KD, mixed)
            residual([done], post_w[:, 0, :], wmark, scaled, 1.0)

        def to_T(src, dstT, after, tiles=range(KD)):
            marks = []
            tiles = list(tiles)
            for t in range(NT):
                for g in range(0, len(tiles), 4):
                    n = min(4, len(tiles) - g)
                    b, free = take()
                    m = pe.do(after + free, *[tr(psum[:, b, P * j:P * j + P], src[:, t, P * (g + j):P * (g + j + 1)]) for j in range(n)])
                    m = V_([m], lambda b=b, g=g, t=t, n=n: V.tensor_copy(
                        dstT[:, tiles[g]:tiles[g] + n, P * t:P * t + P], psum[:, b, 0:P * n].rearrange("p (j n) -> p j n", j=n)))
                    bank_free[b] = [m]
                    marks.append(m)
            return marks

        def cross(l):
            stage_start()
            wmark = load_post(a["norm_post"][l, 2], 0)
            scaled = carve(NT, D)
            stream = SplitStream([columns(a["xattn_q"][l], 256 * i) for i in range(4)] + [rows(a["xattn_o"][l], 2 * i) for i in range(4)])
            stream.ahead(2)
            ready = split_xn(norm_T(x, xnT, 32 * l + 16, scaled, []))
            stream.ahead(4)
            qT, oT = xnT, carve(KD, TOK)
            qm = []
            for i in range(4):
                b, pv, m = split_project_T(stream, ready)
                m = act.do([m] + ready, lambda i=i, pv=pv: S.copy(qT[:, 2 * i:2 * i + 2, :], pv))
                bank_free[b] = [m]
                qm.append(m)
            stream.ahead(4)
            prob, PT = scaled.rearrange("p t (h m) -> p h t m", h=HEADS), carve(HEADS, NT, TOK)
            top, total = (softmax_s[:, 8 * k:8 * k + 8].rearrange("p (h t) -> p h t", h=HEADS) for k in range(2))
            scale = 256 ** -0.5
            om = []
            for h in range(HEADS):
                b, free = take()
                m = pe.do([qm[h]] + free, *[mm(psum[:, b, 256 * t:256 * t + 256], qT[:, 2 * h + k, P * t:P * t + P], memkT[:, 2 * h + k, :], k == 0, k == 1)
                                            for t in range(NT) for k in range(2)])
                pv = psum[:, b, :].rearrange("p (t m) -> p t m", t=2)
                m = V_([m], lambda h=h, pv=pv: V.tensor_reduce(top[:, h], pv, AXX, MAX))
                m = V_([m], lambda h=h: V.tensor_scalar(top[:, h], top[:, h], -scale, None, MUL))
                for t in range(NT):
                    m = act.do([m], lambda h=h, t=t, pv=pv: S.activation(prob[:, h, t, :], pv[:, t, :], ACT.Exp, bias=top[:, h, t:t + 1],
                                                                        scale=scale, accum_out=total[:, h, t:t + 1]))
                bank_free[b] = [m]
                m = V_([m], lambda h=h: V.reciprocal(total[:, h], total[:, h]))
                m = V_([m], *[lambda h=h, t=t: V.tensor_scalar(prob[:, h, t, :], prob[:, h, t, :], total[:, h, t:t + 1], None, MUL) for t in range(2)])
                b, free = take()
                m = pe.do([m] + free, *[tr(psum[:, b, 256 * j + P * t:256 * j + P * t + P], prob[:, h, t, P * j:P * j + P]) for j in range(2) for t in range(2)])
                m = V_([m], lambda h=h, b=b: V.tensor_copy(PT[:, h], psum[:, b, :].rearrange("p (j t) -> p j t", j=2)))
                bank_free[b] = [m]
                b, free = take()
                m = pe.do([m] + free, *[mm(psum[:, b, 256 * e:256 * e + 256], memv[:, j, 256 * h + P * e:256 * h + P * e + P], PT[:, h, j, :], j == 0, j == 1)
                                        for e in range(2) for j in range(2)])
                m = act.do([m], lambda h=h, b=b: S.copy(oT[:, 2 * h:2 * h + 2, :], psum[:, b, :].rearrange("p (j t) -> p j t", j=2)))
                bank_free[b] = [m]
                om.append(split(oT[:, 2 * h:2 * h + 2, :], x_hl[:, 0, 2 * h:2 * h + 2, :], x_hl[:, 1, 2 * h:2 * h + 2, :], [m]))
            for i in range(4):
                done = split_out(stream, lambda h, j, i=i: x_hl[:, h, 2 * i + j, :], i == 0, i == 3, [om[i]])
            residual([done], post_w[:, 0, :], wmark, scaled, 1.0)

        for l in range(DEPTH):
            ffn(a["ffn1_gate"][l], a["ffn1_up"][l], a["ffn1_down"][l], 32 * l, a["norm_post"][l, 0])
            dump(f"x{l}0", x[:, :, :], [])
            stage_start()
            mem_in = carve(NT, D)
            mem_s = carve(NT, D)
            mload = load(mem_in, a["mem"][0].rearrange("(t p) d -> p t d", p=P), group="memory")
            norm_T(mem_in, memT, 64 + 8 * l, mem_s, [mload])
            keep_tail[0] = True
            mixer(l)
            keep_tail[0] = False
            dump(f"x{l}1", x[:, :, :], [])
            cross(l)
            dump(f"x{l}2", x[:, :, :], [])
            ffn(a["ffn2_gate"][l], a["ffn2_up"][l], a["ffn2_down"][l], 32 * l + 24, a["norm_post"][l, 3])
            dump(f"x{l}3", x[:, :, :], [])

        def mixer2():
            stage_start()
            wmark = load_post(a["norm_mix_post_2"][0], 0)
            w = a["w_in_2"][0]
            spare = [memkT[:, :, :].rearrange("p k t -> p (k t)"), memv[:, :, :].rearrange("p t d -> p (t d)")]
            shaped = lambda v, *s_: v.rearrange("p (a b) -> p a b", a=s_[0]) if len(s_) == 1 else \
                v.rearrange("p (a b c) -> p a b c", a=s_[0], b=s_[1])
            scaled = carve(NT, D)
            A0, H0, R0, U0 = 0, 768, 1792, 2688
            reach = carve(4, 384)
            rb = a["attn_rel_bias_2"]
            for h in range(4):
                load(reach[:, h, :], bass.AP(rb.tensor, h * 513 + 1, [[1, P], [1, 384]]), group="small2")
            lora = carve(256)
            load(lora[0:32, :], a["rwkv_w2_2"][0], group="small2")
            load(lora[32:64, :], a["rwkv_a2_2"][0], group="small2")
            load(lora[64:128, :], a["rwkv_g2_2"][0], group="small2")
            gate_w = carve(2, 2, P)
            zm = pool.do([], lambda: G.memset(gate_w, 0.0))
            for k, name in enumerate(("lru_wa_2", "lru_wx_2")):
                for n in range(4):
                    small2 = load(gate_w[64 * (n % 2):64 * (n % 2) + 64, k, n // 2, 64 * (n % 2):64 * (n % 2) + 64],
                                  a[name][0, n], [zm], group="small2")
            ready = norm_T(x, xnT, 80, scaled, [])
            colT = lambda c0: project_T(w, c0, xnT, ready, banks=WORK8)
            colN = lambda c0: project_N(w, c0, xnT, ready, banks=WORK8)

            def kept(job, dst, fn=None, after=(), **kw):
                b, pv, m = job
                if fn is None:
                    m = act.do([m] + list(after), lambda: S.copy(dst, pv))
                else:
                    m = act.do([m] + list(after), lambda: S.activation(dst, pv, fn, **kw))
                bank_free[b] = [m]
                return m

            def half_sums(src, after):
                b, free = take(WORK8)
                m = pe.do(list(after) + free, mm(psum[:, b, :], C("half"), src))
                return b, psum[:, b, :].rearrange("p (j t) -> p j t", j=2), m

            pc = carve(7, TOK + 1)
            xs = carve(7, TOK)
            zc = pool.do([], lambda: G.memset(pc[:, :, 0:1], 0.0))
            pm = []
            for i in range(3):
                pm.append(kept(colT(R0 + 256 * i), pc[:, 2 * i:2 * i + 2, 1:TOK + 1]))
            s, wv, landed = slab(*columns(w, R0 + 768, P))
            b, free = take(WORK8)
            m = pe.do([landed] + free + ready, *[mm(psum[:, b, 0:256], wv[:, k, :], xnT[:, k, :], k == 0, k == KD - 1) for k in range(KD)])
            slot_free[s] = [m]
            m = act.do([m], lambda b=b: S.copy(pc[:, 6, 1:TOK + 1], psum[:, b, 0:256]))
            bank_free[b] = [m]
            pm.append(m)
            m = V_(pm + [zc], lambda: V.tensor_tensor(xs, pc[:, :, 0:TOK], pc[:, :, 1:TOK + 1], SUB))
            xm = V_([m], *[lambda k=k: V.scalar_tensor_tensor(xs[:, k, :], xs[:, k, :], vec("rwkv_mu_2", k), pc[:, k, 1:TOK + 1], MUL, ADD)
                           for k in (6, 2, 3, 0, 1, 4, 5)])
            rT, kT0, vT, lo = xs[:, 0:2, :], xs[:, 2:4, :], xs[:, 4:6, :], xs[:, 6, :]
            m1 = act.do([xm], lambda: S.activation(lo[64:128, :], lo[64:128, :], ACT.Sigmoid))
            m = act.do([xm], lambda: S.activation(lo[0:32, :], lo[0:32, :], ACT.Tanh))
            lw, aT, gT = carve(2, TOK), carve(2, TOK), carve(2, TOK)
            banks3 = []
            for p0, p1 in ((0, 32), (32, 64), (64, 128)):
                b, free = take(WORK8)
                ml = pe.do([m, m1, small2] + free, *[mm(psum[:, b, 256 * j:256 * j + 256], lora[p0:p1, P * j:P * j + P], lo[p0:p1, :]) for j in range(2)])
                banks3.append((b, ml))
            (b, ml) = banks3[0]
            m = act.do([ml], *[lambda j=j, b=b: S.activation(lw[:, j, :], psum[:, b, 256 * j:256 * j + 256], ACT.Sigmoid, bias=vec("rwkv_w0_2", j)) for j in range(2)])
            bank_free[b] = [m]
            lwm = V_([m], lambda: V.tensor_scalar(lw, lw, -float(np.exp(-0.5)), None, MUL))
            (b, ml) = banks3[1]
            am = act.do([ml], *[lambda j=j, b=b: S.activation(aT[:, j, :], psum[:, b, 256 * j:256 * j + 256], ACT.Sigmoid, bias=vec("rwkv_a0_2", j)) for j in range(2)])
            bank_free[b] = [am]
            (b, ml) = banks3[2]
            gm = act.do([ml], lambda b=b: S.copy(gT, psum[:, b, :].rearrange("p (j t) -> p j t", j=2)))
            bank_free[b] = [gm]
            kk, k2, t1 = carve(2, TOK), carve(2, TOK), carve(2, TOK)
            flat = lambda v: v.rearrange("p j t -> p (j t)")
            m = V_([xm], *[lambda j=j: V.tensor_scalar(kk[:, j, :], kT0[:, j, :], vec("rwkv_k_k_2", j), None, MUL) for j in range(2)])
            m2 = V_([m], lambda: V.tensor_tensor(t1, kk, kk, MUL))
            b, pv, m2 = half_sums(flat(t1), [m2])
            m2 = act.do([m2], lambda pv=pv: S.activation(t1, pv, ACT.Sqrt))
            bank_free[b] = [m2]
            m2 = V_([m2], lambda: V.tensor_scalar(t1, t1, 1e-12, None, MAX))
            m2 = V_([m2], lambda: V.reciprocal(t1, t1))
            kkm = V_([m2], lambda: V.tensor_tensor(kk, kk, t1, MUL))
            m = V_([am], *[lambda j=j: V.tensor_scalar(k2[:, j, :], aT[:, j, :], 1.0, vec("rwkv_k_a_2", j), SUB, MUL) for j in range(2)])
            k2m = V_([m], lambda: V.scalar_tensor_tensor(k2, k2, 1.0, kT0, ADD, MUL))
            cum, ecum, eneg, eprev = carve(2, TOK), carve(2, TOK), carve(2, TOK), carve(2, TOK)
            cm = V_([lwm], *[lambda j=j: V.tensor_tensor_scan(cum[:, j, :], C("resets"), lw[:, j, :], 0.0, MUL, ADD) for j in range(2)])
            m = V_([cm], lambda: V.tensor_tensor(eprev, cum, lw, SUB))
            e1 = act.do([cm], lambda: S.activation(ecum, cum, ACT.Exp))
            e2 = act.do([cm], lambda: S.activation(eneg, cum, ACT.Exp, scale=-1.0))
            e3 = act.do([m], lambda: S.activation(eprev, eprev, ACT.Exp))
            alpha, betaT, khat, rhat = eprev, carve(2, TOK), carve(2, TOK), carve(2, TOK)
            alm = pool.do([e3, kkm], lambda: G.tensor_tensor(alpha, eprev, kk, MUL))
            m = pool.do([kkm, am, e2], lambda: G.tensor_tensor(betaT, kk, aT, MUL))
            btm = pool.do([m], lambda: G.tensor_tensor(betaT, betaT, eneg, MUL))
            khm = pool.do([k2m, e2], lambda: G.tensor_tensor(khat, k2, eneg, MUL))
            rhm = pool.do([e1, xm], lambda: G.tensor_tensor(rhat, rT, ecum, MUL))
            natb, natk, natv = carve(4, 256), carve(4, 256), carve(4, 256)
            natm = []
            for src, dst, dep, sign in ((betaT, natb, btm, -1.0), (khat, natk, khm, 1.0), (vT, natv, xm, 1.0)):
                for half in range(2):
                    b, free = take(WORK8)
                    m = pe.do([dep] + free, *[tr(psum[0:64, b, 256 * c + P * j:256 * c + P * j + P],
                                                 src[:, j, 128 * half + 64 * c:128 * half + 64 * c + 64]) for c in range(2) for j in range(2)])
                    m = act.do([m], lambda dst=dst, half=half, b=b, sign=sign: S.mul(
                        dst[0:64, 2 * half:2 * half + 2, :], psum[0:64, b, :].rearrange("p (c n) -> p c n", c=2), sign))
                    bank_free[b] = [m]
                    natm.append(m)
            Lr, Xr, XTr, Ak = (shaped(spare[k // 2][:, 1024 * (k % 2):1024 * (k % 2) + 1024], 2, 8) for k in range(4))
            Rb, Rk = carve(2, 8, 64), carve(2, 8, 64)
            pair_m = {n: [] for n in "LABK"}
            for s2 in range(2):
                for key, left, right, dst, mask in (("L", alpha, betaT, Lr, None), ("A", khat, alpha, Ak, "before"),
                                                    ("B", betaT, rhat, Rb, "upto"), ("K", khat, rhat, Rk, "upto")):
                    for e in range(2):
                        b, free = take(WORK8)
                        bv = psum[0:64, b, 0:256].rearrange("p (n s) -> p n s", n=4)
                        rows64 = slice(64 * e, 64 * e + 64)
                        at = lambda n: slice(64 * (2 * s2 + n // 2), 64 * (2 * s2 + n // 2) + 64)
                        m = pe.do([alm, btm, khm, rhm] + free, *[mm(bv[:, n, :], left[rows64, n % 2, at(n)], right[rows64, n % 2, at(n)])
                                                                for n in range(4)])
                        o = dst[0:64, s2].rearrange("p (n e) s -> p e n s", e=2)[:, e]
                        if mask is None:
                            m = act.do([m], lambda o=o, bv=bv: S.copy(o, bv))
                        else:
                            m = V_([m], lambda o=o, bv=bv, mask=mask: V.tensor_tensor(
                                o, bv, C(mask)[0:64, 0:64].unsqueeze(1).to_broadcast([64, 4, 64]), MUL))
                        bank_free[b] = [m]
                        if key == "B":
                            m = pool.do([m], lambda o=o: G.tensor_scalar(o, o, -1.0, None, MUL))
                        pair_m[key].append(m)

            qa, ka, va = carve(2, TOK), carve(2, TOK), carve(NT, 256)
            prob = shaped(pc.rearrange("p a b -> p (a b)")[:, 0:1536], 4, 3)
            PTa = carve(4, 3, P)
            ya = carve(NT, 256)
            top, total = carve(4, 2), carve(4, 2)
            marks = {}

            def attention_in():
                b, pv, m = colT(A0)
                marks["q"] = act.do([m], lambda pv=pv: S.mul(qa, pv, 64 ** -0.5))
                bank_free[b] = [marks["q"]]
                marks["k"] = kept(colT(A0 + 256), ka)
                marks["v"] = kept(colN(A0 + 512), va)

            def attention_head(h):
                hb, j = 64 * (h % 2), h // 2
                b, free = take(WORK8)
                ops = [mm(psum[:, b, 0:128], qa[hb:hb + 64, j, 0:128], ka[hb:hb + 64, j, 0:128], True, False),
                       mm(psum[:, b, 0:128], C("flip"), reach[:, h, 128:256], False, True),
                       mm(psum[:, b, 128:384], qa[hb:hb + 64, j, 128:256], ka[hb:hb + 64, j, :], True, False),
                       mm(psum[:, b, 128:384], C("flip"), reach[:, h, 0:256], False, True)]
                m = pe.do([marks["q"], marks["k"], small2] + free, *ops)
                m = V_([m], lambda b=b: V.tensor_tensor(psum[:, b, 64:128], psum[:, b, 64:128], C("barred"), ADD),
                       lambda b=b: V.tensor_tensor(psum[:, b, 320:384], psum[:, b, 320:384], C("barred"), ADD))
                m = V_([m], lambda b=b: V.tensor_reduce(top[:, h, 0:1], psum[:, b, 0:128], AXX, MAX),
                       lambda b=b: V.tensor_reduce(top[:, h, 1:2], psum[:, b, 128:384], AXX, MAX))
                m = V_([m], lambda: V.tensor_scalar(top[:, h], top[:, h], -1.0, None, MUL))
                for t, (lo_, hi_) in enumerate(((0, 128), (128, 384))):
                    m = act.do([m, xm], lambda b=b, t=t, lo_=lo_, hi_=hi_: S.activation(
                        prob[:, h].rearrange("p a b -> p (a b)")[:, lo_:hi_], psum[:, b, lo_:hi_], ACT.Exp,
                        bias=top[:, h, t:t + 1], accum_out=total[:, h, t:t + 1]))
                bank_free[b] = [m]
                mr = V_([m], lambda: V.reciprocal(total[:, h], total[:, h]))
                b, free = take(WORK8)
                m = pe.do([m] + free, *[tr(psum[:, b, P * k:P * k + P], prob[:, h, k, :]) for k in range(3)])
                m = act.do([m], lambda b=b: S.copy(PTa[:, h], psum[:, b, 0:384].rearrange("p (a b) -> p a b", a=3)))
                bank_free[b] = [m]
                b, free = take(WORK8)
                m = pe.do([m, marks["v"]] + free, mm(psum[:, b, 0:64], PTa[:, h, 0, :], va[:, 0, 64 * h:64 * h + 64]),
                          *[mm(psum[:, b, 64:128], PTa[:, h, 1 + k, :], va[:, k, 64 * h:64 * h + 64], k == 0, k == 1) for k in range(2)])
                m = V_([m, mr], *[lambda b=b, t=t: V.tensor_scalar(ya[:, t, 64 * h:64 * h + 64], psum[:, b, 64 * t:64 * t + 64],
                                                                  total[:, h, t:t + 1], None, MUL) for t in range(2)])
                bank_free[b] = [m]
                marks[("ya", h)] = m

            xd, conv = carve(2, TOK + 3), kT0
            gr, gi, yd = (shaped(v, 2) for v in (C("ahead"), C("behind"), C("bwd")[:, 0:512]))
            sp_l = carve(2)
            lt = carve(3, 2)

            def lru():
                z0 = pool.do([], lambda: G.memset(xd[:, :, 0:3], 0.0))
                m = kept(colT(U0), xd[:, :, 3:TOK + 3])
                mg = kept(colT(U0 + 256), yd, ACT.Gelu_apprx_tanh)
                for j in range(2):
                    mc = V_([m, z0, k2m], lambda j=j: V.tensor_scalar(conv[:, j, :], xd[:, j, 0:TOK], vec("lru_conv_w_2", j),
                                                                 vec("lru_conv_b_2", j), MUL, ADD))
                    for n in range(1, 4):
                        mc = V_([mc], lambda j=j, n=n: V.scalar_tensor_tensor(conv[:, j, :], xd[:, j, n:n + TOK],
                                                                              vec("lru_conv_w_2", 2 * n + j), conv[:, j, :], MUL, ADD))
                for k, dst, name in ((0, gr, "lru_ba_2"), (1, gi, "lru_bx_2")):
                    b, free = take(WORK8)
                    m = pe.do([mc, small2] + free, *[mm(psum[:, b, 256 * j:256 * j + 256], gate_w[:, k, j, :], conv[:, j, :]) for j in range(2)])
                    m = act.do([m], *[lambda j=j, b=b, dst=dst, name=name: S.activation(
                        dst[:, j, :], psum[:, b, 256 * j:256 * j + 256], ACT.Sigmoid, bias=vec(name, j)) for j in range(2)])
                    bank_free[b] = [m]
                lam = vecs[:, vec_at["lru_lambda_2"]:vec_at["lru_lambda_2"] + 2]
                e_, z_, q_ = lt[:, 0], lt[:, 1], lt[:, 2]
                ml = act.do([], lambda: S.activation(e_, lam, ACT.Abs))
                ml = act.do([ml], lambda: S.activation(e_, e_, ACT.Exp, scale=-1.0))
                ml = V_([ml], lambda: V.tensor_scalar(z_, e_, 2.0, None, ADD))
                ml = V_([ml], lambda: V.reciprocal(z_, z_))
                ml = V_([ml], lambda: V.tensor_tensor(z_, z_, e_, MUL))
                ml = V_([ml], lambda: V.tensor_tensor(q_, z_, z_, MUL))
                ml = V_([ml], lambda: V.tensor_scalar(e_, q_, 1.0 / 17, 1.0 / 15, MUL, ADD))
                for n in (13, 11, 9, 7, 5, 3, 1):
                    ml = V_([ml], lambda: V.tensor_tensor(e_, e_, q_, MUL))
                    ml = V_([ml], lambda n=n: V.tensor_scalar(e_, e_, 1.0 / n, None, ADD))
                ml = V_([ml], lambda: V.tensor_tensor(z_, z_, e_, MUL))
                ml = V_([ml], lambda: V.tensor_scalar(q_, lam, -1.0, 0.0, MUL, MAX))
                ml = V_([ml], lambda: V.scalar_tensor_tensor(sp_l, z_, 2.0, q_, MUL, ADD))
                mu_ = V_([ml, m], *[lambda j=j: V.tensor_scalar(gr[:, j, :], gr[:, j, :], sp_l[:, j:j + 1], 8.0, MUL, MUL) for j in range(2)])
                mi = pool.do([m, mc], lambda: G.tensor_tensor(gi, gi, conv, MUL))
                th, aa = conv, xd[:, :, 0:TOK]
                m1 = act.do([mu_, mi], lambda: S.activation(th, gr, ACT.Tanh))
                m2 = act.do([mu_, mc], lambda: S.activation(aa, gr, ACT.Exp, scale=-1.0))
                m3 = pool.do([m2], lambda: G.tensor_tensor(gr, aa, aa, MUL))
                m3 = V_([m3, m1], lambda: V.scalar_tensor_tensor(th, gr, 1.0, th, ADD, MUL))
                m3 = act.do([m3], lambda: S.activation(th, th, ACT.Sqrt))
                m3 = pool.do([m3], lambda: G.tensor_tensor(gi, gi, th, MUL))
                m3 = V_([m3, m2], *[lambda j=j: V.tensor_tensor_scan(gr[:, j, :], aa[:, j, :], gi[:, j, :], 0.0, MUL, ADD) for j in range(2)])
                marks["yd"] = V_([m3, mg], lambda: V.tensor_tensor(yd, yd, gr, MUL))

            qb, fb, ib, kb = carve(2, TOK), carve(2, TOK), carve(2, TOK), carve(2, TOK)
            gbn, yb = carve(NT, 256), eneg
            lb = carve(4, 2)

            def hgrn_in():
                lgt = vecs[:, vec_at["hgrn_lb_logits_2"]:vec_at["hgrn_lb_logits_2"] + 2]
                m = V_([], lambda: V.tensor_tensor(lb[:, 0], lgt, lgt, SUB))
                m = act.do([m], lambda: S.activation(lb[:, 0], lb[:, 0], ACT.Exp))
                m = V_([m], lambda: V.reciprocal(lb[:, 1], lb[:, 0]))
                m = V_([m], lambda: V.tensor_tensor(lb[:, 0], lb[:, 0], lb[:, 1], MUL))
                m = V_([m], lambda: V.tensor_tensor(lb[:, 2], lb[:, 0], lb[:, 0], SUB))
                m = V_([m], lambda: V.tensor_scalar(lb[:, 2], lb[:, 2], 0.0, None, MAX))
                ml = V_([m], lambda: V.tensor_scalar(lb[:, 3], lb[:, 2], -1.0, 1.0, MUL, ADD))
                marks["hq"] = kept(colT(H0), qb, ACT.Silu)
                b, pv, m = colT(H0 + 256)
                m1 = act.do([m], lambda pv=pv: S.activation(fb, pv, ACT.Sigmoid))
                m2 = act.do([m1], lambda pv=pv: S.activation(kb, pv, ACT.Sigmoid, scale=-1.0))
                bank_free[b] = [m2]
                marks["hf"] = V_([m2, ml], *[lambda j=j: V.tensor_scalar(fb[:, j, :], fb[:, j, :], lb[:, 3, j:j + 1], lb[:, 2, j:j + 1], MUL, ADD) for j in range(2)],
                                 *[lambda j=j: V.tensor_scalar(kb[:, j, :], kb[:, j, :], lb[:, 3, j:j + 1], None, MUL) for j in range(2)])
                marks["hi"] = kept(colT(H0 + 512), ib)
                marks["hg"] = kept(colN(H0 + 768), gbn, ACT.Silu)

            attention_in()
            hgrn_in()
            jobs = [lru] + [lambda h=h: attention_head(h) for h in range(4)]

            def fill(n):
                if jobs:
                    jobs.pop(0)()

            LMr, Wr = (shaped(scaled[:, k, :], 2, 8) for k in range(2))
            xts = inverses([(Lr[0:64, s_], Xr[0:64, s_], XTr[0:64, s_], pair_m["L"][2 * s_:2 * s_ + 2]) for s_ in range(2)],
                           64, 8, ["fwd", "fwd"], LEVELS[:6], fill, LMr, Wr, [])
            while jobs:
                jobs.pop(0)()

            ST = cosT[:, :].rearrange("p (j n) -> p j n", j=2)
            rhs, sa, yn, av = (v.rearrange("p s n t -> p (s n t)").rearrange("p (c n) -> p c n", c=4) for v in (Lr, Xr, LMr, Wr))
            inverted = xts[0] + xts[1]
            stm = pool.do([], lambda: G.memset(ST, 0.0))

            avm = []
            for c in range(4):
                b, free = take((0, 1))
                m = pe.do(pair_m["A"] + natm + free, *[mm(psum[0:64, b, 64 * h:64 * h + 64], Ak[0:64, c // 2, 4 * (c % 2) + h, :], natv[0:64, c, 64 * h:64 * h + 64]) for h in range(4)])
                m = act.do([m] + inverted, lambda c=c, b=b: S.copy(av[0:64, c, :], psum[0:64, b, 0:256]))
                bank_free[b] = [m]
                avm.append(m)

            rw_m = {"st": stm, "y": []}

            def rwkv_chunk(c):
                s_, n0 = c // 2, 4 * (c % 2)
                b, free = take((0, 1))
                m = pe.do([rw_m["st"], alm] + free, *[mm(psum[0:64, b, P * j:P * j + P], alpha[:, j, 64 * c:64 * c + 64], ST[:, j, :]) for j in range(2)])
                yield
                m = V_([m, avm[c]], lambda c=c, b=b: V.tensor_tensor(rhs[0:64, c, :], psum[0:64, b, 0:256], av[0:64, c, :], ADD))
                bank_free[b] = [m]
                b, free = take((0, 1))
                yield
                m = pe.do([m] + xts[s_] + free, *[mm(psum[0:64, b, 64 * h:64 * h + 64], XTr[0:64, s_, n0 + h, :], rhs[0:64, c, 64 * h:64 * h + 64]) for h in range(4)])
                ms = V_([m], lambda c=c, b=b: V.tensor_copy(sa[0:64, c, :], psum[0:64, b, 0:256]))
                bank_free[b] = [ms]
                yield
                if c < 3:
                    b, free = take((2, 3))
                    m = pe.do([ms] + natm + free, *[op for j in range(2) for op in (
                        mm(psum[:, b, P * j:P * j + P], natb[0:64, c, P * j:P * j + P], sa[0:64, c, P * j:P * j + P], True, False),
                        mm(psum[:, b, P * j:P * j + P], natk[0:64, c, P * j:P * j + P], natv[0:64, c, P * j:P * j + P], False, True))])
                b2, free2 = take((2, 3))
                ops = []
                for j in range(2):
                    ops.append(mm(psum[0:64, b2, P * j:P * j + P], rhat[:, j, 64 * c:64 * c + 64], ST[:, j, :], True, False))
                    for h in (2 * j, 2 * j + 1):
                        ops.append(mm(psum[0:64, b2, 64 * h:64 * h + 64], Rb[0:64, s_, n0 + h, :], sa[0:64, c, 64 * h:64 * h + 64], False, False))
                        ops.append(mm(psum[0:64, b2, 64 * h:64 * h + 64], Rk[0:64, s_, n0 + h, :], natv[0:64, c, 64 * h:64 * h + 64], False, h == 2 * j + 1))
                my = pe.do([ms, rw_m["st"]] + pair_m["B"] + pair_m["K"] + free2, *ops)
                mq = act.do([my], lambda c=c, b2=b2: S.copy(yn[0:64, c, :], psum[0:64, b2, 0:256]))
                bank_free[b2] = [mq]
                rw_m["y"].append(mq)
                yield
                if c < 3:
                    m = V_([m, my], lambda b=b: V.tensor_tensor(ST, psum[:, b, 0:256].rearrange("p (j n) -> p j n", j=2), ST, ADD))
                    bank_free[b] = [m]
                    rw_m["st"] = V_([m], *[lambda j=j, c=c: V.scalar_tensor_tensor(ST[:, j, :], ST[:, j, :], ecum[:, j, 64 * c + 63:64 * c + 64],
                                                                                  C("half"), MUL, MUL) for j in range(2)])
                yield

            scratch = [reach.rearrange("p a b -> p (a b)"), PTa.rearrange("p a b c -> p (a b c)")]
            NB, NZ, LAG = 3, 6, 2
            add_b, st_b = (scratch[0][:, 768 * k:768 * k + 768].rearrange("p (n t) -> p n t", n=NB) for k in range(2))
            z_b = scratch[1].rearrange("p (n t) -> p n t", n=NZ)
            attended = [marks[("ya", h)] for h in range(4)]
            z_read = [attended for _ in range(NZ)]
            s_read = [attended for _ in range(NB)]
            a_read = [attended for _ in range(NB)]
            yb_bank = 7
            picks = [sinT[:, 0:128], sinT[:, 128:256]]
            pick_read = [[], []]
            yv = psum[:, yb_bank, :].rearrange("p (t j v h) -> p t j v h", t=2, j=2, h=2)
            yb_free = list(bank_free[yb_bank])
            chunk_steps = (None for c in range(4) for _ in rwkv_chunk(c))
            zm_ = {}
            for v in range(64 + LAG):
                if v < 64:
                    b, free = take((4, 5, 6))
                    pick = picks[v % 2]
                    mp = act.do(pick_read[v % 2], lambda v=v, pick=pick: S.copy(
                        pick.rearrange("p (h k) -> p h k", h=2), ident.rearrange("p (h v) -> p h v", h=2)[:, :, v:v + 1].to_broadcast([P, 2, 64])))
                    mi = pe.do([mp, marks["hi"]] + free, *[mm(psum[:, b, 256 * j:256 * j + 256], pick, ib[:, j, :]) for j in range(2)])
                    pick_read[v % 2] = [mi]
                    for j in range(2):
                        n = 2 * v + j
                        k, kz = n % NB, n % NZ
                        ma = V_([mi, marks["hf"]] + a_read[k], lambda j=j, k=k, b=b: V.tensor_tensor(add_b[:, k, :], kb[:, j, :], psum[:, b, 256 * j:256 * j + 256], MUL))
                        ms = V_([ma] + s_read[k], lambda j=j, k=k: V.tensor_tensor_scan(st_b[:, k, :], fb[:, j, :], add_b[:, k, :], 0.0, MUL, ADD))
                        a_read[k] = [ms]
                        mz = pool.do([ms, marks["hq"]] + z_read[kz], lambda j=j, k=k, kz=kz: G.tensor_tensor(z_b[:, kz, :], st_b[:, k, :], qb[:, j, :], MUL))
                        s_read[k] = [mz]
                        zm_[n] = mz
                    bank_free[b] = [ma]
                if v >= LAG:
                    for j in range(2):
                        n = 2 * (v - LAG) + j
                        my = pe.do([zm_[n]] + yb_free, *[mm(yv[:, t, j, v - LAG, :], z_b[:, n % NZ, P * t:P * t + P], C("headcol")) for t in range(2)])
                        z_read[n % NZ] = [my]
                if v % 2:
                    next(chunk_steps, None)
            for _ in chunk_steps:
                pass
            ybh = yb.rearrange("p t (h v) -> p t h v", h=4)
            sq4, r8 = lw.rearrange("p t (h v) -> p t h v", h=4), carve(NT, 4)
            src = psum[:, yb_bank, :].rearrange("p (t j v h) -> p t j h v", t=2, j=2, h=2)
            m = act.do([my], *[lambda t=t, j=j: S.copy(ybh[:, t, 2 * j:2 * j + 2, :], src[:, t, j]) for t in range(2) for j in range(2)])
            bank_free[yb_bank] = [m]
            m2 = act.do([m], lambda: S.activation(sq4, ybh, ACT.Square))
            m2 = V_([m2], lambda: V.tensor_reduce(r8, sq4, AXX, ADD))
            m2 = inverse_root(r8.rearrange("p t h -> p (t h)"), r8.rearrange("p t h -> p (t h)"), [m2], 1.0 / 64)
            m = V_([m2], lambda: V.tensor_tensor(ybh, ybh, r8.unsqueeze(3).to_broadcast([P, NT, 4, 64]), MUL))
            m = V_([m], lambda: V.tensor_tensor(yb, yb, hgn[:, :].unsqueeze(1).to_broadcast([P, NT, 256]), MUL))
            ybm = V_([m, marks["hg"]], lambda: V.tensor_tensor(yb, yb, gbn, MUL))

            yT = cum
            b, free = take((4, 5, 6))
            m = pe.do(rw_m["y"] + free, *[tr(psum[:, b, 256 * j + 64 * c:256 * j + 64 * c + 64], yn[0:64, c, P * j:P * j + P]) for j in range(2) for c in range(4)])
            m = act.do([m, e1, e2], lambda b=b: S.copy(yT, psum[:, b, :].rearrange("p (j t) -> p j t", j=2)))
            bank_free[b] = [m]
            b, pv, ms = half_sums(flat(yT), [m])
            m = V_([ms, m], lambda pv=pv: V.scalar_tensor_tensor(yT, pv, -1.0 / 64, yT, MUL, ADD))
            bank_free[b] = [m]
            ms = act.do([m], lambda: S.activation(t1, yT, ACT.Square))
            b, pv, ms = half_sums(flat(t1), [ms])
            ms = V_([ms], lambda pv=pv: V.tensor_scalar(t1, pv, 1.0 / 64, 64 * 1e-5, MUL, ADD))
            bank_free[b] = [ms]
            ms = act.do([ms], lambda: S.activation(t1, t1, ACT.Sqrt))
            ms = V_([ms], lambda: V.reciprocal(t1, t1))
            m = V_([m, ms], lambda: V.tensor_tensor(yT, yT, t1, MUL))
            m = V_([m], *[lambda j=j: V.tensor_scalar(yT[:, j, :], yT[:, j, :], vec("rwkv_ln_w_2", j), vec("rwkv_ln_b_2", j), MUL, ADD) for j in range(2)])
            ms = V_([m], *[lambda j=j: V.scalar_tensor_tensor(t1[:, j, :], rT[:, j, :], vec("rwkv_r_k_2", j), k2[:, j, :], MUL, MUL) for j in range(2)])
            b, pv, ms = half_sums(flat(t1), [ms])
            ms = V_([ms], lambda pv=pv: V.tensor_tensor(t1, pv, vT, MUL))
            bank_free[b] = [ms]
            m = V_([ms], lambda: V.tensor_tensor(yT, yT, t1, ADD))
            m = V_([m, gm], lambda: V.tensor_tensor(mixT[:, 4:6, :], yT, gT, MUL))
            m1 = V_([marks["yd"]], lambda: V.tensor_copy(mixT[:, 6:8, :], yd))
            mixed = [m, m1]
            mixed += to_T(ya, mixT, [marks[("ya", h)] for h in range(4)], (0, 1))
            mixed += to_T(yb, mixT, [ybm], (2, 3))
            dump("mix3", mixT[:, :, :], mixed)
            for i in range(4):
                done = project_out(a["w_out_2"][0], 2 * i, 2, mixT, KD, mixed)
            residual([done], post_w[:, 0, :], wmark, scaled, 1.0)

        def relu2_mlp():
            stage_start()
            wmark = load_post(a["norm_mlp_post_2"][0], 0)
            scaled = carve(NT, D)
            n_groups = MLP // 256
            sources = []
            for i in range(n_groups + 1):
                if i < n_groups:
                    sources.append(columns(a["mlp_w1_2"][0], 256 * i))
                if i:
                    sources.append(rows(a["mlp_w2_2"][0], 2 * (i - 1)))
            stream = SplitStream(sources)
            stream.ahead(2)
            ready = split_xn(norm_T(x, xnT, 88, scaled, []))
            stream.ahead(3)
            h32 = carve(2, 2, TOK)
            h_ready, h_read = [None] * n_groups, [[] for _ in range(NH)]
            for i in range(n_groups + 1):
                if i < n_groups:
                    b, pv, m = split_project_T(stream, ready)
                    hv, g = h32[:, i % 2], i % NH
                    m = act.do([m] + (h_ready[i - 2:i - 1] if i > 1 else []), lambda hv=hv, pv=pv: S.activation(hv, pv, ACT.Relu))
                    bank_free[b] = [m]
                    m = V_([m], lambda hv=hv: V.tensor_tensor(hv, hv, hv, MUL))
                    h_ready[i] = split(hv, h_hl[:, g, 0], h_hl[:, g, 1], [m] + h_read[g])
                    stream.ahead(3)
                if i:
                    g = (i - 1) % NH
                    done = split_out(stream, lambda h, j, g=g: h_hl[:, g, h, j, :], i == 1, i == n_groups, [h_ready[i - 1]])
                    h_read[g] = [done]
                    stream.ahead(3)
            residual([done], post_w[:, 0, :], wmark, scaled, 1.0)

        mixer2()
        dump("x20", x[:, :, :], [])
        relu2_mlp()

        stage_start()
        out_sem = sem("out_written")
        wm = sp.dma([], out_sem, 16, out[0].rearrange("(t p) d -> p t d", p=P), x[:, :, :])
        sp.wait([wm] + [(s, n) for s, n in load_sems.values()])

        with nc.Block() as block:
            @block.sync
            def _(e):
                sp.play(e)

            @block.tensor
            def _(e):
                pe.play(e)

            @block.vector
            def _(e):
                dve.play(e)

            @block.scalar
            def _(e):
                act.play(e)

            @block.gpsimd
            def _(e):
                pool.play(e)


def kernel(**inputs):
    import concourse.bacc as bacc
    from concourse.bass_utils import run_bass_kernel_spmd

    nc = bacc.Bacc("TRN2", target_bir_lowering=False, num_devices=1)
    arrays = {f"in_{k}": np.ascontiguousarray(v) for k, v in inputs.items()}
    arrays["in_consts"] = shape_constants()[0]
    a = {k[3:]: nc.dram_tensor(k, v.shape, mybir.dt.from_np(v.dtype), kind="ExternalInput").ap()
         for k, v in arrays.items()}
    out = nc.dram_tensor("out_x", (1, TOK, D), F32, kind="ExternalOutput").ap()
    build(nc, a, out)
    return run_bass_kernel_spmd(nc, [arrays], core_ids=[0]).results[0]["out_x"]
```

```python
from contextlib import ExitStack

import numpy as np

import concourse.bass as bass
from concourse import mybir

F32 = mybir.dt.float32
F32R = mybir.dt.float32r
I32 = mybir.dt.int32
ALU = mybir.AluOpType
ACT = mybir.ActivationFunctionType
AXX = mybir.AxisListType.X
MUL, ADD, SUB, MAX, MIN = ALU.mult, ALU.add, ALU.subtract, ALU.max, ALU.min

P = 128
TOK = 256
NT = TOK // P
D = 1024
KD = D // P
DEPTH = 2
D_FF = 2816
HEADS = 4
HD = 128
MLP = 4096
EPS = 1e-6
SLAB = 2048
NSLOT = 5
LEVELS = (1, 2, 4, 8, 16, 32, 64)


class Queue:

    def __init__(self, sem):
        self.sem, self.count, self.steps, self.seen = sem, 0, [], {}

    def wait(self, marks):
        for sem, value in marks:
            if self.seen.get(sem.name, 0) < value:
                self.seen[sem.name] = value
                self.steps.append(lambda e, s=sem, v=value: e.wait_ge(s, v))

    def do(self, after, *instructions):
        self.wait(after)
        self.steps += [lambda e, f=f: f() for f in instructions[:-1]]
        self.steps.append(lambda e, f=instructions[-1]: f().then_inc(self.sem, 1))
        self.count += 1
        return (self.sem, self.count)

    def last(self):
        return [(self.sem, self.count)] if self.count else []

    def dma(self, after, sem, total, dst, src):
        self.wait(after)
        self.steps.append(lambda e: e.dma_start(dst, src).then_inc(sem, 16))
        return (sem, total)

    def play(self, engine):
        for s in self.steps:
            s(engine)


def shape_constants():
    i = np.arange(P)[:, None]
    j = np.arange(P)[None, :]
    f = lambda a: np.asarray(a, np.float32)
    parts = {"ident": f(i == j), "upto": f(i <= j), "from": f(i >= j), "before": f(i < j)}
    parts["ones"] = np.ones((P, P), np.float32)
    for name in ("fwd", "bwd"):
        masks = []
        for b in LEVELS:
            m = (i // (2 * b) == j // (2 * b)) & (i % (2 * b) >= b) & (j % (2 * b) < b)
            masks.append(f(m if name == "fwd" else m.T))
        parts[name] = np.concatenate(masks, 1)
    n = np.arange(TOK)[None, None, :]
    m = np.arange(NT)[None, :, None] * P + np.arange(P)[:, None, None]
    parts["ahead"] = f(np.maximum(n - m, 0)).reshape(P, -1)
    parts["behind"] = f(np.maximum(m - n, 0)).reshape(P, -1)
    parts["rotate"] = f(i == j - 64) - f(i == j + 64)
    parts["flip"] = f(i + j == P - 1)
    parts["half"] = f(i // 64 == j // 64)
    parts["resets"] = np.broadcast_to(f(np.arange(TOK) % 64 != 0), (P, TOK))
    parts["headcol"] = f(i // 64 == np.arange(2)[None, :])
    inv = np.float32(10000.0) ** (-np.arange(0, HD, 2, dtype=np.float32) / np.float32(HD))
    parts["freq"] = f(np.concatenate([inv, inv])[:, None])
    barred = np.zeros((P, 64), np.float32)
    barred[:64] = -1e30
    parts["barred"] = barred
    at, where = 0, {}
    for k, v in parts.items():
        where[k] = (at, at + v.shape[1])
        at += v.shape[1]
    return np.ascontiguousarray(np.concatenate(list(parts.values()), 1)), where


def build(nc, a, out, dbg=None):
    _, const_at = shape_constants()
    with ExitStack() as ctx:
        def sb(name, shape, dt=F32):
            return ctx.enter_context(nc.sbuf_tensor(name, shape, dt))

        def sem(name):
            return ctx.enter_context(nc.semaphore(name))

        pe, dve, act, pool, sp = (Queue(sem(f"{n}_steps")) for n in ("pe", "dve", "act", "pool", "sp"))
        V, S, G, T = nc.vector, nc.scalar, nc.gpsimd, nc.tensor

        psum = ctx.enter_context(nc.psum_tensor("psum", [P, 8, 512], F32))
        ring = sb("weight_ring", [P, NSLOT, SLAB])
        slot_landed = [sem(f"slab_landed{s}") for s in range(NSLOT)]
        slot_loads = [0] * NSLOT
        slot_free = [[] for _ in range(NSLOT)]
        x = sb("x", [P, NT, D])
        xnT = sb("xnT", [P, KD, TOK])
        memkT = sb("memkT", [P, KD, TOK])
        memv = sb("memv", [P, NT, D])
        mixT = xnT
        consts = sb("consts", [P, max(e for _, e in const_at.values())])
        gains = sb("gains", [P, 96])
        taps = sb("taps", [P, 120])
        vecs = sb("vecs", [P, 48])
        post_w = sb("post_w", [P, 1, D])
        cosT = sb("cosT", [P, TOK])
        sinT = sb("sinT", [P, TOK])
        ssq = sb("ssq", [P, 4])
        inv_rms = sb("inv_rms", [P, 4])
        softmax_s = sb("softmax_s", [P, 16])
        minus_half = sb("minus_half", [P, 16])
        ARENA = 27648
        arena_base = (nc.sbuf_usable_end - 4 * ARENA) // 32 * 32
        arena = nc.alloc_sbuf_tensor_at("arena", [P, ARENA], F32, offset=arena_base)
        NHL = 4
        w_hl = nc.alloc_sbuf_tensor_at("w_hi_lo", [P, NHL, 2, SLAB], F32R, offset=arena_base + 4 * (ARENA - 4096 * NHL))
        x_hl = nc.alloc_sbuf_tensor_at("x_hi_lo", [P, 2, KD, TOK], F32R, offset=arena_base + 4 * (ARENA - 4096 * NHL - 4096))
        NH = 3
        h_hl = nc.alloc_sbuf_tensor_at("h_hi_lo", [P, NH, 2, 2, TOK], F32R, offset=arena_base + 4 * (ARENA - 4096 * NHL - 4096 - 1024 * NH))
        hl_free = [[] for _ in range(NHL)]
        arena_at, keep_tail = [0], [False]
        tail_2k = arena[:, ARENA - 2048:ARENA]
        memT = tail_2k.rearrange("p (k t) -> p k t", k=KD)

        def carve(*shape):
            n = int(np.prod(shape))
            assert arena_at[0] + n <= ARENA, (arena_at, n)
            v = arena[:, arena_at[0]:arena_at[0] + n]
            arena_at[0] += n
            assert arena_at[0] <= ARENA - (2048 if keep_tail[0] else 0), arena_at
            names = "abcd"[:len(shape)]
            if len(shape) == 1:
                return v
            return v.rearrange(f"p ({' '.join(names)}) -> p {' '.join(names)}",
                               **{names[k]: shape[k] for k in range(1, len(shape))})

        def C(name):
            lo, hi = const_at[name]
            return consts[:, lo:hi]

        ident = C("ident")

        x_marks = [[], []]

        def everything():
            return pe.last() + dve.last() + act.last() + pool.last()

        def stage_start(held):
            for q in (pe, dve, act, pool, sp):
                q.wait(held)
            arena_at[0] = 0

        def V_(after, *f):
            return dve.do(after, *f)

        load_sems = {}

        def load(dst, src, after=(), group="setup"):
            if group not in load_sems:
                load_sems[group] = [sem(f"{group}_landed"), 0]
            g = load_sems[group]
            g[1] += 16
            return sp.dma(after, g[0], g[1], dst, src)

        bank_free = [[] for _ in range(8)]
        turn = [0]

        def take(banks=(4, 5, 6, 7)):
            b = banks[turn[0] % len(banks)]
            turn[0] += 1
            return b, bank_free[b]

        slab_no = [0]

        def slab(src, rows, cols):
            s = slab_no[0] % NSLOT
            slab_no[0] += 1
            slot_loads[s] += 16
            view = ring[:, s, 0:rows * cols].rearrange("p (k n) -> p k n", n=cols)
            mark = sp.dma(slot_free[s], slot_landed[s], slot_loads[s], view, src)
            return s, view, mark

        def columns(w, c0, n=256):
            return w[:, c0:c0 + n].rearrange("(k p) n -> p k n", p=P), w.shape[0] // P, n

        def rows(w, r0, n=2):
            return w[r0 * P:(r0 + n) * P, :].rearrange("(k p) n -> p k n", p=P), n, w.shape[1]

        def mm(o, l, r, start=True, stop=True):
            return lambda: T.matmul(o, l, r, start=start, stop=stop)

        def tr(o, i):
            k = i.partition_size()
            b = i.base_partition()
            return lambda: T.transpose(o, i, ident[b:b + k, 0:k])

        def project_T(w, c0, srcT, after, banks=(4, 5, 6, 7)):
            s, wv, landed = slab(*columns(w, c0))
            b, free = take(banks)
            ops = [mm(psum[:, b, 256 * j:256 * j + 256], wv[:, k, P * j:P * j + P], srcT[:, k, :],
                      k == 0, k == KD - 1) for j in range(2) for k in range(KD)]
            m = pe.do([landed] + free + after, *ops)
            slot_free[s] = [m]
            return b, psum[:, b, :].rearrange("p (j t) -> p j t", j=2), m

        def project_N(w, c0, srcT, after, n=256, banks=(4, 5, 6, 7)):
            s, wv, landed = slab(*columns(w, c0, n))
            b, free = take(banks)
            ops = [mm(psum[:, b, n * t:n * t + n], srcT[:, k, P * t:P * t + P], wv[:, k, :],
                      k == 0, k == KD - 1) for t in range(NT) for k in range(KD)]
            m = pe.do([landed] + free + after, *ops)
            slot_free[s] = [m]
            return b, psum[:, b, 0:2 * n].rearrange("p (t n) -> p t n", t=2), m

        def project_out(w, r0, nrows, srcT, total, after):
            s, wv, landed = slab(*rows(w, r0, nrows))
            free = [] if r0 else [m for b in range(4) for m in bank_free[b]]
            done = [pe.do([landed] + free + after,
                          *[mm(psum[:, 2 * t + n, :], srcT[:, r0 + j, P * t:P * t + P], wv[:, j, 512 * n:512 * n + 512],
                               r0 + j == 0, r0 + j == total - 1) for j in range(nrows) for n in range(2)])
                    for t in range(NT)]
            slot_free[s] = done[1:]
            return done

        def split(src, hi, lo, after):
            mh = act.do(after, lambda: S.copy(hi, src))
            return V_([mh], lambda: V.tensor_tensor(lo, src, hi.bitcast(F32), SUB))

        cuts = [0]

        class SplitStream:

            def __init__(self, sources, following=None):
                self.sources, self.cut, self.used, self.following = sources, [], 0, following
                self.loaded = []

            def load(self, n):
                self.loaded = [slab(*source) for source in self.sources[:n]]

            def ahead(self, n):
                while len(self.cut) < min(self.used + n, len(self.sources)):
                    n_cut = len(self.cut)
                    s, view, landed = self.loaded[n_cut] if n_cut < len(self.loaded) else slab(*self.sources[n_cut])
                    k = cuts[0] % NHL
                    cuts[0] += 1
                    m = split(ring[:, s, :], w_hl[:, k, 0, :], w_hl[:, k, 1, :], [landed] + hl_free[k])
                    slot_free[s] = [m]
                    n_cols = self.sources[len(self.cut)][2]
                    self.cut.append((k, [w_hl[:, k, i, :].rearrange("p (k n) -> p k n", n=n_cols) for i in range(2)], m))
                over = self.used + n - len(self.sources)
                if over > 0 and self.following:
                    self.following.ahead(over)

            def next(self):
                self.used += 1
                return self.cut[self.used - 1]

        def three(o, l, r, start, stop):
            return [mm(o, l[0], r[0], start, False), mm(o, l[0], r[1], False, False), mm(o, l[1], r[0], False, stop)]

        def split_project_T(stream, after):
            k_, w, m = stream.next()
            b, free = take()
            ops = [op for j in range(2) for k in range(KD) for op in
                   three(psum[:, b, 256 * j:256 * j + 256], [w[i][:, k, P * j:P * j + P] for i in range(2)],
                         [x_hl[:, i, k, :] for i in range(2)], k == 0, k == KD - 1)]
            m = pe.do([m] + free + after, *ops)
            hl_free[k_] = [m]
            return b, psum[:, b, :].rearrange("p (j t) -> p j t", j=2), m

        def split_out(stream, lhs, first, last, after):
            k_, w, m = stream.next()
            free = [m_ for b in range(4) for m_ in bank_free[b]] if first else []
            done = []
            for t in range(NT):
                ops = [op for j in range(2) for n in range(2) for op in
                       three(psum[:, 2 * t + n, :], [lhs(i, j)[:, P * t:P * t + P] for i in range(2)],
                             [w[i][:, j, 512 * n:512 * n + 512] for i in range(2)], first and j == 0, last and j == 1)]
                done.append(pe.do([m] + free + after, *ops))
            hl_free[k_] = done[1:]
            return done

        staging = carve(P)
        load(x[:, :, :], a["x"][0].rearrange("(t p) d -> p t d", p=P), group="first")
        load(consts[:, 0:P], a["consts"][:, 0:P], group="first")
        flat_rows = lambda v: v.rearrange("a b c -> (a b c)" if len(v.shape) == 3 else "a b -> (a b)").rearrange("(r c) -> r c", c=P)
        r = 0
        for name in ("norm_pre", "mem_norm", "norm_mix_pre_2", "norm_mlp_pre_2"):
            v = flat_rows(a[name])
            first = load(staging[r:r + v.shape[0], :], v, group="first")
            r += v.shape[0]
        half_set = pool.do([], lambda: G.memset(minus_half[:, :], -0.5))
        t0 = pe.do([first], tr(psum[:, 4, 0:96], staging[0:96, :]))
        gains_set = V_([t0], lambda: V.tensor_copy(gains[:, :], psum[:, 4, 0:96]))
        bank_free[4] = [gains_set]
        for q in (pe, act, pool, dve):
            q.wait([first, gains_set, half_set])

        vec_at = {}
        posi = sb("posi", [P, TOK], I32)
        lg, alog, dtb = sb("lg", [P, 16]), sb("alog", [P, 16]), sb("dtb", [P, 16])
        gnw, hgn = sb("gnw", [P, 2 * P]), sb("hgn", [P, 256])
        late_staging = memv[:, 0, 0:256].rearrange("p (a b) -> p a b", a=2)

        def late_loads():
            load(consts[:, P:], a["consts"][:, P:])
            load(late_staging[0:120, 0, :], a["gdn_conv"].rearrange("l j (r c) -> (l j r) c", c=P))
            r = 0
            for name in ("rwkv_mu_2", "rwkv_w0_2", "rwkv_a0_2", "rwkv_k_k_2", "rwkv_k_a_2", "rwkv_r_k_2",
                         "rwkv_ln_w_2", "rwkv_ln_b_2", "lru_conv_w_2", "lru_conv_b_2", "lru_ba_2",
                         "lru_bx_2", "lru_lambda_2", "hgrn_lb_logits_2"):
                v = flat_rows(a[name])
                load(late_staging[r:r + v.shape[0], 1, :], v)
                vec_at[name] = r
                r += v.shape[0]
            vec_at["end"] = r
            load(posi[:, :], a["positions"].partition_broadcast(P))
            for dst, name in ((lg, "ret_log_gamma"), (alog, "gdn_a_log"), (dtb, "gdn_dt_bias")):
                load(dst[:, :], a[name].rearrange("l d h -> (l d h)").partition_broadcast(P))
            load(gnw[:, :], a["gdn_norm"].rearrange("l d -> (l d)").partition_broadcast(P))
            return load(hgn[:, :], a["hgrn_norm_2"].rearrange("l d -> (l d)").partition_broadcast(P))

        def late_setup(landed):
            for q in (pe, dve, act, pool):
                q.wait([landed])
            n = vec_at["end"]
            b, free = take()
            t0 = pe.do(free, tr(psum[:, b, 0:120], late_staging[0:120, 0, :]), tr(psum[:, b, 256:256 + n], late_staging[0:n, 1, :]))
            m = V_([t0], lambda: V.tensor_copy(taps[:, :], psum[:, b, 0:120]),
                   lambda: V.tensor_copy(vecs[:, 0:n], psum[:, b, 256:256 + n]))
            bank_free[b] = [m]
            rotary_tables()
            held.extend([m] + act.last())

        def vec(name, k=0):
            c = vec_at[name] + k
            return vecs[:, c:c + 1]

        def inverse_root(dst, src, after, scale, eps=EPS, gain=1.0):
            p, n = dst.shape
            m = V_(after, lambda: V.tensor_scalar(dst, src, scale / gain ** 2, eps / gain ** 2, MUL, ADD))
            return pool.do([m], lambda: G.tensor_tensor(dst, dst, minus_half[0:p, 0:n], ALU.pow))

        def norm_T(src, dstT, gain_at, scaled, after, split_too=False, banks=(4, 5, 6, 7)):
            squared = [act.do(after[t], lambda t=t: S.activation(scaled[:, t, :], src[:, t, :], ACT.Square,
                                                                 accum_out=ssq[:, t:t + 1])) for t in range(NT)]
            roots = [inverse_root(inv_rms[:, t:t + 1], ssq[:, t:t + 1], [squared[t]], 1.0 / D) for t in range(NT)]
            marks = []
            for t in range(NT):
                m = act.do([roots[t]], lambda t=t: S.mul(scaled[:, t, :], src[:, t, :], inv_rms[:, t:t + 1]))
                for g in range(2):
                    b, free = take(banks)
                    mt = pe.do([m] + free, *[tr(psum[:, b, P * j:P * j + P],
                                                scaled[:, t, P * (4 * g + j):P * (4 * g + j + 1)]) for j in range(4)])
                    c = gain_at + 4 * g
                    piece = dstT[:, 4 * g:4 * g + 4, P * t:P * t + P]
                    mv = V_([mt], lambda b=b, piece=piece, c=c: V.tensor_tensor(
                        piece, psum[:, b, :].rearrange("p (j n) -> p j n", j=4),
                        gains[:, c:c + 4].unsqueeze(2).to_broadcast([P, 4, P]), MUL))
                    bank_free[b] = [mv]
                    if split_too:
                        hi, lo = (x_hl[:, i, 4 * g:4 * g + 4, P * t:P * t + P] for i in range(2))
                        mh = act.do([mv], lambda hi=hi, piece=piece: S.copy(hi, piece))
                        mv = pool.do([mh], lambda hi=hi, lo=lo, piece=piece: G.tensor_tensor(lo, piece, hi.bitcast(F32), SUB))
                    marks.append(mv)
            return marks

        def rotary_tables():
            ang, turns, red = (memkT[:, k, :] for k in range(3))
            TWO_PI = (6.28125, 0.0019350051879882812, float(2 * np.pi - 6.28125 - 0.0019350051879882812))
            MAGIC = 12582912.0
            m = V_([], lambda: V.tensor_copy(ang, posi[:, :]))
            m = V_([m], lambda: V.tensor_scalar(ang, ang, C("freq"), None, MUL))
            for table, shift in ((sinT, 0.0), (cosT, 0.25)):
                m = V_([m], lambda s=shift: V.tensor_scalar(turns, ang, float(1 / (2 * np.pi)), s, MUL, ADD))
                m = V_([m], lambda: V.tensor_scalar(turns, turns, MAGIC, MAGIC, ADD, SUB))
                m = V_([m] + act.last(), lambda: V.scalar_tensor_tensor(red, turns, -TWO_PI[0], ang, MUL, ADD))
                m = V_([m], lambda: V.scalar_tensor_tensor(red, turns, -TWO_PI[1], red, MUL, ADD))
                m = V_([m], lambda: V.scalar_tensor_tensor(red, turns, -TWO_PI[2], red, MUL, ADD))
                m = V_([m], lambda s=shift: V.tensor_scalar(red, red, float(2 * np.pi * s), 3.1415925, ADD, MIN))
                m = V_([m], lambda: V.tensor_scalar(red, red, -3.1415925, None, MAX))
                act.do([m], lambda tb=table: S.activation(tb[:, :], red, ACT.Sin))


        def load_post(src, k):
            return load(post_w[:, k, :], src.partition_broadcast(P), x_marks[0] + x_marks[1], group="post_gain")

        def residual(done, wrow, wmark, scratch, half):
            h = [psum[:, 2 * t:2 * t + 2, :] for t in range(NT)]
            sc = [scratch[:, t, :].rearrange("p (n c) -> p n c", n=2) for t in range(NT)]
            w = wrow.rearrange("p (n c) -> p n c", n=2)
            squared = [act.do([done[t]], lambda t=t: S.activation(sc[t], h[t], ACT.Square, accum_out=ssq[:, t:t + 1]))
                       for t in range(NT)]
            roots = [inverse_root(inv_rms[:, t:t + 1], ssq[:, t:t + 1], [squared[t]], 1.0 / D, gain=half) for t in range(NT)]
            marks = []
            for t in range(NT):
                m = V_([roots[t], wmark], lambda t=t: V.scalar_tensor_tensor(sc[t], h[t], inv_rms[:, t:t + 1], w, MUL, MUL))
                bank_free[2 * t] = bank_free[2 * t + 1] = [m]
                if t == 0:
                    m = V_([m], lambda: V.tensor_tensor(x[:, 0, :], x[:, 0, :], scratch[:, 0, :], ADD))
                else:
                    m = pool.do([m], lambda: G.tensor_tensor(x[:, 1, :], x[:, 1, :], scratch[:, 1, :], ADD))
                marks.append([m])
            x_marks[:] = marks

        def dump(name, tile, marks):
            if dbg and name in dbg:
                load(dbg[name], tile, marks + dve.last() + act.last() + pool.last() + pe.last(), group="dump")

        def ffn_sources(wg, wu, wd):
            sources = []
            for i in range(D_FF // 256 + 1):
                if i < D_FF // 256:
                    sources += [columns(wg, 256 * i), columns(wu, 256 * i)]
                if i:
                    sources.append(rows(wd, 2 * (i - 1)))
            return sources

        held = []

        def ffn(stream, gain_at, post_src):
            stage_start(held)
            stream.ahead(2)
            wmark = load_post(post_src, 0)
            scaled = carve(NT, D)
            silu, h32 = carve(2, TOK), carve(2, TOK)
            n_groups = D_FF // 256
            ready = norm_T(x, xnT, gain_at, scaled, x_marks, True)
            stream.ahead(4)
            h_ready, h_read, h32_read = [None] * n_groups, [[] for _ in range(NH)], [[], []]
            for i in range(n_groups + 1):
                if i < n_groups:
                    kg, gv, gland = stream.next()
                    ku, uv, uland = stream.next()
                    evac = []
                    for j in range(2):
                        b, free = take()
                        m = pe.do([gland, uland] + free + ready,
                                  *[op for o, wv in ((0, gv), (1, uv)) for k in range(KD) for op in
                                    three(psum[:, b, 256 * o:256 * o + 256], [wv[h][:, k, P * j:P * j + P] for h in range(2)],
                                          [x_hl[:, h, k, :] for h in range(2)], k == 0, k == KD - 1)])
                        evac.append((b, m))
                    hl_free[kg] = hl_free[ku] = [m]
                    for j, (b, m) in enumerate(evac):
                        ma = act.do([m] + h32_read[j], lambda b=b, j=j: S.activation(silu[:, j, :], psum[:, b, 0:256], ACT.Silu))
                        mv = V_([ma] + h32_read[j], lambda b=b, j=j: V.tensor_tensor(h32[:, j, :], silu[:, j, :], psum[:, b, 256:512], MUL))
                        bank_free[b] = [mv]
                        h_ready[i] = split(h32[:, j, :], h_hl[:, i % NH, 0, j, :], h_hl[:, i % NH, 1, j, :], [mv] + h_read[i % NH])
                        h32_read[j] = [h_ready[i]]
                    stream.ahead(3)
                if i:
                    g = (i - 1) % NH
                    done = split_out(stream, lambda h, j, g=g: h_hl[:, g, h, j, :], i == 1, i == n_groups, [h_ready[i - 1]])
                    h_read[g] = done
                    stream.ahead(4)
            held[:] = everything()
            residual(done, post_w[:, 0, :], wmark, scaled, 0.5)

        def inverses(systems, size, per, masks, levels, fill, LM, W, taken, banks):
            p = size
            state = []
            for s, (L, X, XT, lm) in enumerate(systems):
                state.append(dict(L=L, X=X, XT=XT, lm=lm, x=[], xt=[], w_read=[]))
            lm_read = [list(taken) for _ in systems]
            eye = ident[0:p, 0:p].unsqueeze(1).to_broadcast([p, per, size])

            def bank():
                b, free = take(banks)
                return b, psum[0:p, b, 0:per * size].rearrange("p (h n) -> p h n", h=per), free

            for n in range(len(levels)):
                last = n == len(levels) - 1
                for s, st in enumerate(state):
                    mk = C(masks[s])[0:p, P * n:P * n + size].unsqueeze(1).to_broadcast([p, per, size])
                    lmm = pool.do(st["lm"] + lm_read[s], lambda s=s, st=st, mk=mk: G.tensor_tensor(
                        LM[0:p, s], st["L"], mk, MUL))
                    b, bv, free = bank()
                    if n == 0:
                        m = pe.do([lmm] + free, *[mm(bv[:, h, :], LM[0:p, s, h, :], ident[0:p, 0:p]) for h in range(per)])
                        st["x"] = [V_([lmm], lambda s=s, st=st: V.tensor_tensor(st["X"], eye, LM[0:p, s], SUB))]
                        st["xt"] = [V_([m], lambda st=st, bv=bv: V.tensor_tensor(st["XT"], eye, bv, SUB))]
                        bank_free[b] = st["xt"]
                        lm_read[s] = st["x"] + [m]
                        continue
                    m = pe.do([lmm] + free + st["xt"], *[mm(bv[:, h, :], LM[0:p, s, h, :], st["XT"][:, h, :])
                                                        for h in range(per)])
                    lm_read[s] = [m]
                    st["w"] = act.do([m] + st["w_read"], lambda s=s, bv=bv: S.copy(W[0:p, s], bv))
                    bank_free[b] = [st["w"]]
                fill()
                if n == 0:
                    continue
                for s, st in enumerate(state):
                    b2, b2v, free2 = bank()
                    m2 = pe.do([st["w"]] + free2 + st["x"], *[mm(b2v[:, h, :], st["X"][:, h, :], W[0:p, s, h, :]) for h in range(per)])
                    st["w_read"] = [m2]
                    if not last:
                        b1, b1v, free1 = bank()
                        m1 = pe.do(free1, *[mm(b1v[:, h, :], W[0:p, s, h, :], st["X"][:, h, :]) for h in range(per)])
                        st["w_read"] = [m1]
                    st["xt"] = [V_([m2], lambda st=st, b2v=b2v: V.tensor_tensor(st["XT"], st["XT"], b2v, SUB))]
                    bank_free[b2] = st["xt"]
                    if not last:
                        st["x"] = [V_([m1], lambda st=st, b1v=b1v: V.tensor_tensor(st["X"], st["X"], b1v, SUB))]
                        bank_free[b1] = st["x"]
                fill()
            return [st["xt"] for st in state]

        def softplus(dst, src, scratch, after):
            m = act.do(after, lambda: S.activation(scratch, src, ACT.Abs))
            m = act.do([m], lambda: S.activation(scratch, scratch, ACT.Exp, scale=-1.0))
            m = act.do([m], lambda: S.activation(scratch, scratch, ACT.Ln, bias=1.0))
            return V_([m], lambda: V.scalar_tensor_tensor(dst, src, 0.0, scratch, MAX, ADD))

        WORK8 = tuple(range(8))

        def mixer(l, following):
            stage_start(held)
            wmark = load_post(a["norm_post"][l, 1], 0)
            mload = load(memv[:, :, :], a["mem"][0].rearrange("(t p) d -> p t d", p=P), group="memory")
            w = a["w_in"][l]
            W = 512
            BANKS = (2, 3, 4, 5, 6, 7)
            mix = carve(NT, D)
            scaled = mix
            ready = norm_T(x, xnT, 32 * l + 8, scaled, x_marks)
            colN = lambda c0, n=256: project_N(w, c0, xnT, ready, n, banks=BANKS)
            colT = lambda c0: project_T(w, c0, xnT, ready, banks=BANKS)

            ab = carve(NT, 16)
            g_a, sp_s, g, beta, ea = carve(NT, 8), carve(NT, 8), carve(NT, 8), carve(NT, 8), carve(8)
            b, pv, m = colN(8 * W, 16)
            m = V_([m], lambda pv=pv: V.tensor_copy(ab, pv))
            bank_free[b] = [m]
            mb = act.do([m], lambda: S.activation(beta, ab[:, :, 8:16], ACT.Sigmoid))
            mea = act.do([], lambda: S.activation(ea, alog[:, 8 * l:8 * l + 8], ACT.Exp))
            m = V_([m], lambda: V.tensor_tensor(g_a, ab[:, :, 0:8], dtb[:, 8 * l:8 * l + 8].unsqueeze(1).to_broadcast([P, NT, 8]), ADD))
            m = softplus(g, g_a, sp_s, [m])
            gm = V_([m, mea], lambda: V.scalar_tensor_tensor(g, g, -1.0, ea.unsqueeze(1).to_broadcast([P, NT, 8]), MUL, MUL))

            raw = carve(12, TOK + 4)
            qkv = carve(12, TOK)
            zero = pool.do([], lambda: G.memset(raw[:, :, 0:2], 0.0), lambda: G.memset(raw[:, :, TOK + 2:TOK + 4], 0.0))
            silu_done = []
            for i in range(6):
                b, pv, m = colT(4 * W + 256 * i)
                m = act.do([m, zero], lambda i=i, pv=pv: S.copy(raw[:, 2 * i:2 * i + 2, 2:TOK + 2], pv))
                bank_free[b] = [m]
                tap = lambda j, c: taps[:, 60 * l + 12 * j + c:60 * l + 12 * j + c + 1]
                pair = (2 * i, 2 * i + 1)
                mc = [V_([m, zero], lambda c=c, tap=tap: V.tensor_scalar(qkv[:, c, :], raw[:, c, 0:TOK], tap(0, c), None, MUL)) for c in pair]
                for j in range(1, 5):
                    mc = [V_([mc[c - 2 * i]], lambda c=c, j=j, tap=tap: V.scalar_tensor_tensor(
                        qkv[:, c, :], raw[:, c, j:j + TOK], tap(j, c), qkv[:, c, :], MUL, ADD)) for c in pair]
                mc = mc[1]
                if i == 1:
                    mem_s = memkT[:, :, :].rearrange("p (t k) n -> p t (k n)", t=NT)
                    mem_ready = norm_T(memv, memT, 64 + 8 * l, mem_s, [[mload], [mload]], banks=BANKS)
                silu_done.append(act.do([mc], lambda i=i: S.activation(qkv[:, 2 * i:2 * i + 2, :], qkv[:, 2 * i:2 * i + 2, :], ACT.Silu)))
            qT, kT, vT = qkv[:, 0:4, :], qkv[:, 4:8, :], qkv[:, 8:12, :]

            work_r = carve(2, 2, TOK)
            qk_done = [None] * 4
            nfree = [[], []]
            mem_jobs = []
            r_marks, dec_read, vbm = {}, [], []

            def keep(b, pv, m, dst, key, fn=None):
                if fn is None:
                    m = act.do([m] + dec_read + vbm, lambda: S.copy(dst, pv))
                else:
                    m = act.do([m], lambda: S.activation(dst, pv, fn))
                bank_free[b] = [m]
                r_marks[key] = m

            wk, wv_ = a["xattn_k"][l], a["xattn_v"][l]
            for i in range(4):
                mem_jobs.append(lambda i=i: keep(*project_T(wk, 256 * i, memT, mem_ready, BANKS), memkT[:, 2 * i:2 * i + 2, :], ("mk", i)))
                mem_jobs.append(lambda i=i: keep(*project_N(wv_, 256 * i, memT, mem_ready, banks=BANKS), memv[:, :, 256 * i:256 * i + 256], ("mv", i)))
            for i in range(4):
                sl = qkv[:, 2 * i:2 * i + 2, :]
                norm_s = work_r[:, i % 2]
                m = pool.do([silu_done[i]] + nfree[i % 2], lambda sl=sl, norm_s=norm_s: G.tensor_tensor(norm_s, sl, sl, MUL))
                b, free = take(BANKS)
                m = pe.do([m] + free, mm(psum[:, b, :], C("ones"), norm_s.rearrange("p a b -> p (a b)")))
                pv = psum[:, b, :].rearrange("p (a b) -> p a b", a=2)
                m = V_([m], lambda pv=pv, norm_s=norm_s: V.tensor_scalar(norm_s, pv, EPS, None, ADD))
                bank_free[b] = [m]
                m = act.do([m], lambda norm_s=norm_s: S.activation(norm_s, norm_s, ACT.Sqrt))
                m = V_([m], lambda norm_s=norm_s: V.reciprocal(norm_s, norm_s))
                sc = HD ** -0.5 if i < 2 else 1.0
                m = V_([m], lambda sl=sl, sc=sc, norm_s=norm_s: V.scalar_tensor_tensor(sl, sl, sc, norm_s, MUL, MUL))
                qk_done[i] = m
                nfree[i % 2] = [m]
                mem_jobs.pop(0)()

            kN, vN = carve(NT, HEADS, HD), carve(NT, HEADS, HD)
            kv_nat = []
            for src, dst, dep in ((kT, kN, qk_done[2:]), (vT, vN, silu_done[4:])):
                for t in range(NT):
                    b, free = take(BANKS)
                    m = pe.do(list(dep) + free, *[tr(psum[:, b, P * h:P * h + P], src[:, h, P * t:P * t + P]) for h in range(4)])
                    m = act.do([m], lambda dst=dst, t=t, b=b: S.copy(dst[:, t], psum[:, b, :].rearrange("p (h d) -> p h d", h=4)))
                    bank_free[b] = [m]
                    kv_nat.append(m)

            mem_jobs.pop(0)()
            combos = [(d, t) for d in range(2) for t in range(NT)]
            first = {0: 0, 1: 1}
            order = ("upto", "from")
            Gn, Gt = carve(4, 4), carve(4, 4)
            b, free = take(BANKS)
            ops = [mm(psum[:, b, 4 * c:4 * c + 4], C(order[d]), g[:, t, 4 * d:4 * d + 4]) for c, (d, t) in enumerate(combos)]
            ops += [mm(psum[:, b, 16 + 4 * c:20 + 4 * c], C("ones"), g[:, t, 4 * d:4 * d + 4]) for c, (d, t) in enumerate(combos)]
            m = pe.do([gm] + free, *ops)
            gn = V_([m], lambda b=b: V.tensor_copy(Gn, psum[:, b, 0:16].rearrange("p (c h) -> p c h", c=4)),
                    lambda b=b: V.tensor_copy(Gt, psum[:, b, 16:32].rearrange("p (c h) -> p c h", c=4)))
            bank_free[b] = [gn]
            tail, ebg = carve(4, 4), carve(4, 4)
            m = V_([gn], lambda: V.tensor_tensor(tail, Gt, Gn, SUB))
            mt_ = act.do([m], lambda: S.activation(tail, tail, ACT.Exp))
            m = act.do([gn], lambda: S.activation(ebg, Gn, ACT.Exp))
            me = V_([m, mb], *[lambda c=c, d=d, t=t: V.tensor_tensor(ebg[:, c], ebg[:, c], beta[:, t, 4 * d:4 * d + 4], MUL)
                               for c, (d, t) in enumerate(combos)])

            L, X, XT = carve(4, 4, P), carve(4, 4, P), carve(4, 4, P)
            QK = carve(4, 4, P)
            qg, vb, kbg, kt = carve(2, 4, P), carve(4, 4, P), carve(2, 4, P), carve(2, 4, P)
            dec = raw.rearrange("p a b -> p (a b)")[:, 0:1024].rearrange("p (a h n) -> p a h n", a=2, h=4)
            dec_read.append(silu_done[-1])
            lmarks, qkmarks, qgm, kbm, ktm = [], [], {}, {}, {}
            bc = lambda v: v.unsqueeze(2).to_broadcast([P, 4, P])
            for c, (d, t) in enumerate(combos):
                later = t != first[d]
                b, free = take(BANKS)
                bv = psum[:, b, :].rearrange("p (h n) -> p h n", h=4)
                m = pe.do([gm] + free, *[mm(bv[:, h, :], g[:, t, 4 * d + h:4 * d + h + 1].to_broadcast([P, P]), C(order[d])) for h in range(4)])
                m1 = V_([m, gn] + dec_read, *[lambda h=h, c=c, bv=bv: V.tensor_scalar(dec[:, 0, h, :], bv[:, h, :], Gn[:, c, h:h + 1], 0.0, SUB, MAX) for h in range(4)])
                m2 = V_([m1], *[lambda h=h, c=c, bv=bv: V.tensor_scalar(dec[:, 1, h, :], bv[:, h, :], Gn[:, c, h:h + 1], 0.0, SUB, MIN) for h in range(4)])
                fr = [m2]
                if later:
                    mq = act.do([m] + fr, lambda c=c, d=d, bv=bv: S.activation(qg[:, d], bv, ACT.Exp))
                    fr = fr + [mq]
                    qgm[d] = pool.do([mq] + qk_done[0:2], lambda d=d, t=t: G.tensor_tensor(qg[:, d], qg[:, d], qT[:, :, P * t:P * t + P], MUL))
                bank_free[b] = fr
                ma = act.do([m1], lambda: S.activation(dec[:, 0], dec[:, 0], ACT.Exp, scale=-1.0))
                mb2 = act.do([m2], lambda: S.activation(dec[:, 1], dec[:, 1], ACT.Exp))
                b1, free = take(BANKS)
                b1v = psum[:, b1, :].rearrange("p (h n) -> p h n", h=4)
                mk = pe.do(qk_done[2:] + free, *[mm(b1v[:, h, :], kT[:, h, P * t:P * t + P], kT[:, h, P * t:P * t + P]) for h in range(4)])
                ml = V_([mk, ma, mb], *[lambda h=h, c=c, d=d, t=t, b1v=b1v: V.scalar_tensor_tensor(
                    L[:, c, h, :], b1v[:, h, :], beta[:, t, 4 * d + h:4 * d + h + 1], dec[:, 0, h, :], MUL, MUL) for h in range(4)])
                bank_free[b1] = [ml]
                lmarks.append(ml)
                b2, free = take(BANKS)
                b2v = psum[:, b2, :].rearrange("p (h n) -> p h n", h=4)
                mk = pe.do(qk_done + free, *[mm(b2v[:, h, :], kT[:, h, P * t:P * t + P], qT[:, h, P * t:P * t + P]) for h in range(4)])
                mi = pool.do([mb2], lambda d=d: G.tensor_tensor(dec[:, 1], dec[:, 1], C(order[d]).unsqueeze(1).to_broadcast([P, 4, P]), MUL))
                mq = V_([mk, mi], lambda c=c, b2v=b2v: V.tensor_tensor(QK[:, c], b2v, dec[:, 1], MUL))
                bank_free[b2] = [mq]
                qkmarks.append(mq)
                dec_read[:] = [mq, ml]
                vbm.append(pool.do(kv_nat[2:] + [mb], lambda c=c, d=d, t=t: G.tensor_tensor(vb[:, c], vN[:, t], bc(beta[:, t, 4 * d:4 * d + 4]), MUL)))
                if later:
                    kbm[d] = pool.do(kv_nat[:2] + [me], lambda c=c, d=d, t=t: G.tensor_tensor(kbg[:, d], kN[:, t], bc(ebg[:, c]), MUL))
                else:
                    ktm[d] = pool.do(kv_nat[:2] + [mt_], lambda c=c, d=d, t=t: G.tensor_tensor(kt[:, d], kN[:, t], bc(tail[:, c]), MUL))
                if mem_jobs:
                    mem_jobs.pop(0)()

            qr = raw.rearrange("p a b -> p (a b)")[:, 0:2048].rearrange("p (a b) -> p a b", a=8)
            rv = vN.rearrange("p t h d -> p t (h d)")
            rg, z = (tail_2k[:, 1024 * k:1024 * k + 1024].rearrange("p (t n) -> p t n", t=NT) for k in range(2))
            pt_ring = [qkv[:, 8 + 2 * k:10 + 2 * k, :] for k in range(2)]
            decay = [work_r[:, k].rearrange("p a b -> p (a b)") for k in range(2)]
            ret_o = work_r.rearrange("p a b c -> p a (b c)")
            r4, sq_r = carve(4, 4), pt_ring[0].rearrange("p a (b n) -> p (a b) n", n=P)
            ret = {"decay": [[], []], "pt": [kv_nat, kv_nat], "o": [], "rt": {}}

            def rotary(i):
                src, rot_s = qr[:, 2 * i:2 * i + 2, :], pt_ring[i % 2]
                b, free = take(BANKS)
                pv = psum[:, b, :].rearrange("p (a b) -> p a b", a=2)
                m = pe.do([r_marks[("r", i)]] + free, mm(psum[:, b, :], C("rotate"), src.rearrange("p a b -> p (a b)")))
                ms = V_([m] + ret["pt"][i % 2], lambda: V.tensor_tensor(rot_s, pv, sinT[:, :].unsqueeze(1).to_broadcast([P, 2, TOK]), MUL))
                bank_free[b] = [ms]
                m = pool.do([m], lambda: G.tensor_tensor(src, src, cosT[:, :].unsqueeze(1).to_broadcast([P, 2, TOK]), MUL))
                ret["rt"][i] = V_([m, ms], lambda: V.tensor_tensor(src, src, rot_s, ADD))
                ret["pt"][i % 2] = [ret["rt"][i]]

            def retain(h):
                gf, gb = lg[:, 8 * l + h:8 * l + h + 1], lg[:, 8 * l + 4 + h:8 * l + 5 + h]
                dh, PT = decay[h % 2], pt_ring[h % 2].rearrange("p a b -> p (a b)")
                m = V_(ret["decay"][h % 2] + qk_done, lambda: V.tensor_scalar(dh, C("ahead"), gf, None, MUL))
                m = V_([m], lambda: V.scalar_tensor_tensor(dh, C("behind"), gb, dh, MUL, ADD))
                md = act.do([m], lambda: S.activation(dh, dh, ACT.Exp))
                b, free = take(BANKS)
                m = pe.do([ret["rt"][h // 2], ret["rt"][2 + h // 2]] + free,
                          *[mm(psum[:, b, 256 * j:256 * j + 256], qr[:, 4 + h, P * j:P * j + P], qr[:, h, :]) for j in range(2)])
                m = V_([m, md] + ret["pt"][h % 2], lambda: V.scalar_tensor_tensor(PT, psum[:, b, :], HD ** -0.5, dh, MUL, MUL))
                bank_free[b] = [m]
                ret["decay"][h % 2] = [m]
                if h == 0:
                    ret["o_free"] = bank_free[0] + bank_free[1]
                m = pe.do([m, r_marks[("v", 0)], r_marks[("v", 1)]] + ret["o_free"],
                          *[mm(psum[:, t, HD * h:HD * h + HD], PT[:, 256 * j + P * t:256 * j + P * t + P], rv[:, j, HD * h:HD * h + HD], j == 0, j == 1)
                            for t in range(NT) for j in range(2)])
                ret["pt"][h % 2] = [m]
                ret["o"].append(m)

            def retained(t):
                o = ret_o[:, t].rearrange("p (h n) -> p h n", h=4)
                bv = psum[:, t, :].rearrange("p (h n) -> p h n", h=4)
                mu, var = r4[:, 2, :], r4[:, 3, :]
                before = ret.get("ln", [])
                m = V_(ret["o"] + before, lambda: V.tensor_reduce(mu, bv, AXX, ADD))
                m = V_([m], lambda: V.tensor_scalar(mu, mu, 1.0 / HD, None, MUL))
                mc = V_([m] + ret["decay"][0] + ret["decay"][1], lambda: V.tensor_tensor(o, bv, bc(mu), SUB))
                bank_free[t] = [mc]
                ms = act.do([mc] + ret["pt"][0] + before, lambda: S.activation(sq_r, o, ACT.Square))
                mr = V_([ms], lambda: V.tensor_reduce(var, sq_r, AXX, ADD))
                mr = inverse_root(var, var, [mr], 1.0 / HD)
                m = V_([mr], lambda: V.tensor_tensor(o, o, bc(var), MUL))
                m = pool.do([m, r_marks[("g", 0)], r_marks[("g", 1)]], lambda: G.tensor_tensor(ret_o[:, t], ret_o[:, t], rg[:, t, :], MUL))
                ret["ln"] = [m]

            fills = [] + mem_jobs
            for i in range(4):
                fills.append(lambda i=i: keep(*colT(256 * i), qr[:, 2 * i:2 * i + 2, :], ("r", i)))
            for i in range(2):
                fills.append(lambda i=i: keep(*colN(2 * W + 256 * i), rv[:, :, 256 * i:256 * i + 256], ("v", i)))
                fills += [lambda i=i: rotary(2 * i), lambda i=i: rotary(2 * i + 1)]
            for i in range(2):
                fills.append(lambda i=i: keep(*colN(3 * W + 256 * i), rg[:, :, 256 * i:256 * i + 256], ("g", i), ACT.Silu))
                fills += [lambda i=i: retain(2 * i), lambda i=i: retain(2 * i + 1)]
            for i in range(2):
                fills.append(lambda i=i: keep(*colN(7 * W + 256 * i), z[:, :, 256 * i:256 * i + 256], ("z", i), ACT.Silu))
                fills.append(lambda i=i: retained(i))
            points = [2 * len(LEVELS) - 1]

            def fill():
                for _ in range(-(-len(fills) // max(points[0], 1))):
                    if fills:
                        fills.pop(0)()
                points[0] -= 1

            xts = inverses([(L[:, c], X[:, c], XT[:, c], [lmarks[c]]) for c in range(4)], P, 4,
                           ["fwd", "fwd", "bwd", "bwd"], LEVELS, fill,
                           mix.rearrange("p t (a h n) -> p (t a) h n", h=4, n=P),
                           qkv[:, 0:8, :].rearrange("p (c b) (h n) -> p c (b h) n", c=4, h=2),
                           qk_done + qkmarks + kv_nat + list(qgm.values()), BANKS)
            while fills:
                fills.pop(0)()

            u = L
            wT = X
            um, wm = [], {}
            for c, (d, t) in enumerate(combos):
                b, free = take(BANKS)
                bv = psum[:, b, :].rearrange("p (h n) -> p h n", h=4)
                m = pe.do(xts[c] + [vbm[c]] + free, *[mm(bv[:, h, :], XT[:, c, h, :], vb[:, c, h, :]) for h in range(4)])
                m = V_([m], lambda c=c, bv=bv: V.tensor_copy(u[:, c], bv))
                bank_free[b] = [m]
                um.append(m)
                if t != first[d]:
                    b, free = take(BANKS)
                    bv2 = psum[:, b, :].rearrange("p (h n) -> p h n", h=4)
                    m = pe.do(xts[c] + [kbm[d]] + free, *[mm(bv2[:, h, :], kbg[:, d, h, :], XT[:, c, h, :]) for h in range(4)])
                    m = act.do([m], lambda c=c, bv2=bv2: S.copy(wT[:, c], bv2))
                    bank_free[b] = [m]
                    wm[d] = m
            state = kN
            stm = {}
            for d in range(2):
                c1 = combos.index((d, first[d]))
                c2 = combos.index((d, 1 - first[d]))
                b, free = take(BANKS)
                bv = psum[:, b, :].rearrange("p (h n) -> p h n", h=4)
                m = pe.do([um[c1], ktm[d]] + free, *[mm(bv[:, h, :], kt[:, d, h, :], u[:, c1, h, :]) for h in range(4)])
                m = act.do([m] + list(kbm.values()) + list(ktm.values()), lambda d=d, bv=bv: S.copy(state[:, d], bv))
                bank_free[b] = [m]
                stm[d] = m
                b, free = take(BANKS)
                bv2 = psum[:, b, :].rearrange("p (h n) -> p h n", h=4)
                m = pe.do([stm[d], wm[d]] + free, *[mm(bv2[:, h, :], wT[:, c2, h, :], state[:, d, h, :]) for h in range(4)])
                m = V_([m, um[c2]], lambda c2=c2, bv2=bv2: V.tensor_tensor(u[:, c2], u[:, c2], bv2, SUB))
                bank_free[b] = [m]
                um[c2] = m
            sq = kbg[:, 1]
            mix_marks = []
            for t in range(NT):
                b, free = take(BANKS)
                bv = psum[:, b, :].rearrange("p (h n) -> p h n", h=4)
                ops = []
                dl = t if first[0] != t else 1
                for h in range(4):
                    dlate = 0 if first[0] != t else 1
                    dearly = 1 - dlate
                    cl, ce = combos.index((dlate, t)), combos.index((dearly, t))
                    ops += [mm(bv[:, h, :], qg[:, dlate, h, :], state[:, dlate, h, :], True, False),
                            mm(bv[:, h, :], QK[:, cl, h, :], u[:, cl, h, :], False, False),
                            mm(bv[:, h, :], QK[:, ce, h, :], u[:, ce, h, :], False, True)]
                m = pe.do(um + qkmarks + [qgm[0], qgm[1], stm[0], stm[1]] + free, *ops)
                ms = act.do([m] + mix_marks + list(wm.values()), lambda bv=bv: S.activation(sq, bv, ACT.Square))
                mr = V_([ms], lambda t=t: V.tensor_reduce(r4[:, t], sq, AXX, ADD))
                mr = inverse_root(r4[:, t], r4[:, t], [mr], 1.0 / HD)
                o = mix[:, t, W:2 * W].rearrange("p (h n) -> p h n", h=4)
                mo = V_([mr], lambda t=t, o=o, bv=bv: V.tensor_tensor(o, bv, bc(r4[:, t]), MUL))
                bank_free[b] = [mo]
                mo = pool.do([mo], lambda o=o: G.tensor_tensor(o, o, gnw[:, P * l:P * l + P].unsqueeze(1).to_broadcast([P, 4, P]), MUL))
                mo = pool.do([mo, r_marks[("z", 0)], r_marks[("z", 1)]], lambda t=t: G.tensor_tensor(mix[:, t, W:2 * W], mix[:, t, W:2 * W], z[:, t, :], MUL))
                mix_marks = [mo]
            gdn_done = mix_marks

            mixed = to_T(ret_o, mixT, ret["ln"], range(4)) + to_T(mix[:, :, W:2 * W], mixT, gdn_done, range(4, 8))
            arena_free = everything()
            for i in range(4):
                done = project_out(a["w_out"][l], 2 * i, 2, mixT, KD, mixed)
            for k in range(NHL):
                hl_free[k] = arena_free
            following.ahead(3)
            held[:] = everything()
            residual(done, post_w[:, 0, :], wmark, scaled, 1.0)

        def to_T(src, dstT, after, tiles=range(KD)):
            marks = []
            tiles = list(tiles)
            for t in range(NT):
                for g in range(0, len(tiles), 4):
                    n = min(4, len(tiles) - g)
                    b, free = take()
                    m = pe.do(after + free, *[tr(psum[:, b, P * j:P * j + P], src[:, t, P * (g + j):P * (g + j + 1)]) for j in range(n)])
                    m = V_([m], lambda b=b, g=g, t=t, n=n: V.tensor_copy(
                        dstT[:, tiles[g]:tiles[g] + n, P * t:P * t + P], psum[:, b, 0:P * n].rearrange("p (j n) -> p j n", j=n)))
                    bank_free[b] = [m]
                    marks.append(m)
            return marks

        def cross_sources(l):
            return [columns(a["xattn_q"][l], 256 * i) for i in range(4)] + [rows(a["xattn_o"][l], 2 * i) for i in range(4)]

        def cross(l, stream):
            stage_start(held)
            stream.ahead(3)
            wmark = load_post(a["norm_post"][l, 2], 0)
            scaled = carve(NT, D)
            ready = norm_T(x, xnT, 32 * l + 16, scaled, x_marks, True)
            stream.ahead(4)
            qT, oT = xnT, carve(KD, TOK)
            qm = []
            for i in range(4):
                b, pv, m = split_project_T(stream, ready)
                m = act.do([m] + ready, lambda i=i, pv=pv: S.copy(qT[:, 2 * i:2 * i + 2, :], pv))
                bank_free[b] = [m]
                qm.append(m)
            stream.ahead(4)
            prob, PT = scaled.rearrange("p t (h m) -> p h t m", h=HEADS), carve(HEADS, NT, TOK)
            top, total = (softmax_s[:, 8 * k:8 * k + 8].rearrange("p (h t) -> p h t", h=HEADS) for k in range(2))
            scale = 256 ** -0.5
            om = []
            for h in range(HEADS):
                b, free = take()
                m = pe.do([qm[h]] + free, *[mm(psum[:, b, 256 * t:256 * t + 256], qT[:, 2 * h + k, P * t:P * t + P], memkT[:, 2 * h + k, :], k == 0, k == 1)
                                            for t in range(NT) for k in range(2)])
                pv = psum[:, b, :].rearrange("p (t m) -> p t m", t=2)
                m = V_([m], lambda h=h, pv=pv: V.tensor_reduce(top[:, h], pv, AXX, MAX))
                m = V_([m], lambda h=h: V.tensor_scalar(top[:, h], top[:, h], -scale, None, MUL))
                for t in range(NT):
                    m = act.do([m], lambda h=h, t=t, pv=pv: S.activation(prob[:, h, t, :], pv[:, t, :], ACT.Exp, bias=top[:, h, t:t + 1],
                                                                        scale=scale, accum_out=total[:, h, t:t + 1]))
                bank_free[b] = [m]
                m = V_([m], lambda h=h: V.reciprocal(total[:, h], total[:, h]))
                m = V_([m], *[lambda h=h, t=t: V.tensor_scalar(prob[:, h, t, :], prob[:, h, t, :], total[:, h, t:t + 1], None, MUL) for t in range(2)])
                b, free = take()
                m = pe.do([m] + free, *[tr(psum[:, b, 256 * j + P * t:256 * j + P * t + P], prob[:, h, t, P * j:P * j + P]) for j in range(2) for t in range(2)])
                m = V_([m], lambda h=h, b=b: V.tensor_copy(PT[:, h], psum[:, b, :].rearrange("p (j t) -> p j t", j=2)))
                bank_free[b] = [m]
                b, free = take()
                m = pe.do([m] + free, *[mm(psum[:, b, 256 * e:256 * e + 256], memv[:, j, 256 * h + P * e:256 * h + P * e + P], PT[:, h, j, :], j == 0, j == 1)
                                        for e in range(2) for j in range(2)])
                m = act.do([m], lambda h=h, b=b: S.copy(oT[:, 2 * h:2 * h + 2, :], psum[:, b, :].rearrange("p (j t) -> p j t", j=2)))
                bank_free[b] = [m]
                om.append(split(oT[:, 2 * h:2 * h + 2, :], x_hl[:, 0, 2 * h:2 * h + 2, :], x_hl[:, 1, 2 * h:2 * h + 2, :], [m]))
            for i in range(4):
                stream.ahead(3)
                done = split_out(stream, lambda h, j, i=i: x_hl[:, h, 2 * i + j, :], i == 0, i == 3, [om[i]])
            stream.ahead(3)
            held[:] = everything()
            residual(done, post_w[:, 0, :], wmark, scaled, 1.0)

        def mlp_sources():
            sources = []
            for i in range(MLP // 256 + 1):
                if i < MLP // 256:
                    sources.append(columns(a["mlp_w1_2"][0], 256 * i))
                if i:
                    sources.append(rows(a["mlp_w2_2"][0], 2 * (i - 1)))
            return sources

        mlp_stream = SplitStream(mlp_sources())
        plan, nxt = {}, None
        for l in reversed(range(DEPTH)):
            plan["ffn2", l] = SplitStream(ffn_sources(a["ffn2_gate"][l], a["ffn2_up"][l], a["ffn2_down"][l]), nxt)
            plan["cross", l] = SplitStream(cross_sources(l), plan["ffn2", l])
            nxt = plan["ffn1", l] = SplitStream(ffn_sources(a["ffn1_gate"][l], a["ffn1_up"][l], a["ffn1_down"][l]))
        plan["ffn1", 0].load(3)
        late = late_loads()
        for l in range(DEPTH):
            ffn(plan["ffn1", l], 32 * l, a["norm_post"][l, 0])
            if l == 0:
                late_setup(late)
            dump(f"x{l}0", x[:, :, :], [])
            keep_tail[0] = True
            mixer(l, plan["cross", l])
            keep_tail[0] = False
            dump(f"x{l}1", x[:, :, :], [])
            cross(l, plan["cross", l])
            dump(f"x{l}2", x[:, :, :], [])
            ffn(plan["ffn2", l], 32 * l + 24, a["norm_post"][l, 3])
            dump(f"x{l}3", x[:, :, :], [])

        def mixer2(following):
            stage_start(held)
            wmark = load_post(a["norm_mix_post_2"][0], 0)
            w = a["w_in_2"][0]
            spare = [memkT[:, :, :].rearrange("p k t -> p (k t)"), memv[:, :, :].rearrange("p t d -> p (t d)")]
            shaped = lambda v, *s_: v.rearrange("p (a b) -> p a b", a=s_[0]) if len(s_) == 1 else \
                v.rearrange("p (a b c) -> p a b c", a=s_[0], b=s_[1])
            scaled = carve(NT, D)
            A0, H0, R0, U0 = 0, 768, 1792, 2688
            reach = carve(4, 384)
            rb = a["attn_rel_bias_2"]
            for h in range(4):
                load(reach[:, h, :], bass.AP(rb.tensor, h * 513 + 1, [[1, P], [1, 384]]), group="small2")
            lora = carve(256)
            load(lora[0:32, :], a["rwkv_w2_2"][0], group="small2")
            load(lora[32:64, :], a["rwkv_a2_2"][0], group="small2")
            load(lora[64:128, :], a["rwkv_g2_2"][0], group="small2")
            gate_w = carve(2, 2, P)
            zm = pool.do([], lambda: G.memset(gate_w, 0.0))
            for k, name in enumerate(("lru_wa_2", "lru_wx_2")):
                for n in range(4):
                    small2 = load(gate_w[64 * (n % 2):64 * (n % 2) + 64, k, n // 2, 64 * (n % 2):64 * (n % 2) + 64],
                                  a[name][0, n], [zm], group="small2")
            ready = norm_T(x, xnT, 80, scaled, x_marks)
            colT = lambda c0: project_T(w, c0, xnT, ready, banks=WORK8)
            colN = lambda c0: project_N(w, c0, xnT, ready, banks=WORK8)

            def kept(job, dst, fn=None, after=(), **kw):
                b, pv, m = job
                if fn is None:
                    m = act.do([m] + list(after), lambda: S.copy(dst, pv))
                else:
                    m = act.do([m] + list(after), lambda: S.activation(dst, pv, fn, **kw))
                bank_free[b] = [m]
                return m

            def half_sums(src, after):
                b, free = take(WORK8)
                m = pe.do(list(after) + free, mm(psum[:, b, :], C("half"), src))
                return b, psum[:, b, :].rearrange("p (j t) -> p j t", j=2), m

            pc = carve(7, TOK + 1)
            xs = carve(7, TOK)
            zc = pool.do([], lambda: G.memset(pc[:, :, 0:1], 0.0))
            pm = []
            for i in range(3):
                pm.append(kept(colT(R0 + 256 * i), pc[:, 2 * i:2 * i + 2, 1:TOK + 1]))
            s, wv, landed = slab(*columns(w, R0 + 768, P))
            b, free = take(WORK8)
            m = pe.do([landed] + free + ready, *[mm(psum[:, b, 0:256], wv[:, k, :], xnT[:, k, :], k == 0, k == KD - 1) for k in range(KD)])
            slot_free[s] = [m]
            m = act.do([m], lambda b=b: S.copy(pc[:, 6, 1:TOK + 1], psum[:, b, 0:256]))
            bank_free[b] = [m]
            pm.append(m)
            m = V_(pm + [zc], lambda: V.tensor_tensor(xs, pc[:, :, 0:TOK], pc[:, :, 1:TOK + 1], SUB))
            xm = V_([m], *[lambda k=k: V.scalar_tensor_tensor(xs[:, k, :], xs[:, k, :], vec("rwkv_mu_2", k), pc[:, k, 1:TOK + 1], MUL, ADD)
                           for k in (6, 2, 3, 0, 1, 4, 5)])
            rT, kT0, vT, lo = xs[:, 0:2, :], xs[:, 2:4, :], xs[:, 4:6, :], xs[:, 6, :]
            m1 = act.do([xm], lambda: S.activation(lo[64:128, :], lo[64:128, :], ACT.Sigmoid))
            m = act.do([xm], lambda: S.activation(lo[0:32, :], lo[0:32, :], ACT.Tanh))
            lw, aT, gT = carve(2, TOK), carve(2, TOK), carve(2, TOK)
            banks3 = []
            for p0, p1 in ((0, 32), (32, 64), (64, 128)):
                b, free = take(WORK8)
                ml = pe.do([m, m1, small2] + free, *[mm(psum[:, b, 256 * j:256 * j + 256], lora[p0:p1, P * j:P * j + P], lo[p0:p1, :]) for j in range(2)])
                banks3.append((b, ml))
            (b, ml) = banks3[0]
            m = act.do([ml], *[lambda j=j, b=b: S.activation(lw[:, j, :], psum[:, b, 256 * j:256 * j + 256], ACT.Sigmoid, bias=vec("rwkv_w0_2", j)) for j in range(2)])
            bank_free[b] = [m]
            lwm = V_([m], lambda: V.tensor_scalar(lw, lw, -float(np.exp(-0.5)), None, MUL))
            (b, ml) = banks3[1]
            am = act.do([ml], *[lambda j=j, b=b: S.activation(aT[:, j, :], psum[:, b, 256 * j:256 * j + 256], ACT.Sigmoid, bias=vec("rwkv_a0_2", j)) for j in range(2)])
            bank_free[b] = [am]
            (b, ml) = banks3[2]
            gm = act.do([ml], lambda b=b: S.copy(gT, psum[:, b, :].rearrange("p (j t) -> p j t", j=2)))
            bank_free[b] = [gm]
            kk, k2, t1 = carve(2, TOK), carve(2, TOK), carve(2, TOK)
            flat = lambda v: v.rearrange("p j t -> p (j t)")
            m = V_([xm], *[lambda j=j: V.tensor_scalar(kk[:, j, :], kT0[:, j, :], vec("rwkv_k_k_2", j), None, MUL) for j in range(2)])
            m2 = V_([m], lambda: V.tensor_tensor(t1, kk, kk, MUL))
            b, pv, m2 = half_sums(flat(t1), [m2])
            m2 = act.do([m2], lambda pv=pv: S.activation(t1, pv, ACT.Sqrt))
            bank_free[b] = [m2]
            m2 = V_([m2], lambda: V.tensor_scalar(t1, t1, 1e-12, None, MAX))
            m2 = V_([m2], lambda: V.reciprocal(t1, t1))
            kkm = V_([m2], lambda: V.tensor_tensor(kk, kk, t1, MUL))
            m = V_([am], *[lambda j=j: V.tensor_scalar(k2[:, j, :], aT[:, j, :], 1.0, vec("rwkv_k_a_2", j), SUB, MUL) for j in range(2)])
            k2m = V_([m], lambda: V.scalar_tensor_tensor(k2, k2, 1.0, kT0, ADD, MUL))
            cum, ecum, eneg, eprev = carve(2, TOK), carve(2, TOK), carve(2, TOK), carve(2, TOK)
            cm = V_([lwm], *[lambda j=j: V.tensor_tensor_scan(cum[:, j, :], C("resets"), lw[:, j, :], 0.0, MUL, ADD) for j in range(2)])
            m = V_([cm], lambda: V.tensor_tensor(eprev, cum, lw, SUB))
            e1 = act.do([cm], lambda: S.activation(ecum, cum, ACT.Exp))
            e2 = act.do([cm], lambda: S.activation(eneg, cum, ACT.Exp, scale=-1.0))
            e3 = act.do([m], lambda: S.activation(eprev, eprev, ACT.Exp))
            alpha, betaT, khat, rhat = eprev, carve(2, TOK), carve(2, TOK), carve(2, TOK)
            alm = pool.do([e3, kkm], lambda: G.tensor_tensor(alpha, eprev, kk, MUL))
            m = pool.do([kkm, am, e2], lambda: G.tensor_tensor(betaT, kk, aT, MUL))
            btm = pool.do([m], lambda: G.tensor_tensor(betaT, betaT, eneg, MUL))
            khm = pool.do([k2m, e2], lambda: G.tensor_tensor(khat, k2, eneg, MUL))
            rhm = pool.do([e1, xm], lambda: G.tensor_tensor(rhat, rT, ecum, MUL))
            natb, natk, natv = carve(4, 256), carve(4, 256), carve(4, 256)
            natm = []
            for src, dst, dep, sign in ((betaT, natb, btm, -1.0), (khat, natk, khm, 1.0), (vT, natv, xm, 1.0)):
                for half in range(2):
                    b, free = take(WORK8)
                    m = pe.do([dep] + free, *[tr(psum[0:64, b, 256 * c + P * j:256 * c + P * j + P],
                                                 src[:, j, 128 * half + 64 * c:128 * half + 64 * c + 64]) for c in range(2) for j in range(2)])
                    m = act.do([m], lambda dst=dst, half=half, b=b, sign=sign: S.mul(
                        dst[0:64, 2 * half:2 * half + 2, :], psum[0:64, b, :].rearrange("p (c n) -> p c n", c=2), sign))
                    bank_free[b] = [m]
                    natm.append(m)
            Lr, Xr, XTr, Ak = (shaped(spare[k // 2][:, 1024 * (k % 2):1024 * (k % 2) + 1024], 2, 8) for k in range(4))
            Rb, Rk = carve(2, 8, 64), carve(2, 8, 64)
            pair_m = {n: [] for n in "LABK"}
            for s2 in range(2):
                for key, left, right, dst, mask in (("L", alpha, betaT, Lr, None), ("A", khat, alpha, Ak, "before"),
                                                    ("B", betaT, rhat, Rb, "upto"), ("K", khat, rhat, Rk, "upto")):
                    for e in range(2):
                        b, free = take(WORK8)
                        bv = psum[0:64, b, 0:256].rearrange("p (n s) -> p n s", n=4)
                        rows64 = slice(64 * e, 64 * e + 64)
                        at = lambda n: slice(64 * (2 * s2 + n // 2), 64 * (2 * s2 + n // 2) + 64)
                        m = pe.do([alm, btm, khm, rhm] + free, *[mm(bv[:, n, :], left[rows64, n % 2, at(n)], right[rows64, n % 2, at(n)])
                                                                for n in range(4)])
                        o = dst[0:64, s2].rearrange("p (n e) s -> p e n s", e=2)[:, e]
                        if mask is None:
                            m = act.do([m], lambda o=o, bv=bv: S.copy(o, bv))
                        else:
                            m = V_([m], lambda o=o, bv=bv, mask=mask: V.tensor_tensor(
                                o, bv, C(mask)[0:64, 0:64].unsqueeze(1).to_broadcast([64, 4, 64]), MUL))
                        bank_free[b] = [m]
                        if key == "B":
                            m = pool.do([m], lambda o=o: G.tensor_scalar(o, o, -1.0, None, MUL))
                        pair_m[key].append(m)

            qa, ka, va = carve(2, TOK), carve(2, TOK), carve(NT, 256)
            prob = shaped(pc.rearrange("p a b -> p (a b)")[:, 0:1536], 4, 3)
            PTa = carve(4, 3, P)
            ya = carve(NT, 256)
            top, total = carve(4, 2), carve(4, 2)
            marks = {}

            def attention_in():
                b, pv, m = colT(A0)
                marks["q"] = act.do([m], lambda pv=pv: S.mul(qa, pv, 64 ** -0.5))
                bank_free[b] = [marks["q"]]
                marks["k"] = kept(colT(A0 + 256), ka)
                marks["v"] = kept(colN(A0 + 512), va)

            def attention_head(h):
                hb, j = 64 * (h % 2), h // 2
                b, free = take(WORK8)
                ops = [mm(psum[:, b, 0:128], qa[hb:hb + 64, j, 0:128], ka[hb:hb + 64, j, 0:128], True, False),
                       mm(psum[:, b, 0:128], C("flip"), reach[:, h, 128:256], False, True),
                       mm(psum[:, b, 128:384], qa[hb:hb + 64, j, 128:256], ka[hb:hb + 64, j, :], True, False),
                       mm(psum[:, b, 128:384], C("flip"), reach[:, h, 0:256], False, True)]
                m = pe.do([marks["q"], marks["k"], small2] + free, *ops)
                m = V_([m], lambda b=b: V.tensor_tensor(psum[:, b, 64:128], psum[:, b, 64:128], C("barred"), ADD),
                       lambda b=b: V.tensor_tensor(psum[:, b, 320:384], psum[:, b, 320:384], C("barred"), ADD))
                m = V_([m], lambda b=b: V.tensor_reduce(top[:, h, 0:1], psum[:, b, 0:128], AXX, MAX),
                       lambda b=b: V.tensor_reduce(top[:, h, 1:2], psum[:, b, 128:384], AXX, MAX))
                m = V_([m], lambda: V.tensor_scalar(top[:, h], top[:, h], -1.0, None, MUL))
                for t, (lo_, hi_) in enumerate(((0, 128), (128, 384))):
                    m = act.do([m, xm], lambda b=b, t=t, lo_=lo_, hi_=hi_: S.activation(
                        prob[:, h].rearrange("p a b -> p (a b)")[:, lo_:hi_], psum[:, b, lo_:hi_], ACT.Exp,
                        bias=top[:, h, t:t + 1], accum_out=total[:, h, t:t + 1]))
                bank_free[b] = [m]
                mr = V_([m], lambda: V.reciprocal(total[:, h], total[:, h]))
                b, free = take(WORK8)
                m = pe.do([m] + free, *[tr(psum[:, b, P * k:P * k + P], prob[:, h, k, :]) for k in range(3)])
                m = act.do([m], lambda b=b: S.copy(PTa[:, h], psum[:, b, 0:384].rearrange("p (a b) -> p a b", a=3)))
                bank_free[b] = [m]
                b, free = take(WORK8)
                m = pe.do([m, marks["v"]] + free, mm(psum[:, b, 0:64], PTa[:, h, 0, :], va[:, 0, 64 * h:64 * h + 64]),
                          *[mm(psum[:, b, 64:128], PTa[:, h, 1 + k, :], va[:, k, 64 * h:64 * h + 64], k == 0, k == 1) for k in range(2)])
                m = V_([m, mr], *[lambda b=b, t=t: V.tensor_scalar(ya[:, t, 64 * h:64 * h + 64], psum[:, b, 64 * t:64 * t + 64],
                                                                  total[:, h, t:t + 1], None, MUL) for t in range(2)])
                bank_free[b] = [m]
                marks[("ya", h)] = m

            xd, conv = carve(2, TOK + 3), kT0
            gr, gi, yd = (shaped(v, 2) for v in (C("ahead"), C("behind"), C("bwd")[:, 0:512]))
            sp_l = carve(2)
            lt = carve(3, 2)

            def lru():
                z0 = pool.do([], lambda: G.memset(xd[:, :, 0:3], 0.0))
                m = kept(colT(U0), xd[:, :, 3:TOK + 3])
                mg = kept(colT(U0 + 256), yd, ACT.Gelu_apprx_tanh)
                for j in range(2):
                    mc = V_([m, z0, k2m], lambda j=j: V.tensor_scalar(conv[:, j, :], xd[:, j, 0:TOK], vec("lru_conv_w_2", j),
                                                                 vec("lru_conv_b_2", j), MUL, ADD))
                    for n in range(1, 4):
                        mc = V_([mc], lambda j=j, n=n: V.scalar_tensor_tensor(conv[:, j, :], xd[:, j, n:n + TOK],
                                                                              vec("lru_conv_w_2", 2 * n + j), conv[:, j, :], MUL, ADD))
                for k, dst, name in ((0, gr, "lru_ba_2"), (1, gi, "lru_bx_2")):
                    b, free = take(WORK8)
                    m = pe.do([mc, small2] + free, *[mm(psum[:, b, 256 * j:256 * j + 256], gate_w[:, k, j, :], conv[:, j, :]) for j in range(2)])
                    m = act.do([m], *[lambda j=j, b=b, dst=dst, name=name: S.activation(
                        dst[:, j, :], psum[:, b, 256 * j:256 * j + 256], ACT.Sigmoid, bias=vec(name, j)) for j in range(2)])
                    bank_free[b] = [m]
                lam = vecs[:, vec_at["lru_lambda_2"]:vec_at["lru_lambda_2"] + 2]
                e_, z_, q_ = lt[:, 0], lt[:, 1], lt[:, 2]
                ml = act.do([], lambda: S.activation(e_, lam, ACT.Abs))
                ml = act.do([ml], lambda: S.activation(e_, e_, ACT.Exp, scale=-1.0))
                ml = V_([ml], lambda: V.tensor_scalar(z_, e_, 2.0, None, ADD))
                ml = V_([ml], lambda: V.reciprocal(z_, z_))
                ml = V_([ml], lambda: V.tensor_tensor(z_, z_, e_, MUL))
                ml = V_([ml], lambda: V.tensor_tensor(q_, z_, z_, MUL))
                ml = V_([ml], lambda: V.tensor_scalar(e_, q_, 1.0 / 17, 1.0 / 15, MUL, ADD))
                for n in (13, 11, 9, 7, 5, 3, 1):
                    ml = V_([ml], lambda: V.tensor_tensor(e_, e_, q_, MUL))
                    ml = V_([ml], lambda n=n: V.tensor_scalar(e_, e_, 1.0 / n, None, ADD))
                ml = V_([ml], lambda: V.tensor_tensor(z_, z_, e_, MUL))
                ml = V_([ml], lambda: V.tensor_scalar(q_, lam, -1.0, 0.0, MUL, MAX))
                ml = V_([ml], lambda: V.scalar_tensor_tensor(sp_l, z_, 2.0, q_, MUL, ADD))
                mu_ = V_([ml, m], *[lambda j=j: V.tensor_scalar(gr[:, j, :], gr[:, j, :], sp_l[:, j:j + 1], 8.0, MUL, MUL) for j in range(2)])
                mi = pool.do([m, mc], lambda: G.tensor_tensor(gi, gi, conv, MUL))
                th, aa = conv, xd[:, :, 0:TOK]
                m1 = act.do([mu_, mi], lambda: S.activation(th, gr, ACT.Tanh))
                m2 = act.do([mu_, mc], lambda: S.activation(aa, gr, ACT.Exp, scale=-1.0))
                m3 = pool.do([m2], lambda: G.tensor_tensor(gr, aa, aa, MUL))
                m3 = V_([m3, m1], lambda: V.scalar_tensor_tensor(th, gr, 1.0, th, ADD, MUL))
                m3 = act.do([m3], lambda: S.activation(th, th, ACT.Sqrt))
                m3 = pool.do([m3], lambda: G.tensor_tensor(gi, gi, th, MUL))
                m3 = V_([m3, m2], *[lambda j=j: V.tensor_tensor_scan(gr[:, j, :], aa[:, j, :], gi[:, j, :], 0.0, MUL, ADD) for j in range(2)])
                marks["yd"] = V_([m3, mg], lambda: V.tensor_tensor(yd, yd, gr, MUL))

            qb, fb, ib, kb = carve(2, TOK), carve(2, TOK), carve(2, TOK), carve(2, TOK)
            gbn, yb = carve(NT, 256), eneg
            lb = carve(4, 2)

            def hgrn_in():
                lgt = vecs[:, vec_at["hgrn_lb_logits_2"]:vec_at["hgrn_lb_logits_2"] + 2]
                m = V_([], lambda: V.tensor_tensor(lb[:, 0], lgt, lgt, SUB))
                m = act.do([m], lambda: S.activation(lb[:, 0], lb[:, 0], ACT.Exp))
                m = V_([m], lambda: V.reciprocal(lb[:, 1], lb[:, 0]))
                m = V_([m], lambda: V.tensor_tensor(lb[:, 0], lb[:, 0], lb[:, 1], MUL))
                m = V_([m], lambda: V.tensor_tensor(lb[:, 2], lb[:, 0], lb[:, 0], SUB))
                m = V_([m], lambda: V.tensor_scalar(lb[:, 2], lb[:, 2], 0.0, None, MAX))
                ml = V_([m], lambda: V.tensor_scalar(lb[:, 3], lb[:, 2], -1.0, 1.0, MUL, ADD))
                marks["hq"] = kept(colT(H0), qb, ACT.Silu)
                b, pv, m = colT(H0 + 256)
                m1 = act.do([m], lambda pv=pv: S.activation(fb, pv, ACT.Sigmoid))
                m2 = act.do([m1], lambda pv=pv: S.activation(kb, pv, ACT.Sigmoid, scale=-1.0))
                bank_free[b] = [m2]
                marks["hf"] = V_([m2, ml], *[lambda j=j: V.tensor_scalar(fb[:, j, :], fb[:, j, :], lb[:, 3, j:j + 1], lb[:, 2, j:j + 1], MUL, ADD) for j in range(2)],
                                 *[lambda j=j: V.tensor_scalar(kb[:, j, :], kb[:, j, :], lb[:, 3, j:j + 1], None, MUL) for j in range(2)])
                marks["hi"] = kept(colT(H0 + 512), ib)
                marks["hg"] = kept(colN(H0 + 768), gbn, ACT.Silu)

            attention_in()
            hgrn_in()
            jobs = [lru] + [lambda h=h: attention_head(h) for h in range(4)]

            def fill():
                if jobs:
                    jobs.pop(0)()

            LMr, Wr = (shaped(scaled[:, k, :], 2, 8) for k in range(2))
            xts = inverses([(Lr[0:64, s_], Xr[0:64, s_], XTr[0:64, s_], pair_m["L"][2 * s_:2 * s_ + 2]) for s_ in range(2)],
                           64, 8, ["fwd", "fwd"], LEVELS[:6], fill, LMr, Wr, [], WORK8)
            while jobs:
                jobs.pop(0)()

            ST = cosT[:, :].rearrange("p (j n) -> p j n", j=2)
            rhs, sa, yn, av = (v.rearrange("p s n t -> p (s n t)").rearrange("p (c n) -> p c n", c=4) for v in (Lr, Xr, LMr, Wr))
            inverted = xts[0] + xts[1]
            stm = pool.do([], lambda: G.memset(ST, 0.0))

            avm = []
            for c in range(4):
                b, free = take((0, 1))
                m = pe.do(pair_m["A"] + natm + free, *[mm(psum[0:64, b, 64 * h:64 * h + 64], Ak[0:64, c // 2, 4 * (c % 2) + h, :], natv[0:64, c, 64 * h:64 * h + 64]) for h in range(4)])
                m = act.do([m] + inverted, lambda c=c, b=b: S.copy(av[0:64, c, :], psum[0:64, b, 0:256]))
                bank_free[b] = [m]
                avm.append(m)

            rw_m = {"st": stm, "y": []}

            def rwkv_chunk(c):
                s_, n0 = c // 2, 4 * (c % 2)
                b, free = take((0, 1))
                m = pe.do([rw_m["st"], alm] + free, *[mm(psum[0:64, b, P * j:P * j + P], alpha[:, j, 64 * c:64 * c + 64], ST[:, j, :]) for j in range(2)])
                yield
                m = V_([m, avm[c]], lambda c=c, b=b: V.tensor_tensor(rhs[0:64, c, :], psum[0:64, b, 0:256], av[0:64, c, :], ADD))
                bank_free[b] = [m]
                b, free = take((0, 1))
                yield
                m = pe.do([m] + xts[s_] + free, *[mm(psum[0:64, b, 64 * h:64 * h + 64], XTr[0:64, s_, n0 + h, :], rhs[0:64, c, 64 * h:64 * h + 64]) for h in range(4)])
                ms = V_([m], lambda c=c, b=b: V.tensor_copy(sa[0:64, c, :], psum[0:64, b, 0:256]))
                bank_free[b] = [ms]
                yield
                if c < 3:
                    b, free = take((2, 3))
                    m = pe.do([ms] + natm + free, *[op for j in range(2) for op in (
                        mm(psum[:, b, P * j:P * j + P], natb[0:64, c, P * j:P * j + P], sa[0:64, c, P * j:P * j + P], True, False),
                        mm(psum[:, b, P * j:P * j + P], natk[0:64, c, P * j:P * j + P], natv[0:64, c, P * j:P * j + P], False, True))])
                b2, free2 = take((2, 3))
                ops = []
                for j in range(2):
                    ops.append(mm(psum[0:64, b2, P * j:P * j + P], rhat[:, j, 64 * c:64 * c + 64], ST[:, j, :], True, False))
                    for h in (2 * j, 2 * j + 1):
                        ops.append(mm(psum[0:64, b2, 64 * h:64 * h + 64], Rb[0:64, s_, n0 + h, :], sa[0:64, c, 64 * h:64 * h + 64], False, False))
                        ops.append(mm(psum[0:64, b2, 64 * h:64 * h + 64], Rk[0:64, s_, n0 + h, :], natv[0:64, c, 64 * h:64 * h + 64], False, h == 2 * j + 1))
                my = pe.do([ms, rw_m["st"]] + pair_m["B"] + pair_m["K"] + free2, *ops)
                mq = act.do([my], lambda c=c, b2=b2: S.copy(yn[0:64, c, :], psum[0:64, b2, 0:256]))
                bank_free[b2] = [mq]
                rw_m["y"].append(mq)
                yield
                if c < 3:
                    m = V_([m, my], lambda b=b: V.tensor_tensor(ST, psum[:, b, 0:256].rearrange("p (j n) -> p j n", j=2), ST, ADD))
                    bank_free[b] = [m]
                    rw_m["st"] = V_([m], *[lambda j=j, c=c: V.scalar_tensor_tensor(ST[:, j, :], ST[:, j, :], ecum[:, j, 64 * c + 63:64 * c + 64],
                                                                                  C("half"), MUL, MUL) for j in range(2)])
                yield

            scratch = [reach.rearrange("p a b -> p (a b)"), PTa.rearrange("p a b c -> p (a b c)")]
            NB, NZ, LAG = 2, 3, 2
            pair = lambda v, n: [v[:, 512 * k:512 * k + 512] for k in range(n)]
            add_b, st_b, z_b = pair(scratch[0], 2), [scratch[0][:, 1024:1536], flat(aT)], pair(scratch[1], 3)
            attended = [marks[("ya", h)] for h in range(4)] + [btm, k2m]
            z_read = [attended for _ in range(NZ)]
            s_read = [attended for _ in range(NB)]
            a_read = [attended for _ in range(NB)]
            yb_bank = 7
            picks = [sinT[:, 0:128], sinT[:, 128:256]]
            pick_read = [[], []]
            yv = psum[:, yb_bank, :].rearrange("p (t j v h) -> p t j v h", t=2, j=2, h=2)
            yb_free = list(bank_free[yb_bank])
            chunk_steps = (None for c in range(4) for _ in rwkv_chunk(c))
            zm_ = {}
            fz = V_([marks["hf"]], lambda: V.memset(fb[:, :, 0:1], 0.0))
            for v in range(64 + LAG):
                if v < 64:
                    b, free = take((4, 5, 6))
                    pick = picks[v % 2]
                    mp = act.do(pick_read[v % 2], lambda v=v, pick=pick: S.copy(
                        pick.rearrange("p (h k) -> p h k", h=2), ident.rearrange("p (h v) -> p h v", h=2)[:, :, v:v + 1].to_broadcast([P, 2, 64])))
                    mi = pe.do([mp, marks["hi"]] + free, mm(psum[:, b, :], pick, flat(ib)))
                    pick_read[v % 2] = [mi]
                    k, kz = v % NB, v % NZ
                    ma = V_([mi, marks["hf"]] + a_read[k], lambda k=k, b=b: V.tensor_tensor(add_b[k], flat(kb), psum[:, b, :], MUL))
                    ms = V_([ma, fz] + s_read[k], lambda k=k: V.tensor_tensor_scan(st_b[k], flat(fb), add_b[k], 0.0, MUL, ADD))
                    a_read[k] = [ms]
                    mz = pool.do([ms, marks["hq"]] + z_read[kz], lambda k=k, kz=kz: G.tensor_tensor(z_b[kz], st_b[k], flat(qb), MUL))
                    s_read[k] = [mz]
                    zm_[v] = mz
                    bank_free[b] = [ma]
                if v >= LAG:
                    n = v - LAG
                    my = pe.do([zm_[n]] + yb_free, *[mm(yv[:, t, j, n, :], z_b[n % NZ][:, 256 * j + P * t:256 * j + P * t + P], C("headcol"))
                                                     for j in range(2) for t in range(2)])
                    z_read[n % NZ] = [my]
                if v % 2:
                    next(chunk_steps, None)
            for _ in chunk_steps:
                pass
            ybh = yb.rearrange("p t (h v) -> p t h v", h=4)
            sq4, r8 = lw.rearrange("p t (h v) -> p t h v", h=4), carve(NT, 4)
            src = psum[:, yb_bank, :].rearrange("p (t j v h) -> p t j h v", t=2, j=2, h=2)
            m = act.do([my], *[lambda t=t, j=j: S.copy(ybh[:, t, 2 * j:2 * j + 2, :], src[:, t, j]) for t in range(2) for j in range(2)])
            bank_free[yb_bank] = [m]
            m2 = act.do([m], lambda: S.activation(sq4, ybh, ACT.Square))
            m2 = V_([m2], lambda: V.tensor_reduce(r8, sq4, AXX, ADD))
            m2 = inverse_root(r8.rearrange("p t h -> p (t h)"), r8.rearrange("p t h -> p (t h)"), [m2], 1.0 / 64)
            m = V_([m2], lambda: V.tensor_tensor(ybh, ybh, r8.unsqueeze(3).to_broadcast([P, NT, 4, 64]), MUL))
            m = V_([m], lambda: V.tensor_tensor(yb, yb, hgn[:, :].unsqueeze(1).to_broadcast([P, NT, 256]), MUL))
            ybm = V_([m, marks["hg"]], lambda: V.tensor_tensor(yb, yb, gbn, MUL))

            yT = cum
            b, free = take((4, 5, 6))
            m = pe.do(rw_m["y"] + free, *[tr(psum[:, b, 256 * j + 64 * c:256 * j + 64 * c + 64], yn[0:64, c, P * j:P * j + P]) for j in range(2) for c in range(4)])
            m = act.do([m, e1, e2], lambda b=b: S.copy(yT, psum[:, b, :].rearrange("p (j t) -> p j t", j=2)))
            bank_free[b] = [m]
            b, pv, ms = half_sums(flat(yT), [m])
            m = V_([ms, m], lambda pv=pv: V.scalar_tensor_tensor(yT, pv, -1.0 / 64, yT, MUL, ADD))
            bank_free[b] = [m]
            ms = act.do([m], lambda: S.activation(t1, yT, ACT.Square))
            b, pv, ms = half_sums(flat(t1), [ms])
            ms = V_([ms], lambda pv=pv: V.tensor_scalar(t1, pv, 1.0 / 64, 64 * 1e-5, MUL, ADD))
            bank_free[b] = [ms]
            ms = act.do([ms], lambda: S.activation(t1, t1, ACT.Sqrt))
            ms = V_([ms], lambda: V.reciprocal(t1, t1))
            m = V_([m, ms], lambda: V.tensor_tensor(yT, yT, t1, MUL))
            m = V_([m], *[lambda j=j: V.tensor_scalar(yT[:, j, :], yT[:, j, :], vec("rwkv_ln_w_2", j), vec("rwkv_ln_b_2", j), MUL, ADD) for j in range(2)])
            ms = V_([m], *[lambda j=j: V.scalar_tensor_tensor(t1[:, j, :], rT[:, j, :], vec("rwkv_r_k_2", j), k2[:, j, :], MUL, MUL) for j in range(2)])
            b, pv, ms = half_sums(flat(t1), [ms])
            ms = V_([ms], lambda pv=pv: V.tensor_tensor(t1, pv, vT, MUL))
            bank_free[b] = [ms]
            m = V_([ms], lambda: V.tensor_tensor(yT, yT, t1, ADD))
            m = V_([m, gm], lambda: V.tensor_tensor(mixT[:, 4:6, :], yT, gT, MUL))
            m1 = V_([marks["yd"]], lambda: V.tensor_copy(mixT[:, 6:8, :], yd))
            mixed = [m, m1]
            mixed += to_T(ya, mixT, [marks[("ya", h)] for h in range(4)], (0, 1))
            mixed += to_T(yb, mixT, [ybm], (2, 3))
            dump("mix3", mixT[:, :, :], mixed)
            arena_free = everything()
            for i in range(4):
                done = project_out(a["w_out_2"][0], 2 * i, 2, mixT, KD, mixed)
            for k in range(NHL):
                hl_free[k] = arena_free
            following.ahead(3)
            held[:] = everything()
            residual(done, post_w[:, 0, :], wmark, scaled, 1.0)

        def relu2_mlp(stream):
            stage_start(held)
            stream.ahead(3)
            wmark = load_post(a["norm_mlp_post_2"][0], 0)
            scaled = carve(NT, D)
            n_groups = MLP // 256
            ready = norm_T(x, xnT, 88, scaled, x_marks, True)
            stream.ahead(3)
            h32 = carve(2, 2, TOK)
            h_ready, h_read = [None] * n_groups, [[] for _ in range(NH)]
            for i in range(n_groups + 1):
                if i < n_groups:
                    b, pv, m = split_project_T(stream, ready)
                    hv, g = h32[:, i % 2], i % NH
                    m = act.do([m] + (h_ready[i - 2:i - 1] if i > 1 else []), lambda hv=hv, pv=pv: S.activation(hv, pv, ACT.Relu))
                    bank_free[b] = [m]
                    m = V_([m], lambda hv=hv: V.tensor_tensor(hv, hv, hv, MUL))
                    h_ready[i] = split(hv, h_hl[:, g, 0], h_hl[:, g, 1], [m] + h_read[g])
                    stream.ahead(3)
                if i:
                    g = (i - 1) % NH
                    done = split_out(stream, lambda h, j, g=g: h_hl[:, g, h, j, :], i == 1, i == n_groups, [h_ready[i - 1]])
                    h_read[g] = done
                    stream.ahead(3)
            residual(done, post_w[:, 0, :], wmark, scaled, 1.0)

        mixer2(mlp_stream)
        dump("x20", x[:, :, :], [])
        relu2_mlp(mlp_stream)

        out_sem = sem("out_written")
        for t in range(NT):
            wm = sp.dma(x_marks[t], out_sem, 16 * (t + 1), out[0, P * t:P * t + P, :], x[:, t, :])
        sp.wait([wm] + [(s, n) for s, n in load_sems.values()])

        with nc.Block() as block:
            @block.sync
            def _(e):
                sp.play(e)

            @block.tensor
            def _(e):
                pe.play(e)

            @block.vector
            def _(e):
                dve.play(e)

            @block.scalar
            def _(e):
                act.play(e)

            @block.gpsimd
            def _(e):
                pool.play(e)


def kernel(**inputs):
    import concourse.bacc as bacc
    from concourse.bass_utils import run_bass_kernel_spmd

    nc = bacc.Bacc("TRN2", target_bir_lowering=False, num_devices=1)
    arrays = {f"in_{k}": np.ascontiguousarray(v) for k, v in inputs.items()}
    arrays["in_consts"] = shape_constants()[0]
    a = {k[3:]: nc.dram_tensor(k, v.shape, mybir.dt.from_np(v.dtype), kind="ExternalInput").ap()
         for k, v in arrays.items()}
    out = nc.dram_tensor("out_x", (1, TOK, D), F32, kind="ExternalOutput").ap()
    build(nc, a, out)
    return run_bass_kernel_spmd(nc, [arrays], core_ids=[0]).results[0]["out_x"]
```

```python
from contextlib import ExitStack

import numpy as np

import concourse.bass as bass
from concourse import mybir

F32 = mybir.dt.float32
F32R = mybir.dt.float32r
I32 = mybir.dt.int32
ALU = mybir.AluOpType
ACT = mybir.ActivationFunctionType
AXX = mybir.AxisListType.X
MUL, ADD, SUB, MAX, MIN = ALU.mult, ALU.add, ALU.subtract, ALU.max, ALU.min

P = 128
TOK = 256
NT = TOK // P
D = 1024
KD = D // P
DEPTH = 2
D_FF = 2816
HEADS = 4
HD = 128
MLP = 4096
EPS = 1e-6
SLAB = 2048
NSLOT = 5
LEVELS = (1, 2, 4, 8, 16, 32, 64)


class Queue:

    def __init__(self, sem):
        self.sem, self.count, self.steps, self.seen = sem, 0, [], {}

    def wait(self, marks):
        for sem, value in marks:
            if self.seen.get(sem.name, 0) < value:
                self.seen[sem.name] = value
                self.steps.append(lambda e, s=sem, v=value: e.wait_ge(s, v))

    def do(self, after, *instructions):
        self.wait(after)
        self.steps += [lambda e, f=f: f() for f in instructions[:-1]]
        self.steps.append(lambda e, f=instructions[-1]: f().then_inc(self.sem, 1))
        self.count += 1
        return (self.sem, self.count)

    def last(self):
        return [(self.sem, self.count)] if self.count else []

    def dma(self, after, sem, total, dst, src):
        self.wait(after)
        self.steps.append(lambda e: e.dma_start(dst, src).then_inc(sem, 16))
        return (sem, total)

    def play(self, engine):
        for s in self.steps:
            s(engine)


def shape_constants():
    i = np.arange(P)[:, None]
    j = np.arange(P)[None, :]
    f = lambda a: np.asarray(a, np.float32)
    parts = {"ident": f(i == j), "upto": f(i <= j), "from": f(i >= j), "before": f(i < j)}
    parts["ones"] = np.ones((P, P), np.float32)
    for name in ("fwd", "bwd"):
        masks = []
        for b in LEVELS:
            m = (i // (2 * b) == j // (2 * b)) & (i % (2 * b) >= b) & (j % (2 * b) < b)
            masks.append(f(m if name == "fwd" else m.T))
        parts[name] = np.concatenate(masks, 1)
    n = np.arange(TOK)[None, None, :]
    m = np.arange(NT)[None, :, None] * P + np.arange(P)[:, None, None]
    parts["ahead"] = f(np.maximum(n - m, 0)).reshape(P, -1)
    parts["behind"] = f(np.maximum(m - n, 0)).reshape(P, -1)
    parts["rotate"] = f(i == j - 64) - f(i == j + 64)
    parts["flip"] = f(i + j == P - 1)
    parts["half"] = f(i // 64 == j // 64)
    parts["resets"] = np.broadcast_to(f(np.arange(TOK) % 64 != 0), (P, TOK))
    parts["headcol"] = f(i // 64 == np.arange(2)[None, :])
    inv = np.float32(10000.0) ** (-np.arange(0, HD, 2, dtype=np.float32) / np.float32(HD))
    parts["freq"] = f(np.concatenate([inv, inv])[:, None])
    barred = np.zeros((P, 64), np.float32)
    barred[:64] = -1e30
    parts["barred"] = barred
    at, where = 0, {}
    for k, v in parts.items():
        where[k] = (at, at + v.shape[1])
        at += v.shape[1]
    return np.ascontiguousarray(np.concatenate(list(parts.values()), 1)), where


def build(nc, a, out, dbg=None):
    _, const_at = shape_constants()
    with ExitStack() as ctx:
        def sb(name, shape, dt=F32):
            return ctx.enter_context(nc.sbuf_tensor(name, shape, dt))

        def sem(name):
            return ctx.enter_context(nc.semaphore(name))

        pe, dve, act, pool, sp = (Queue(sem(f"{n}_steps")) for n in ("pe", "dve", "act", "pool", "sp"))
        V, S, G, T = nc.vector, nc.scalar, nc.gpsimd, nc.tensor

        psum = ctx.enter_context(nc.psum_tensor("psum", [P, 8, 512], F32))
        ring = sb("weight_ring", [P, NSLOT, SLAB])
        slot_landed = [sem(f"slab_landed{s}") for s in range(NSLOT)]
        slot_loads = [0] * NSLOT
        slot_free = [[] for _ in range(NSLOT)]
        x = sb("x", [P, NT, D])
        xnT = sb("xnT", [P, KD, TOK])
        memkT = sb("memkT", [P, KD, TOK])
        memv = sb("memv", [P, NT, D])
        mixT = xnT
        consts = sb("consts", [P, max(e for _, e in const_at.values())])
        gains = sb("gains", [P, 96])
        taps = sb("taps", [P, 120])
        vecs = sb("vecs", [P, 48])
        post_w = sb("post_w", [P, 1, D])
        cosT = sb("cosT", [P, TOK])
        sinT = sb("sinT", [P, TOK])
        ssq = sb("ssq", [P, 4])
        sp_l = sb("softplus_lambda", [P, 2])[:, :]
        lt, lb = sb("lambda_steps", [P, 6]), sb("forget_floor", [P, 8])
        lt, lb = (v[:, :].rearrange("p (a b) -> p a b", b=2) for v in (lt, lb))
        inv_rms = sb("inv_rms", [P, 4])
        softmax_s = sb("softmax_s", [P, 16])
        minus_half = sb("minus_half", [P, 16])
        ARENA = 27648
        arena_base = (nc.sbuf_usable_end - 4 * ARENA) // 32 * 32
        arena = nc.alloc_sbuf_tensor_at("arena", [P, ARENA], F32, offset=arena_base)
        NHL = 4
        w_hl = nc.alloc_sbuf_tensor_at("w_hi_lo", [P, NHL, 2, SLAB], F32R, offset=arena_base + 4 * (ARENA - 4096 * NHL))
        x_hl = nc.alloc_sbuf_tensor_at("x_hi_lo", [P, 2, KD, TOK], F32R, offset=arena_base + 4 * (ARENA - 4096 * NHL - 4096))
        NH = 3
        h_hl = nc.alloc_sbuf_tensor_at("h_hi_lo", [P, NH, 2, 2, TOK], F32R, offset=arena_base + 4 * (ARENA - 4096 * NHL - 4096 - 1024 * NH))
        hl_free = [[] for _ in range(NHL)]
        stage_scratch = arena[:, 0:NT * D].rearrange("p (t n) -> p t n", t=NT)
        arena_at, keep_tail = [0], [False]
        tail_2k = arena[:, ARENA - 2048:ARENA]
        memT = tail_2k.rearrange("p (k t) -> p k t", k=KD)

        def carve(*shape):
            n = int(np.prod(shape))
            assert arena_at[0] + n <= ARENA, (arena_at, n)
            v = arena[:, arena_at[0]:arena_at[0] + n]
            arena_at[0] += n
            assert arena_at[0] <= ARENA - (2048 if keep_tail[0] else 0), arena_at
            names = "abcd"[:len(shape)]
            if len(shape) == 1:
                return v
            return v.rearrange(f"p ({' '.join(names)}) -> p {' '.join(names)}",
                               **{names[k]: shape[k] for k in range(1, len(shape))})

        def C(name):
            lo, hi = const_at[name]
            return consts[:, lo:hi]

        ident = C("ident")

        x_marks = [[], []]

        def everything():
            return pe.last() + dve.last() + act.last() + pool.last()

        def stage_start(held):
            for q in (pe, dve, act, pool):
                q.wait(held)
            arena_at[0] = 0

        def V_(after, *f):
            return dve.do(after, *f)

        load_sems = {}

        def load(dst, src, after=(), group="setup"):
            if group not in load_sems:
                load_sems[group] = [sem(f"{group}_landed"), 0]
            g = load_sems[group]
            g[1] += 16
            return sp.dma(after, g[0], g[1], dst, src)

        bank_free = [[] for _ in range(8)]
        turn = [0]

        def take(banks=(4, 5, 6, 7)):
            b = banks[turn[0] % len(banks)]
            turn[0] += 1
            return b, bank_free[b]

        slab_no = [0]

        def slab(src, rows, cols):
            s = slab_no[0] % NSLOT
            slab_no[0] += 1
            slot_loads[s] += 16
            view = ring[:, s, 0:rows * cols].rearrange("p (k n) -> p k n", n=cols)
            mark = sp.dma(slot_free[s], slot_landed[s], slot_loads[s], view, src)
            return s, view, mark

        def columns(w, c0, n=256):
            return w[:, c0:c0 + n].rearrange("(k p) n -> p k n", p=P), w.shape[0] // P, n

        def rows(w, r0, n=2):
            return w[r0 * P:(r0 + n) * P, :].rearrange("(k p) n -> p k n", p=P), n, w.shape[1]

        def mm(o, l, r, start=True, stop=True):
            return lambda: T.matmul(o, l, r, start=start, stop=stop)

        def tr(o, i):
            k = i.partition_size()
            b = i.base_partition()
            return lambda: T.transpose(o, i, ident[b:b + k, 0:k])

        def project_T(w, c0, srcT, after, banks=(4, 5, 6, 7)):
            s, wv, landed = slab(*columns(w, c0))
            b, free = take(banks)
            ops = [mm(psum[:, b, 256 * j:256 * j + 256], wv[:, k, P * j:P * j + P], srcT[:, k, :],
                      k == 0, k == KD - 1) for j in range(2) for k in range(KD)]
            m = pe.do([landed] + free + after, *ops)
            slot_free[s] = [m]
            return b, psum[:, b, :].rearrange("p (j t) -> p j t", j=2), m

        def project_N(w, c0, srcT, after, n=256, banks=(4, 5, 6, 7)):
            s, wv, landed = slab(*columns(w, c0, n))
            b, free = take(banks)
            ops = [mm(psum[:, b, n * t:n * t + n], srcT[:, k, P * t:P * t + P], wv[:, k, :],
                      k == 0, k == KD - 1) for t in range(NT) for k in range(KD)]
            m = pe.do([landed] + free + after, *ops)
            slot_free[s] = [m]
            return b, psum[:, b, 0:2 * n].rearrange("p (t n) -> p t n", t=2), m

        def project_out(w, srcT, after):
            slabs = [slab(*rows(w, r0)) for r0 in range(0, KD, 2)]
            free = [m for b in range(4) for m in bank_free[b]]
            done = {}
            for i, t in ((0, 0), (0, 1), (1, 0), (1, 1), (2, 0), (3, 0), (2, 1), (3, 1)):
                s, wv, landed = slabs[i]
                done[i, t] = pe.do([landed] + free + after,
                                   *[mm(psum[:, 2 * t + n, :], srcT[:, 2 * i + j, P * t:P * t + P], wv[:, j, 512 * n:512 * n + 512],
                                        i + j == 0, 2 * i + j == KD - 1) for j in range(2) for n in range(2)])
                slot_free[s] = [done[i, t]]
            return [done[3, t] for t in range(NT)]

        def split(src, hi, lo, after):
            mh = act.do(after, lambda: S.copy(hi, src))
            return V_([mh], lambda: V.tensor_tensor(lo, src, hi.bitcast(F32), SUB))

        cuts = [0]

        class SplitStream:

            def __init__(self, sources, following=None):
                self.sources, self.cut, self.used, self.following = sources, [], 0, following
                self.loaded = []

            def load(self, n):
                self.loaded = [slab(*source) for source in self.sources[:n]]

            def ahead(self, n):
                while len(self.cut) < min(self.used + n, len(self.sources)):
                    n_cut = len(self.cut)
                    s, view, landed = self.loaded[n_cut] if n_cut < len(self.loaded) else slab(*self.sources[n_cut])
                    k = cuts[0] % NHL
                    cuts[0] += 1
                    m = split(ring[:, s, :], w_hl[:, k, 0, :], w_hl[:, k, 1, :], [landed] + hl_free[k])
                    slot_free[s] = [m]
                    n_cols = self.sources[len(self.cut)][2]
                    self.cut.append((k, [w_hl[:, k, i, :].rearrange("p (k n) -> p k n", n=n_cols) for i in range(2)], m))
                over = self.used + n - len(self.sources)
                if over > 0 and self.following:
                    self.following.ahead(over)

            def next(self):
                self.used += 1
                return self.cut[self.used - 1]

        def three(o, l, r, start, stop):
            return [mm(o, l[0], r[0], start, False), mm(o, l[0], r[1], False, False), mm(o, l[1], r[0], False, stop)]

        def split_project_T(stream, after):
            k_, w, m = stream.next()
            b, free = take()
            ops = [op for j in range(2) for k in range(KD) for op in
                   three(psum[:, b, 256 * j:256 * j + 256], [w[i][:, k, P * j:P * j + P] for i in range(2)],
                         [x_hl[:, i, k, :] for i in range(2)], k == 0, k == KD - 1)]
            pe.do([m] + free + after[0], *ops[:3 * KD // 2])
            m = pe.do(after[1], *ops[3 * KD // 2:])
            hl_free[k_] = [m]
            return b, psum[:, b, :].rearrange("p (j t) -> p j t", j=2), m

        def out_products(w, lhs, t, n, first, last):
            return [op for j in range(2) for op in
                    three(psum[:, 2 * t + n, :], [lhs(i, j)[:, P * t:P * t + P] for i in range(2)],
                          [w[i][:, j, 512 * n:512 * n + 512] for i in range(2)], first and j == 0, last and j == 1)]

        def split_out(stream, lhs, first, after):
            k_, w, m = stream.next()
            free = [m_ for b in range(4) for m_ in bank_free[b]] if first else []
            m = pe.do([m] + free + after, *[op for t in range(NT) for n in range(2) for op in out_products(w, lhs, t, n, first, False)])
            hl_free[k_] = [m]
            return m

        def split_out_last(stream, lhs, after):
            (ka, wa, ma), (kb, wb, mb) = stream.next(), stream.next()
            a_, b_ = (lambda t, n: out_products(wa, lhs[0], t, n, False, False)), (lambda t, n: out_products(wb, lhs[1], t, n, False, True))
            pe.do([ma] + after[0], *(a_(0, 0) + a_(0, 1) + a_(1, 0)))
            done0 = pe.do([mb] + after[1], *(b_(0, 0) + b_(0, 1)))
            hl_free[ka] = [pe.do([], *a_(1, 1))]
            done1 = pe.do([], *(b_(1, 0) + b_(1, 1)))
            hl_free[kb] = [done1]
            return [done0, done1]

        staging = carve(P)
        load(x[:, :, :], a["x"][0].rearrange("(t p) d -> p t d", p=P), group="first")
        load(consts[:, 0:P], a["consts"][:, 0:P], group="first")
        flat_rows = lambda v: v.rearrange("a b c -> (a b c)" if len(v.shape) == 3 else "a b -> (a b)").rearrange("(r c) -> r c", c=P)
        r = 0
        for name in ("norm_pre", "mem_norm", "norm_mix_pre_2", "norm_mlp_pre_2"):
            v = flat_rows(a[name])
            first = load(staging[r:r + v.shape[0], :], v, group="first")
            r += v.shape[0]
        half_set = pool.do([], lambda: G.memset(minus_half[:, :], -0.5))
        t0 = pe.do([first], tr(psum[:, 4, 0:96], staging[0:96, :]))
        gains_set = V_([t0], lambda: V.tensor_copy(gains[:, :], psum[:, 4, 0:96]))
        bank_free[4] = [gains_set]
        for q in (pe, act, pool, dve):
            q.wait([first, gains_set, half_set])

        vec_at = {}
        posi = sb("posi", [P, TOK], I32)
        lg, alog, dtb = sb("lg", [P, 16]), sb("alog", [P, 16]), sb("dtb", [P, 16])
        gnw, hgn = sb("gnw", [P, 2 * P]), sb("hgn", [P, 256])
        late_staging = memv[:, 0, 0:256].rearrange("p (a b) -> p a b", a=2)

        def late_loads():
            load(consts[:, P:], a["consts"][:, P:])
            load(late_staging[0:120, 0, :], a["gdn_conv"].rearrange("l j (r c) -> (l j r) c", c=P))
            r = 0
            for name in ("rwkv_mu_2", "rwkv_w0_2", "rwkv_a0_2", "rwkv_k_k_2", "rwkv_k_a_2", "rwkv_r_k_2",
                         "rwkv_ln_w_2", "rwkv_ln_b_2", "lru_conv_w_2", "lru_conv_b_2", "lru_ba_2",
                         "lru_bx_2", "lru_lambda_2", "hgrn_lb_logits_2"):
                v = flat_rows(a[name])
                load(late_staging[r:r + v.shape[0], 1, :], v)
                vec_at[name] = r
                r += v.shape[0]
            vec_at["end"] = r
            load(posi[:, :], a["positions"].partition_broadcast(P))
            for dst, name in ((lg, "ret_log_gamma"), (alog, "gdn_a_log"), (dtb, "gdn_dt_bias")):
                load(dst[:, :], a[name].rearrange("l d h -> (l d h)").partition_broadcast(P))
            load(gnw[:, :], a["gdn_norm"].rearrange("l d -> (l d)").partition_broadcast(P))
            return load(hgn[:, :], a["hgrn_norm_2"].rearrange("l d -> (l d)").partition_broadcast(P))

        def late_setup(landed):
            for q in (pe, dve, act, pool):
                q.wait([landed])
            n = vec_at["end"]
            b, free = take()
            t0 = pe.do(free, tr(psum[:, b, 0:120], late_staging[0:120, 0, :]), tr(psum[:, b, 256:256 + n], late_staging[0:n, 1, :]))
            m = V_([t0], lambda: V.tensor_copy(taps[:, :], psum[:, b, 0:120]),
                   lambda: V.tensor_copy(vecs[:, 0:n], psum[:, b, 256:256 + n]))
            bank_free[b] = [m]
            for q in (dve, act):
                q.wait([m])
            yield
            yield from rotary_tables()
            yield from recurrent_constants()

        def vec(name, k=0):
            c = vec_at[name] + k
            return vecs[:, c:c + 1]

        def inverse_root(dst, src, after, scale, eps=EPS, gain=1.0):
            p, n = dst.shape
            m = V_(after, lambda: V.tensor_scalar(dst, src, scale / gain ** 2, eps / gain ** 2, MUL, ADD))
            return pool.do([m], lambda: G.tensor_tensor(dst, dst, minus_half[0:p, 0:n], ALU.pow))

        def normed_rows(src, scaled, t, after):
            m = act.do(after, lambda: S.activation(scaled[:, t, :], src[:, t, :], ACT.Square, accum_out=ssq[:, t:t + 1]))
            root = inverse_root(inv_rms[:, t:t + 1], ssq[:, t:t + 1], [m], 1.0 / D)
            return root

        def normed_columns(src, scaled, dstT, gain_at, t, root, split_too, banks, held):
            marks = []
            for g in range(2):
                half = slice(512 * g, 512 * g + 512)
                m = act.do([root], lambda half=half: S.mul(scaled[:, t, half], src[:, t, half], inv_rms[:, t:t + 1]))
                b, free = take(banks)
                mt = pe.do([m] + free, *[tr(psum[:, b, P * j:P * j + P],
                                            scaled[:, t, P * (4 * g + j):P * (4 * g + j + 1)]) for j in range(4)])
                c = gain_at + 4 * g
                piece = dstT[:, 4 * g:4 * g + 4, P * t:P * t + P]
                mv = V_([mt] + held, lambda b=b, piece=piece, c=c: V.tensor_tensor(
                    piece, psum[:, b, :].rearrange("p (j n) -> p j n", j=4),
                    gains[:, c:c + 4].unsqueeze(2).to_broadcast([P, 4, P]), MUL))
                bank_free[b] = [mv]
                marks.append((g, piece, mv))
            ready = []
            for g, piece, mv in marks:
                if split_too:
                    hi, lo = (x_hl[:, i, 4 * g:4 * g + 4, P * t:P * t + P] for i in range(2))
                    mh = act.do([mv] + held, lambda hi=hi, piece=piece: S.copy(hi, piece))
                    mv = V_([mh], lambda hi=hi, lo=lo, piece=piece: V.tensor_tensor(lo, piece, hi.bitcast(F32), SUB))
                ready.append(mv)
            return ready

        def norm_T(src, dstT, gain_at, scaled, after, split_too=False, banks=(4, 5, 6, 7)):
            roots = [normed_rows(src, scaled, t, after[t]) for t in range(NT)]
            ready = [normed_columns(src, scaled, dstT, gain_at, t, roots[t], split_too, banks, []) for t in range(NT)]
            return [ready[0][0], ready[1][0]], [ready[0][1], ready[1][1]]

        def recurrent_constants():
            lam = vecs[:, vec_at["lru_lambda_2"]:vec_at["lru_lambda_2"] + 2]
            e_, z_, q_ = lt[:, 0], lt[:, 1], lt[:, 2]
            ml = act.do([], lambda: S.activation(e_, lam, ACT.Abs))
            ml = act.do([ml], lambda: S.activation(e_, e_, ACT.Exp, scale=-1.0))
            ml = V_([ml], lambda: V.tensor_scalar(z_, e_, 2.0, None, ADD))
            ml = V_([ml], lambda: V.reciprocal(z_, z_))
            ml = V_([ml], lambda: V.tensor_tensor(z_, z_, e_, MUL))
            ml = V_([ml], lambda: V.tensor_tensor(q_, z_, z_, MUL))
            yield
            ml = V_([ml], lambda: V.tensor_scalar(e_, q_, 1.0 / 17, 1.0 / 15, MUL, ADD))
            for n in (13, 11, 9, 7, 5, 3, 1):
                ml = V_([ml], lambda: V.tensor_tensor(e_, e_, q_, MUL))
                ml = V_([ml], lambda n=n: V.tensor_scalar(e_, e_, 1.0 / n, None, ADD))
                if n in (11, 7, 3):
                    yield
            ml = V_([ml], lambda: V.tensor_tensor(z_, z_, e_, MUL))
            ml = V_([ml], lambda: V.tensor_scalar(q_, lam, -1.0, 0.0, MUL, MAX))
            ml = V_([ml], lambda: V.scalar_tensor_tensor(sp_l, z_, 2.0, q_, MUL, ADD))
            yield
            lgt = vecs[:, vec_at["hgrn_lb_logits_2"]:vec_at["hgrn_lb_logits_2"] + 2]
            m = V_([], lambda: V.tensor_tensor(lb[:, 0], lgt, lgt, SUB))
            m = act.do([m], lambda: S.activation(lb[:, 0], lb[:, 0], ACT.Exp))
            m = V_([m], lambda: V.reciprocal(lb[:, 1], lb[:, 0]))
            m = V_([m], lambda: V.tensor_tensor(lb[:, 0], lb[:, 0], lb[:, 1], MUL))
            m = V_([m], lambda: V.tensor_tensor(lb[:, 2], lb[:, 0], lb[:, 0], SUB))
            m = V_([m], lambda: V.tensor_scalar(lb[:, 2], lb[:, 2], 0.0, None, MAX))
            ml = V_([m], lambda: V.tensor_scalar(lb[:, 3], lb[:, 2], -1.0, 1.0, MUL, ADD))

        def rotary_tables():
            ang, turns, red = (memkT[:, k, :] for k in range(3))
            TWO_PI = (6.28125, 0.0019350051879882812, float(2 * np.pi - 6.28125 - 0.0019350051879882812))
            MAGIC = 12582912.0
            m = V_([], lambda: V.tensor_copy(ang, posi[:, :]))
            m = V_([m], lambda: V.tensor_scalar(ang, ang, C("freq"), None, MUL))
            yield
            for table, shift in ((sinT, 0.0), (cosT, 0.25)):
                m = V_([m], lambda s=shift: V.tensor_scalar(turns, ang, float(1 / (2 * np.pi)), s, MUL, ADD))
                m = V_([m], lambda: V.tensor_scalar(turns, turns, MAGIC, MAGIC, ADD, SUB))
                yield
                m = V_([m] + act.last(), lambda: V.scalar_tensor_tensor(red, turns, -TWO_PI[0], ang, MUL, ADD))
                m = V_([m], lambda: V.scalar_tensor_tensor(red, turns, -TWO_PI[1], red, MUL, ADD))
                m = V_([m], lambda: V.scalar_tensor_tensor(red, turns, -TWO_PI[2], red, MUL, ADD))
                m = V_([m], lambda s=shift: V.tensor_scalar(red, red, float(2 * np.pi * s), 3.1415925, ADD, MIN))
                m = V_([m], lambda: V.tensor_scalar(red, red, -3.1415925, None, MAX))
                act.do([m], lambda tb=table: S.activation(tb[:, :], red, ACT.Sin))
                yield


        def load_post(src, k):
            return load(post_w[:, k, :], src.partition_broadcast(P), x_marks[0] + x_marks[1], group="post_gain")

        normed = [None]

        def residual(done, wmark, half, following_norm, held=()):
            held = list(held)
            h = [psum[:, 2 * t:2 * t + 2, :] for t in range(NT)]
            sc = [stage_scratch[:, t, :].rearrange("p (n c) -> p n c", n=2) for t in range(NT)]
            w = post_w[:, 0, :].rearrange("p (n c) -> p n c", n=2)
            roots = []

            def length(t):
                m = act.do([done[t]] + held, lambda: S.activation(sc[t], h[t], ACT.Square, accum_out=ssq[:, t:t + 1]))
                return inverse_root(inv_rms[:, t:t + 1], ssq[:, t:t + 1], [m], 1.0 / D, gain=half)

            def add(t, root):
                ma = V_([root, wmark], lambda: V.scalar_tensor_tensor(sc[t][:, 0], h[t][:, 0], inv_rms[:, t:t + 1], w[:, 0], MUL, MUL))
                mp = pool.do([ma], lambda: G.tensor_tensor(x[:, t, 0:512], x[:, t, 0:512], stage_scratch[:, t, 0:512], ADD))
                mb = V_([], lambda: V.scalar_tensor_tensor(sc[t][:, 1], h[t][:, 1], inv_rms[:, t:t + 1], w[:, 1], MUL, MUL))
                bank_free[2 * t] = bank_free[2 * t + 1] = [mb]
                mv = V_([mb], lambda: V.tensor_tensor(x[:, t, 512:], x[:, t, 512:], stage_scratch[:, t, 512:], ADD))
                x_marks[t] = [mp, mv]

            add(0, length(0))
            if following_norm is None:
                add(1, length(1))
                return
            gain_at, split_too = following_norm
            columns_of = lambda t, root: normed_columns(x, stage_scratch, xnT, gain_at, t, root, split_too, (4, 5, 6, 7), held)
            root = normed_rows(x, stage_scratch, 0, x_marks[0])
            later = length(1)
            add(1, later)
            first = columns_of(0, root)
            second = columns_of(1, normed_rows(x, stage_scratch, 1, x_marks[1]))
            normed[0] = ([first[0], second[0]], [first[1], second[1]])

        def dump(name, tile, marks):
            if dbg and name in dbg:
                load(dbg[name], tile, marks + dve.last() + act.last() + pool.last() + pe.last(), group="dump")

        def ffn_sources(wg, wu, wd):
            sources = []
            for i in range(D_FF // 256 + 1):
                if i < D_FF // 256:
                    sources += [columns(wg, 256 * i), columns(wu, 256 * i)]
                if i:
                    sources.append(rows(wd, 2 * (i - 1)))
            return sources

        held = []

        def ffn(stream, post_src, following_norm, aside=iter(())):
            stage_start(held)
            stream.ahead(4)
            scaled = carve(NT, D)
            silu, h32 = carve(2, TOK), carve(2, TOK)
            n_groups = D_FF // 256
            ready = normed[0]
            h_ready, h_read, h32_read = [None] * n_groups, [[] for _ in range(NH)], [[], []]
            half_of = lambda g: (lambda h, j: h_hl[:, g % NH, h, j, :])
            for i in range(n_groups):
                kg, gv, gland = stream.next()
                ku, uv, uland = stream.next()
                evac = []
                for j in range(2):
                    b, free = take()
                    ops = [op for o, wv in ((0, gv), (1, uv)) for k in range(KD) for op in
                           three(psum[:, b, 256 * o:256 * o + 256], [wv[h][:, k, P * j:P * j + P] for h in range(2)],
                                 [x_hl[:, h, k, :] for h in range(2)], k == 0, k == KD - 1)]
                    if i + j == 0:
                        pe.do([gland] + free + ready[0], *ops[:3 * KD // 2])
                        pe.do(ready[1], *ops[3 * KD // 2:3 * KD])
                        ops = ops[3 * KD:]
                    m = pe.do([gland, uland] + free, *ops)
                    evac.append((b, m))
                hl_free[kg] = hl_free[ku] = [m]
                for j, (b, m) in enumerate(evac):
                    ma = act.do([m] + h32_read[j], lambda b=b, j=j: S.activation(silu[:, j, :], psum[:, b, 0:256], ACT.Silu))
                    mv = V_([ma] + h32_read[j], lambda b=b, j=j: V.tensor_tensor(h32[:, j, :], silu[:, j, :], psum[:, b, 256:512], MUL))
                    bank_free[b] = [mv]
                    h_ready[i] = split(h32[:, j, :], h_hl[:, i % NH, 0, j, :], h_hl[:, i % NH, 1, j, :], [mv] + h_read[i % NH])
                    h32_read[j] = [h_ready[i]]
                stream.ahead(3)
                if i > 2:
                    next(aside, None)
                    next(aside, None)
                if i == 0:
                    wmark = load_post(post_src, 0)
                elif i < n_groups - 1:
                    g = i - 1
                    h_read[g % NH] = [split_out(stream, half_of(g), i == 1, [h_ready[g]])]
                    stream.ahead(4)
                else:
                    g = i - 1
                    done = split_out_last(stream, [half_of(g), half_of(i)], [[h_ready[g]], [h_ready[i]]])
                    stream.ahead(2)
            for _ in aside:
                pass
            held[:] = everything()
            residual(done, wmark, 0.5, following_norm)

        def inverses(systems, size, per, masks, levels, fill, LM, W, taken, banks):
            p = size
            state = []
            for s, (L, X, XT, lm) in enumerate(systems):
                state.append(dict(L=L, X=X, XT=XT, lm=lm, x=[], xt=[], w_read=[]))
            lm_read = [list(taken) for _ in systems]
            eye = ident[0:p, 0:p].unsqueeze(1).to_broadcast([p, per, size])

            def bank():
                b, free = take(banks)
                return b, psum[0:p, b, 0:per * size].rearrange("p (h n) -> p h n", h=per), free

            for n in range(len(levels)):
                last = n == len(levels) - 1
                for s, st in enumerate(state):
                    mk = C(masks[s])[0:p, P * n:P * n + size].unsqueeze(1).to_broadcast([p, per, size])
                    lmm = pool.do(st["lm"] + lm_read[s], lambda s=s, st=st, mk=mk: G.tensor_tensor(
                        LM[0:p, s], st["L"], mk, MUL))
                    b, bv, free = bank()
                    if n == 0:
                        m = pe.do([lmm] + free, *[mm(bv[:, h, :], LM[0:p, s, h, :], ident[0:p, 0:p]) for h in range(per)])
                        st["x"] = [V_([lmm], lambda s=s, st=st: V.tensor_tensor(st["X"], eye, LM[0:p, s], SUB))]
                        st["xt"] = [V_([m], lambda st=st, bv=bv: V.tensor_tensor(st["XT"], eye, bv, SUB))]
                        bank_free[b] = st["xt"]
                        lm_read[s] = st["x"] + [m]
                        continue
                    m = pe.do([lmm] + free + st["xt"], *[mm(bv[:, h, :], LM[0:p, s, h, :], st["XT"][:, h, :])
                                                        for h in range(per)])
                    lm_read[s] = [m]
                    st["w"] = act.do([m] + st["w_read"], lambda s=s, bv=bv: S.copy(W[0:p, s], bv))
                    bank_free[b] = [st["w"]]
                fill()
                if n == 0:
                    continue
                for s, st in enumerate(state):
                    b2, b2v, free2 = bank()
                    m2 = pe.do([st["w"]] + free2 + st["x"], *[mm(b2v[:, h, :], st["X"][:, h, :], W[0:p, s, h, :]) for h in range(per)])
                    st["w_read"] = [m2]
                    if not last:
                        b1, b1v, free1 = bank()
                        m1 = pe.do(free1, *[mm(b1v[:, h, :], W[0:p, s, h, :], st["X"][:, h, :]) for h in range(per)])
                        st["w_read"] = [m1]
                    st["xt"] = [V_([m2], lambda st=st, b2v=b2v: V.tensor_tensor(st["XT"], st["XT"], b2v, SUB))]
                    bank_free[b2] = st["xt"]
                    if not last:
                        st["x"] = [V_([m1], lambda st=st, b1v=b1v: V.tensor_tensor(st["X"], st["X"], b1v, SUB))]
                        bank_free[b1] = st["x"]
                fill()
            return [st["xt"] for st in state]

        def softplus(dst, src, scratch, after):
            m = act.do(after, lambda: S.activation(scratch, src, ACT.Abs))
            m = act.do([m], lambda: S.activation(scratch, scratch, ACT.Exp, scale=-1.0))
            m = act.do([m], lambda: S.activation(scratch, scratch, ACT.Ln, bias=1.0))
            return V_([m], lambda: V.scalar_tensor_tensor(dst, src, 0.0, scratch, MAX, ADD))

        WORK8 = tuple(range(8))

        def mixer(l, following):
            stage_start(held)
            w = a["w_in"][l]
            W = 512
            BANKS = (2, 3, 4, 5, 6, 7)
            mix = carve(NT, D)
            ready = normed[0][0] + normed[0][1]
            colN = lambda c0, n=256: project_N(w, c0, xnT, ready, n, banks=BANKS)
            colT = lambda c0: project_T(w, c0, xnT, ready, banks=BANKS)

            ab = carve(NT, 16)
            g_a, sp_s, g, beta, ea = carve(NT, 8), carve(NT, 8), carve(NT, 8), carve(NT, 8), carve(8)
            b, pv, m = colN(8 * W, 16)
            m = V_([m], lambda pv=pv: V.tensor_copy(ab, pv))
            bank_free[b] = [m]
            mb = act.do([m], lambda: S.activation(beta, ab[:, :, 8:16], ACT.Sigmoid))
            mea = act.do([], lambda: S.activation(ea, alog[:, 8 * l:8 * l + 8], ACT.Exp))
            m = V_([m], lambda: V.tensor_tensor(g_a, ab[:, :, 0:8], dtb[:, 8 * l:8 * l + 8].unsqueeze(1).to_broadcast([P, NT, 8]), ADD))
            m = softplus(g, g_a, sp_s, [m])
            gm = V_([m, mea], lambda: V.scalar_tensor_tensor(g, g, -1.0, ea.unsqueeze(1).to_broadcast([P, NT, 8]), MUL, MUL))

            mload = load(memv[:, :, :], a["mem"][0].rearrange("(t p) d -> p t d", p=P), held, group="memory")
            wmark = load_post(a["norm_post"][l, 1], 0)

            raw = carve(12, TOK + 4)
            qkv = carve(12, TOK)
            zero = pool.do([], lambda: G.memset(raw[:, :, 0:2], 0.0), lambda: G.memset(raw[:, :, TOK + 2:TOK + 4], 0.0))
            silu_done = []
            for i in range(6):
                b, pv, m = colT(4 * W + 256 * i)
                m = act.do([m, zero], lambda i=i, pv=pv: S.copy(raw[:, 2 * i:2 * i + 2, 2:TOK + 2], pv))
                bank_free[b] = [m]
                tap = lambda j, c: taps[:, 60 * l + 12 * j + c:60 * l + 12 * j + c + 1]
                pair = (2 * i, 2 * i + 1)
                mc = [V_([m, zero], lambda c=c, tap=tap: V.tensor_scalar(qkv[:, c, :], raw[:, c, 0:TOK], tap(0, c), None, MUL)) for c in pair]
                for j in range(1, 5):
                    mc = [V_([mc[c - 2 * i]], lambda c=c, j=j, tap=tap: V.scalar_tensor_tensor(
                        qkv[:, c, :], raw[:, c, j:j + TOK], tap(j, c), qkv[:, c, :], MUL, ADD)) for c in pair]
                mc = mc[1]
                if i == 1:
                    mem_s = memkT[:, :, :].rearrange("p (t k) n -> p t (k n)", t=NT)
                    mem_ready = norm_T(memv, memT, 64 + 8 * l, mem_s, [[mload], [mload]], banks=BANKS)
                    mem_ready = mem_ready[0] + mem_ready[1]
                silu_done.append(act.do([mc], lambda i=i: S.activation(qkv[:, 2 * i:2 * i + 2, :], qkv[:, 2 * i:2 * i + 2, :], ACT.Silu)))
            qT, kT, vT = qkv[:, 0:4, :], qkv[:, 4:8, :], qkv[:, 8:12, :]

            work_r = carve(2, 2, TOK)
            qk_done = [None] * 4
            nfree = [[], []]
            mem_jobs = []
            r_marks, dec_read, vbm = {}, [], []

            def keep(b, pv, m, dst, key, fn=None):
                if fn is None:
                    m = act.do([m] + dec_read + vbm, lambda: S.copy(dst, pv))
                else:
                    m = act.do([m], lambda: S.activation(dst, pv, fn))
                bank_free[b] = [m]
                r_marks[key] = m

            wk, wv_ = a["xattn_k"][l], a["xattn_v"][l]
            for i in range(4):
                mem_jobs.append(lambda i=i: keep(*project_T(wk, 256 * i, memT, mem_ready, BANKS), memkT[:, 2 * i:2 * i + 2, :], ("mk", i)))
                mem_jobs.append(lambda i=i: keep(*project_N(wv_, 256 * i, memT, mem_ready, banks=BANKS), memv[:, :, 256 * i:256 * i + 256], ("mv", i)))
            for i in range(4):
                sl = qkv[:, 2 * i:2 * i + 2, :]
                norm_s = work_r[:, i % 2]
                m = pool.do([silu_done[i]] + nfree[i % 2], lambda sl=sl, norm_s=norm_s: G.tensor_tensor(norm_s, sl, sl, MUL))
                b, free = take(BANKS)
                m = pe.do([m] + free, mm(psum[:, b, :], C("ones"), norm_s.rearrange("p a b -> p (a b)")))
                pv = psum[:, b, :].rearrange("p (a b) -> p a b", a=2)
                m = V_([m], lambda pv=pv, norm_s=norm_s: V.tensor_scalar(norm_s, pv, EPS, None, ADD))
                bank_free[b] = [m]
                m = act.do([m], lambda norm_s=norm_s: S.activation(norm_s, norm_s, ACT.Sqrt))
                m = V_([m], lambda norm_s=norm_s: V.reciprocal(norm_s, norm_s))
                sc = HD ** -0.5 if i < 2 else 1.0
                m = V_([m], lambda sl=sl, sc=sc, norm_s=norm_s: V.scalar_tensor_tensor(sl, sl, sc, norm_s, MUL, MUL))
                qk_done[i] = m
                nfree[i % 2] = [m]
                mem_jobs.pop(0)()

            kN, vN = carve(NT, HEADS, HD), carve(NT, HEADS, HD)
            kv_nat = []
            for src, dst, dep in ((kT, kN, qk_done[2:]), (vT, vN, silu_done[4:])):
                for t in range(NT):
                    b, free = take(BANKS)
                    m = pe.do(list(dep) + free, *[tr(psum[:, b, P * h:P * h + P], src[:, h, P * t:P * t + P]) for h in range(4)])
                    m = act.do([m], lambda dst=dst, t=t, b=b: S.copy(dst[:, t], psum[:, b, :].rearrange("p (h d) -> p h d", h=4)))
                    bank_free[b] = [m]
                    kv_nat.append(m)

            mem_jobs.pop(0)()
            combos = [(d, t) for d in range(2) for t in range(NT)]
            first = {0: 0, 1: 1}
            order = ("upto", "from")
            Gn, Gt = carve(4, 4), carve(4, 4)
            b, free = take(BANKS)
            ops = [mm(psum[:, b, 4 * c:4 * c + 4], C(order[d]), g[:, t, 4 * d:4 * d + 4]) for c, (d, t) in enumerate(combos)]
            ops += [mm(psum[:, b, 16 + 4 * c:20 + 4 * c], C("ones"), g[:, t, 4 * d:4 * d + 4]) for c, (d, t) in enumerate(combos)]
            m = pe.do([gm] + free, *ops)
            gn = V_([m], lambda b=b: V.tensor_copy(Gn, psum[:, b, 0:16].rearrange("p (c h) -> p c h", c=4)),
                    lambda b=b: V.tensor_copy(Gt, psum[:, b, 16:32].rearrange("p (c h) -> p c h", c=4)))
            bank_free[b] = [gn]
            tail, ebg = carve(4, 4), carve(4, 4)
            m = V_([gn], lambda: V.tensor_tensor(tail, Gt, Gn, SUB))
            mt_ = act.do([m], lambda: S.activation(tail, tail, ACT.Exp))
            m = act.do([gn], lambda: S.activation(ebg, Gn, ACT.Exp))
            me = V_([m, mb], *[lambda c=c, d=d, t=t: V.tensor_tensor(ebg[:, c], ebg[:, c], beta[:, t, 4 * d:4 * d + 4], MUL)
                               for c, (d, t) in enumerate(combos)])

            L, X, XT = carve(4, 4, P), carve(4, 4, P), carve(4, 4, P)
            QK = carve(4, 4, P)
            qg, vb, kbg, kt = carve(2, 4, P), carve(4, 4, P), carve(2, 4, P), carve(2, 4, P)
            dec = raw.rearrange("p a b -> p (a b)")[:, 0:1024].rearrange("p (a h n) -> p a h n", a=2, h=4)
            dec_read.append(silu_done[-1])
            lmarks, qkmarks, qgm, kbm, ktm = [], [], {}, {}, {}
            bc = lambda v: v.unsqueeze(2).to_broadcast([P, 4, P])
            for c, (d, t) in enumerate(combos):
                later = t != first[d]
                b, free = take(BANKS)
                bv = psum[:, b, :].rearrange("p (h n) -> p h n", h=4)
                m = pe.do([gm] + free, *[mm(bv[:, h, :], g[:, t, 4 * d + h:4 * d + h + 1].to_broadcast([P, P]), C(order[d])) for h in range(4)])
                m1 = V_([m, gn] + dec_read, *[lambda h=h, c=c, bv=bv: V.tensor_scalar(dec[:, 0, h, :], bv[:, h, :], Gn[:, c, h:h + 1], 0.0, SUB, MAX) for h in range(4)])
                m2 = V_([m1], *[lambda h=h, c=c, bv=bv: V.tensor_scalar(dec[:, 1, h, :], bv[:, h, :], Gn[:, c, h:h + 1], 0.0, SUB, MIN) for h in range(4)])
                fr = [m2]
                if later:
                    mq = act.do([m] + fr, lambda c=c, d=d, bv=bv: S.activation(qg[:, d], bv, ACT.Exp))
                    fr = fr + [mq]
                    qgm[d] = pool.do([mq] + qk_done[0:2], lambda d=d, t=t: G.tensor_tensor(qg[:, d], qg[:, d], qT[:, :, P * t:P * t + P], MUL))
                bank_free[b] = fr
                ma = act.do([m1], lambda: S.activation(dec[:, 0], dec[:, 0], ACT.Exp, scale=-1.0))
                mb2 = act.do([m2], lambda: S.activation(dec[:, 1], dec[:, 1], ACT.Exp))
                b1, free = take(BANKS)
                b1v = psum[:, b1, :].rearrange("p (h n) -> p h n", h=4)
                mk = pe.do(qk_done[2:] + free, *[mm(b1v[:, h, :], kT[:, h, P * t:P * t + P], kT[:, h, P * t:P * t + P]) for h in range(4)])
                ml = V_([mk, ma, mb], *[lambda h=h, c=c, d=d, t=t, b1v=b1v: V.scalar_tensor_tensor(
                    L[:, c, h, :], b1v[:, h, :], beta[:, t, 4 * d + h:4 * d + h + 1], dec[:, 0, h, :], MUL, MUL) for h in range(4)])
                bank_free[b1] = [ml]
                lmarks.append(ml)
                b2, free = take(BANKS)
                b2v = psum[:, b2, :].rearrange("p (h n) -> p h n", h=4)
                mk = pe.do(qk_done + free, *[mm(b2v[:, h, :], kT[:, h, P * t:P * t + P], qT[:, h, P * t:P * t + P]) for h in range(4)])
                mi = pool.do([mb2], lambda d=d: G.tensor_tensor(dec[:, 1], dec[:, 1], C(order[d]).unsqueeze(1).to_broadcast([P, 4, P]), MUL))
                mq = V_([mk, mi], lambda c=c, b2v=b2v: V.tensor_tensor(QK[:, c], b2v, dec[:, 1], MUL))
                bank_free[b2] = [mq]
                qkmarks.append(mq)
                dec_read[:] = [mq, ml]
                vbm.append(pool.do(kv_nat[2:] + [mb], lambda c=c, d=d, t=t: G.tensor_tensor(vb[:, c], vN[:, t], bc(beta[:, t, 4 * d:4 * d + 4]), MUL)))
                if later:
                    kbm[d] = pool.do(kv_nat[:2] + [me], lambda c=c, d=d, t=t: G.tensor_tensor(kbg[:, d], kN[:, t], bc(ebg[:, c]), MUL))
                else:
                    ktm[d] = pool.do(kv_nat[:2] + [mt_], lambda c=c, d=d, t=t: G.tensor_tensor(kt[:, d], kN[:, t], bc(tail[:, c]), MUL))
                if mem_jobs:
                    mem_jobs.pop(0)()

            qr = raw.rearrange("p a b -> p (a b)")[:, 0:2048].rearrange("p (a b) -> p a b", a=8)
            rv = vN.rearrange("p t h d -> p t (h d)")
            rg, z = (tail_2k[:, 1024 * k:1024 * k + 1024].rearrange("p (t n) -> p t n", t=NT) for k in range(2))
            pt_ring = [qkv[:, 8 + 2 * k:10 + 2 * k, :] for k in range(2)]
            decay = [work_r[:, k].rearrange("p a b -> p (a b)") for k in range(2)]
            ret_o = work_r.rearrange("p a b c -> p a (b c)")
            r4, sq_r = carve(4, 4), pt_ring[0].rearrange("p a (b n) -> p (a b) n", n=P)
            ret = {"decay": [[], []], "pt": [kv_nat, kv_nat], "o": [], "rt": {}}

            def rotary(i):
                src, rot_s = qr[:, 2 * i:2 * i + 2, :], pt_ring[i % 2]
                b, free = take(BANKS)
                pv = psum[:, b, :].rearrange("p (a b) -> p a b", a=2)
                m = pe.do([r_marks[("r", i)]] + free, mm(psum[:, b, :], C("rotate"), src.rearrange("p a b -> p (a b)")))
                ms = V_([m] + ret["pt"][i % 2], lambda: V.tensor_tensor(rot_s, pv, sinT[:, :].unsqueeze(1).to_broadcast([P, 2, TOK]), MUL))
                bank_free[b] = [ms]
                m = pool.do([m], lambda: G.tensor_tensor(src, src, cosT[:, :].unsqueeze(1).to_broadcast([P, 2, TOK]), MUL))
                ret["rt"][i] = V_([m, ms], lambda: V.tensor_tensor(src, src, rot_s, ADD))
                ret["pt"][i % 2] = [ret["rt"][i]]

            def retain(h):
                gf, gb = lg[:, 8 * l + h:8 * l + h + 1], lg[:, 8 * l + 4 + h:8 * l + 5 + h]
                dh, PT = decay[h % 2], pt_ring[h % 2].rearrange("p a b -> p (a b)")
                m = V_(ret["decay"][h % 2] + qk_done, lambda: V.tensor_scalar(dh, C("ahead"), gf, None, MUL))
                m = V_([m], lambda: V.scalar_tensor_tensor(dh, C("behind"), gb, dh, MUL, ADD))
                md = act.do([m], lambda: S.activation(dh, dh, ACT.Exp))
                b, free = take(BANKS)
                m = pe.do([ret["rt"][h // 2], ret["rt"][2 + h // 2]] + free,
                          *[mm(psum[:, b, 256 * j:256 * j + 256], qr[:, 4 + h, P * j:P * j + P], qr[:, h, :]) for j in range(2)])
                m = V_([m, md] + ret["pt"][h % 2], lambda: V.scalar_tensor_tensor(PT, psum[:, b, :], HD ** -0.5, dh, MUL, MUL))
                bank_free[b] = [m]
                ret["decay"][h % 2] = [m]
                if h == 0:
                    ret["o_free"] = bank_free[0] + bank_free[1]
                m = pe.do([m, r_marks[("v", 0)], r_marks[("v", 1)]] + ret["o_free"],
                          *[mm(psum[:, t, HD * h:HD * h + HD], PT[:, 256 * j + P * t:256 * j + P * t + P], rv[:, j, HD * h:HD * h + HD], j == 0, j == 1)
                            for t in range(NT) for j in range(2)])
                ret["pt"][h % 2] = [m]
                ret["o"].append(m)

            def retained(t):
                o = ret_o[:, t].rearrange("p (h n) -> p h n", h=4)
                bv = psum[:, t, :].rearrange("p (h n) -> p h n", h=4)
                mu, var = r4[:, 2, :], r4[:, 3, :]
                before = ret.get("ln", [])
                m = V_(ret["o"] + before, lambda: V.tensor_reduce(mu, bv, AXX, ADD))
                m = V_([m], lambda: V.tensor_scalar(mu, mu, 1.0 / HD, None, MUL))
                mc = V_([m] + ret["decay"][0] + ret["decay"][1], lambda: V.tensor_tensor(o, bv, bc(mu), SUB))
                bank_free[t] = [mc]
                ms = act.do([mc] + ret["pt"][0] + before, lambda: S.activation(sq_r, o, ACT.Square))
                mr = V_([ms], lambda: V.tensor_reduce(var, sq_r, AXX, ADD))
                mr = inverse_root(var, var, [mr], 1.0 / HD)
                m = V_([mr], lambda: V.tensor_tensor(o, o, bc(var), MUL))
                m = pool.do([m, r_marks[("g", 0)], r_marks[("g", 1)]], lambda: G.tensor_tensor(ret_o[:, t], ret_o[:, t], rg[:, t, :], MUL))
                ret["ln"] = [m]

            fills = [] + mem_jobs
            for i in range(4):
                fills.append(lambda i=i: keep(*colT(256 * i), qr[:, 2 * i:2 * i + 2, :], ("r", i)))
            for i in range(2):
                fills.append(lambda i=i: keep(*colN(2 * W + 256 * i), rv[:, :, 256 * i:256 * i + 256], ("v", i)))
                fills += [lambda i=i: rotary(2 * i), lambda i=i: rotary(2 * i + 1)]
            for i in range(2):
                fills.append(lambda i=i: keep(*colN(3 * W + 256 * i), rg[:, :, 256 * i:256 * i + 256], ("g", i), ACT.Silu))
                fills += [lambda i=i: retain(2 * i), lambda i=i: retain(2 * i + 1)]
            for i in range(2):
                fills.append(lambda i=i: keep(*colN(7 * W + 256 * i), z[:, :, 256 * i:256 * i + 256], ("z", i), ACT.Silu))
                fills.append(lambda i=i: retained(i))
            points = [2 * len(LEVELS) - 1]

            def fill():
                for _ in range(-(-len(fills) // max(points[0], 1))):
                    if fills:
                        fills.pop(0)()
                points[0] -= 1

            xts = inverses([(L[:, c], X[:, c], XT[:, c], [lmarks[c]]) for c in range(4)], P, 4,
                           ["fwd", "fwd", "bwd", "bwd"], LEVELS, fill,
                           mix.rearrange("p t (a h n) -> p (t a) h n", h=4, n=P),
                           qkv[:, 0:8, :].rearrange("p (c b) (h n) -> p c (b h) n", c=4, h=2),
                           qk_done + qkmarks + kv_nat + list(qgm.values()), BANKS)
            while fills:
                fills.pop(0)()

            u = L
            wT = X
            um, wm = [], {}
            for c, (d, t) in enumerate(combos):
                b, free = take(BANKS)
                bv = psum[:, b, :].rearrange("p (h n) -> p h n", h=4)
                m = pe.do(xts[c] + [vbm[c]] + free, *[mm(bv[:, h, :], XT[:, c, h, :], vb[:, c, h, :]) for h in range(4)])
                m = V_([m], lambda c=c, bv=bv: V.tensor_copy(u[:, c], bv))
                bank_free[b] = [m]
                um.append(m)
                if t != first[d]:
                    b, free = take(BANKS)
                    bv2 = psum[:, b, :].rearrange("p (h n) -> p h n", h=4)
                    m = pe.do(xts[c] + [kbm[d]] + free, *[mm(bv2[:, h, :], kbg[:, d, h, :], XT[:, c, h, :]) for h in range(4)])
                    m = act.do([m], lambda c=c, bv2=bv2: S.copy(wT[:, c], bv2))
                    bank_free[b] = [m]
                    wm[d] = m
            state = kN
            stm = {}
            for d in range(2):
                c1 = combos.index((d, first[d]))
                c2 = combos.index((d, 1 - first[d]))
                b, free = take(BANKS)
                bv = psum[:, b, :].rearrange("p (h n) -> p h n", h=4)
                m = pe.do([um[c1], ktm[d]] + free, *[mm(bv[:, h, :], kt[:, d, h, :], u[:, c1, h, :]) for h in range(4)])
                m = act.do([m] + list(kbm.values()) + list(ktm.values()), lambda d=d, bv=bv: S.copy(state[:, d], bv))
                bank_free[b] = [m]
                stm[d] = m
                b, free = take(BANKS)
                bv2 = psum[:, b, :].rearrange("p (h n) -> p h n", h=4)
                m = pe.do([stm[d], wm[d]] + free, *[mm(bv2[:, h, :], wT[:, c2, h, :], state[:, d, h, :]) for h in range(4)])
                m = V_([m, um[c2]], lambda c2=c2, bv2=bv2: V.tensor_tensor(u[:, c2], u[:, c2], bv2, SUB))
                bank_free[b] = [m]
                um[c2] = m
            sq = kbg[:, 1]
            mix_marks = []
            for t in range(NT):
                b, free = take(BANKS)
                bv = psum[:, b, :].rearrange("p (h n) -> p h n", h=4)
                ops = []
                dl = t if first[0] != t else 1
                for h in range(4):
                    dlate = 0 if first[0] != t else 1
                    dearly = 1 - dlate
                    cl, ce = combos.index((dlate, t)), combos.index((dearly, t))
                    ops += [mm(bv[:, h, :], qg[:, dlate, h, :], state[:, dlate, h, :], True, False),
                            mm(bv[:, h, :], QK[:, cl, h, :], u[:, cl, h, :], False, False),
                            mm(bv[:, h, :], QK[:, ce, h, :], u[:, ce, h, :], False, True)]
                m = pe.do(um + qkmarks + [qgm[0], qgm[1], stm[0], stm[1]] + free, *ops)
                ms = act.do([m] + mix_marks + list(wm.values()), lambda bv=bv: S.activation(sq, bv, ACT.Square))
                mr = V_([ms], lambda t=t: V.tensor_reduce(r4[:, t], sq, AXX, ADD))
                mr = inverse_root(r4[:, t], r4[:, t], [mr], 1.0 / HD)
                o = mix[:, t, W:2 * W].rearrange("p (h n) -> p h n", h=4)
                mo = V_([mr], lambda t=t, o=o, bv=bv: V.tensor_tensor(o, bv, bc(r4[:, t]), MUL))
                bank_free[b] = [mo]
                mo = pool.do([mo], lambda o=o: G.tensor_tensor(o, o, gnw[:, P * l:P * l + P].unsqueeze(1).to_broadcast([P, 4, P]), MUL))
                mo = pool.do([mo, r_marks[("z", 0)], r_marks[("z", 1)]], lambda t=t: G.tensor_tensor(mix[:, t, W:2 * W], mix[:, t, W:2 * W], z[:, t, :], MUL))
                mix_marks = [mo]
            gdn_done = mix_marks

            mixed = to_T(ret_o, mixT, ret["ln"], range(4)) + to_T(mix[:, :, W:2 * W], mixT, gdn_done, range(4, 8))
            arena_free = everything()
            done = project_out(a["w_out"][l], mixT, mixed)
            for k in range(NHL):
                hl_free[k] = arena_free
            following.ahead(3)
            held[:] = everything()
            residual(done, wmark, 1.0, (32 * l + 16, True), arena_free)

        def to_T(src, dstT, after, tiles=range(KD)):
            marks = []
            tiles = list(tiles)
            for t in range(NT):
                for g in range(0, len(tiles), 4):
                    n = min(4, len(tiles) - g)
                    b, free = take()
                    m = pe.do(after + free, *[tr(psum[:, b, P * j:P * j + P], src[:, t, P * (g + j):P * (g + j + 1)]) for j in range(n)])
                    m = V_([m], lambda b=b, g=g, t=t, n=n: V.tensor_copy(
                        dstT[:, tiles[g]:tiles[g] + n, P * t:P * t + P], psum[:, b, 0:P * n].rearrange("p (j n) -> p j n", j=n)))
                    bank_free[b] = [m]
                    marks.append(m)
            return marks

        def cross_sources(l):
            return [columns(a["xattn_q"][l], 256 * i) for i in range(4)] + [rows(a["xattn_o"][l], 2 * i) for i in range(4)]

        def cross(l, stream):
            stage_start(held)
            stream.ahead(4)
            scaled = carve(NT, D)
            ready = normed[0]
            qT, oT = xnT, carve(KD, TOK)
            qm, weighed, spread, om = [], {}, {}, {}

            def query(i):
                b, pv, m = split_project_T(stream, ready)
                m = act.do([m] + ready[0] + ready[1], lambda: S.copy(qT[:, 2 * i:2 * i + 2, :], pv))
                bank_free[b] = [m]
                qm.append(m)

            prob, PT = scaled.rearrange("p t (h m) -> p h t m", h=HEADS), carve(HEADS, NT, TOK)
            top, total = (softmax_s[:, 8 * k:8 * k + 8].rearrange("p (h t) -> p h t", h=HEADS) for k in range(2))
            scale = 256 ** -0.5

            def weigh(h):
                b, free = take()
                m = pe.do([qm[h]] + free, *[mm(psum[:, b, 256 * t:256 * t + 256], qT[:, 2 * h + k, P * t:P * t + P], memkT[:, 2 * h + k, :], k == 0, k == 1)
                                            for t in range(NT) for k in range(2)])
                pv = psum[:, b, :].rearrange("p (t m) -> p t m", t=2)
                m = V_([m], lambda: V.tensor_reduce(top[:, h], pv, AXX, MAX))
                m = V_([m], lambda: V.tensor_scalar(top[:, h], top[:, h], -scale, None, MUL))
                for t in range(NT):
                    m = act.do([m], lambda t=t: S.activation(prob[:, h, t, :], pv[:, t, :], ACT.Exp, bias=top[:, h, t:t + 1],
                                                             scale=scale, accum_out=total[:, h, t:t + 1]))
                bank_free[b] = [m]
                m = V_([m], lambda: V.reciprocal(total[:, h], total[:, h]))
                weighed[h] = V_([m], *[lambda t=t: V.tensor_scalar(prob[:, h, t, :], prob[:, h, t, :], total[:, h, t:t + 1], None, MUL)
                                       for t in range(2)])

            def turn_over(h):
                b, free = take()
                m = pe.do([weighed[h]] + free, *[tr(psum[:, b, 256 * j + P * t:256 * j + P * t + P], prob[:, h, t, P * j:P * j + P])
                                                 for j in range(2) for t in range(2)])
                spread[h] = V_([m], lambda: V.tensor_copy(PT[:, h], psum[:, b, :].rearrange("p (j t) -> p j t", j=2)))
                bank_free[b] = [spread[h]]

            def attend(h):
                b, free = take()
                m = pe.do([spread[h]] + free, *[mm(psum[:, b, 256 * e:256 * e + 256], memv[:, j, 256 * h + P * e:256 * h + P * e + P], PT[:, h, j, :], j == 0, j == 1)
                                                for e in range(2) for j in range(2)])
                m = act.do([m], lambda: S.copy(oT[:, 2 * h:2 * h + 2, :], psum[:, b, :].rearrange("p (j t) -> p j t", j=2)))
                bank_free[b] = [m]
                om[h] = split(oT[:, 2 * h:2 * h + 2, :], x_hl[:, 0, 2 * h:2 * h + 2, :], x_hl[:, 1, 2 * h:2 * h + 2, :], [m, qm[3]])

            half_of = lambda n: (lambda h, j: x_hl[:, h, 2 * n + j, :])
            query(0)
            wmark = load_post(a["norm_post"][l, 2], 0)
            query(1)
            stream.ahead(2)
            weigh(0)
            query(2)
            weigh(1)
            stream.ahead(2)
            turn_over(0)
            query(3)
            weigh(2)
            turn_over(1)
            attend(0)
            weigh(3)
            stream.ahead(2)
            turn_over(2)
            attend(1)
            split_out(stream, half_of(0), True, [om[0]])
            stream.ahead(2)
            turn_over(3)
            attend(2)
            split_out(stream, half_of(1), False, [om[1]])
            attend(3)
            stream.ahead(3)
            done = split_out_last(stream, [half_of(2), half_of(3)], [[om[2]], [om[3]]])
            stream.ahead(2)
            held[:] = everything()
            residual(done, wmark, 1.0, (32 * l + 24, True))

        def mlp_sources():
            sources = []
            for i in range(MLP // 256 + 1):
                if i < MLP // 256:
                    sources.append(columns(a["mlp_w1_2"][0], 256 * i))
                if i:
                    sources.append(rows(a["mlp_w2_2"][0], 2 * (i - 1)))
            return sources

        mlp_stream = SplitStream(mlp_sources())
        plan, nxt = {}, None
        for l in reversed(range(DEPTH)):
            plan["ffn2", l] = SplitStream(ffn_sources(a["ffn2_gate"][l], a["ffn2_up"][l], a["ffn2_down"][l]), nxt)
            plan["cross", l] = SplitStream(cross_sources(l), plan["ffn2", l])
            nxt = plan["ffn1", l] = SplitStream(ffn_sources(a["ffn1_gate"][l], a["ffn1_up"][l], a["ffn1_down"][l]))
        plan["ffn1", 0].load(3)
        late = late_loads()
        normed[0] = norm_T(x, xnT, 0, stage_scratch, x_marks, True)
        for l in range(DEPTH):
            ffn(plan["ffn1", l], a["norm_post"][l, 0], (32 * l + 8, False), iter(()) if l else late_setup(late))
            dump(f"x{l}0", x[:, :, :], [])
            keep_tail[0] = True
            mixer(l, plan["cross", l])
            keep_tail[0] = False
            dump(f"x{l}1", x[:, :, :], [])
            cross(l, plan["cross", l])
            dump(f"x{l}2", x[:, :, :], [])
            ffn(plan["ffn2", l], a["norm_post"][l, 3], (32 * l + 32, True) if l + 1 < DEPTH else (80, False))
            dump(f"x{l}3", x[:, :, :], [])

        def mixer2(following):
            stage_start(held)
            w = a["w_in_2"][0]
            spare = [memkT[:, :, :].rearrange("p k t -> p (k t)"), memv[:, :, :].rearrange("p t d -> p (t d)")]
            shaped = lambda v, *s_: v.rearrange("p (a b) -> p a b", a=s_[0]) if len(s_) == 1 else \
                v.rearrange("p (a b c) -> p a b c", a=s_[0], b=s_[1])
            scaled = carve(NT, D)
            A0, H0, R0, U0 = 0, 768, 1792, 2688
            ready = normed[0][0] + normed[0][1]
            colT = lambda c0: project_T(w, c0, xnT, ready, banks=WORK8)
            colN = lambda c0: project_N(w, c0, xnT, ready, banks=WORK8)

            def kept(job, dst, fn=None, after=(), **kw):
                b, pv, m = job
                if fn is None:
                    m = act.do([m] + list(after), lambda: S.copy(dst, pv))
                else:
                    m = act.do([m] + list(after), lambda: S.activation(dst, pv, fn, **kw))
                bank_free[b] = [m]
                return m

            def half_sums(src, after):
                b, free = take(WORK8)
                m = pe.do(list(after) + free, mm(psum[:, b, :], C("half"), src))
                return b, psum[:, b, :].rearrange("p (j t) -> p j t", j=2), m

            qa, ka, va = carve(2, TOK), carve(2, TOK), carve(NT, 256)
            marks = {}

            def attention_in():
                b, pv, m = colT(A0)
                marks["q"] = act.do([m], lambda pv=pv: S.mul(qa, pv, 64 ** -0.5))
                bank_free[b] = [marks["q"]]
                marks["k"] = kept(colT(A0 + 256), ka)
                marks["v"] = kept(colN(A0 + 512), va)

            qb, fb, ib, kb = carve(2, TOK), carve(2, TOK), carve(2, TOK), carve(2, TOK)
            gbn = carve(NT, 256)

            def recurrence_query():
                marks["hq"] = kept(colT(H0), qb, ACT.Silu)

            def recurrence_gates():
                b, pv, m = colT(H0 + 256)
                m1 = act.do([m], lambda pv=pv: S.activation(fb, pv, ACT.Sigmoid))
                m2 = act.do([m1], lambda pv=pv: S.activation(kb, pv, ACT.Sigmoid, scale=-1.0))
                bank_free[b] = [m2]
                marks["hf"] = V_([m2], *[lambda j=j: V.tensor_scalar(fb[:, j, :], fb[:, j, :], lb[:, 3, j:j + 1], lb[:, 2, j:j + 1], MUL, ADD) for j in range(2)],
                                 *[lambda j=j: V.tensor_scalar(kb[:, j, :], kb[:, j, :], lb[:, 3, j:j + 1], None, MUL) for j in range(2)])

            def recurrence_values():
                marks["hi"] = kept(colT(H0 + 512), ib)

            def recurrence_gate():
                marks["hg"] = kept(colN(H0 + 768), gbn, ACT.Silu)

            pc = carve(7, TOK + 1)
            xs = carve(7, TOK)
            zc = pool.do([], lambda: G.memset(pc[:, :, 0:1], 0.0))
            pm = []
            for i in range(3):
                pm.append(kept(colT(R0 + 256 * i), pc[:, 2 * i:2 * i + 2, 1:TOK + 1]))
            s, wv, landed = slab(*columns(w, R0 + 768, P))
            b, free = take(WORK8)
            m = pe.do([landed] + free + ready, *[mm(psum[:, b, 0:256], wv[:, k, :], xnT[:, k, :], k == 0, k == KD - 1) for k in range(KD)])
            slot_free[s] = [m]
            m = act.do([m], lambda b=b: S.copy(pc[:, 6, 1:TOK + 1], psum[:, b, 0:256]))
            bank_free[b] = [m]
            pm.append(m)
            attention_in()
            sp.wait(held)
            reach = carve(4, 384)
            rb = a["attn_rel_bias_2"]
            for h in range(4):
                load(reach[:, h, :], bass.AP(rb.tensor, h * 513 + 1, [[1, P], [1, 384]]), group="small2")
            lora = carve(256)
            load(lora[0:32, :], a["rwkv_w2_2"][0], group="small2")
            load(lora[32:64, :], a["rwkv_a2_2"][0], group="small2")
            load(lora[64:128, :], a["rwkv_g2_2"][0], group="small2")
            gate_w = carve(2, 2, P)
            zm = pool.do([], lambda: G.memset(gate_w, 0.0))
            for k, name in enumerate(("lru_wa_2", "lru_wx_2")):
                for n in range(4):
                    small2 = load(gate_w[64 * (n % 2):64 * (n % 2) + 64, k, n // 2, 64 * (n % 2):64 * (n % 2) + 64],
                                  a[name][0, n], [zm], group="small2")
            wmark = load_post(a["norm_mix_post_2"][0], 0)
            m = V_(pm + [zc], lambda: V.tensor_tensor(xs, pc[:, :, 0:TOK], pc[:, :, 1:TOK + 1], SUB))
            xm = V_([m], *[lambda k=k: V.scalar_tensor_tensor(xs[:, k, :], xs[:, k, :], vec("rwkv_mu_2", k), pc[:, k, 1:TOK + 1], MUL, ADD)
                           for k in (6, 2, 3, 0, 1, 4, 5)])
            rT, kT0, vT, lo = xs[:, 0:2, :], xs[:, 2:4, :], xs[:, 4:6, :], xs[:, 6, :]
            m1 = act.do([xm], lambda: S.activation(lo[64:128, :], lo[64:128, :], ACT.Sigmoid))
            mtanh = act.do([xm], lambda: S.activation(lo[0:32, :], lo[0:32, :], ACT.Tanh))
            kk, k2, t1 = carve(2, TOK), carve(2, TOK), carve(2, TOK)
            flat = lambda v: v.rearrange("p j t -> p (j t)")
            m = V_([xm], *[lambda j=j: V.tensor_scalar(kk[:, j, :], kT0[:, j, :], vec("rwkv_k_k_2", j), None, MUL) for j in range(2)])
            m2 = V_([m], lambda: V.tensor_tensor(t1, kk, kk, MUL))
            b, pv, m2 = half_sums(flat(t1), [m2])
            m2 = act.do([m2], lambda pv=pv: S.activation(t1, pv, ACT.Sqrt))
            bank_free[b] = [m2]
            m2 = V_([m2], lambda: V.tensor_scalar(t1, t1, 1e-12, None, MAX))
            m2 = V_([m2], lambda: V.reciprocal(t1, t1))
            kkm = V_([m2], lambda: V.tensor_tensor(kk, kk, t1, MUL))
            lw, aT, gT = carve(2, TOK), carve(2, TOK), carve(2, TOK)
            banks3 = []
            for p0, p1 in ((0, 32), (32, 64), (64, 128)):
                b, free = take(WORK8)
                ml = pe.do([mtanh, m1, small2] + free, *[mm(psum[:, b, 256 * j:256 * j + 256], lora[p0:p1, P * j:P * j + P], lo[p0:p1, :]) for j in range(2)])
                banks3.append((b, ml))
            (b, ml) = banks3[0]
            m = act.do([ml], *[lambda j=j, b=b: S.activation(lw[:, j, :], psum[:, b, 256 * j:256 * j + 256], ACT.Sigmoid, bias=vec("rwkv_w0_2", j)) for j in range(2)])
            bank_free[b] = [m]
            lwm = V_([m], lambda: V.tensor_scalar(lw, lw, -float(np.exp(-0.5)), None, MUL))
            (b, ml) = banks3[1]
            am = act.do([ml], *[lambda j=j, b=b: S.activation(aT[:, j, :], psum[:, b, 256 * j:256 * j + 256], ACT.Sigmoid, bias=vec("rwkv_a0_2", j)) for j in range(2)])
            bank_free[b] = [am]
            (b, ml) = banks3[2]
            gm = act.do([ml], lambda b=b: S.copy(gT, psum[:, b, :].rearrange("p (j t) -> p j t", j=2)))
            bank_free[b] = [gm]
            recurrence_query()
            m = V_([am], *[lambda j=j: V.tensor_scalar(k2[:, j, :], aT[:, j, :], 1.0, vec("rwkv_k_a_2", j), SUB, MUL) for j in range(2)])
            k2m = V_([m], lambda: V.scalar_tensor_tensor(k2, k2, 1.0, kT0, ADD, MUL))
            recurrence_gates()
            recurrence_values()
            cum, ecum, eneg, eprev = carve(2, TOK), carve(2, TOK), carve(2, TOK), carve(2, TOK)
            cm = V_([lwm], *[lambda j=j: V.tensor_tensor_scan(cum[:, j, :], C("resets"), lw[:, j, :], 0.0, MUL, ADD) for j in range(2)])
            m = V_([cm], lambda: V.tensor_tensor(eprev, cum, lw, SUB))
            e1 = act.do([cm], lambda: S.activation(ecum, cum, ACT.Exp))
            e2 = act.do([cm], lambda: S.activation(eneg, cum, ACT.Exp, scale=-1.0))
            e3 = act.do([m], lambda: S.activation(eprev, eprev, ACT.Exp))
            alpha, betaT, khat, rhat = eprev, carve(2, TOK), carve(2, TOK), carve(2, TOK)
            alm = pool.do([e3, kkm], lambda: G.tensor_tensor(alpha, eprev, kk, MUL))
            m = pool.do([kkm, am, e2], lambda: G.tensor_tensor(betaT, kk, aT, MUL))
            btm = pool.do([m], lambda: G.tensor_tensor(betaT, betaT, eneg, MUL))
            khm = pool.do([k2m, e2], lambda: G.tensor_tensor(khat, k2, eneg, MUL))
            rhm = pool.do([e1, xm], lambda: G.tensor_tensor(rhat, rT, ecum, MUL))
            natb, natk, natv = carve(4, 256), carve(4, 256), carve(4, 256)
            natm = []
            for src, dst, dep, sign in ((betaT, natb, btm, -1.0), (khat, natk, khm, 1.0), (vT, natv, xm, 1.0)):
                for half in range(2):
                    b, free = take(WORK8)
                    m = pe.do([dep] + free, *[tr(psum[0:64, b, 256 * c + P * j:256 * c + P * j + P],
                                                 src[:, j, 128 * half + 64 * c:128 * half + 64 * c + 64]) for c in range(2) for j in range(2)])
                    m = act.do([m], lambda dst=dst, half=half, b=b, sign=sign: S.mul(
                        dst[0:64, 2 * half:2 * half + 2, :], psum[0:64, b, :].rearrange("p (c n) -> p c n", c=2), sign))
                    bank_free[b] = [m]
                    natm.append(m)
            Lr, Xr, XTr, Ak = (shaped(spare[k // 2][:, 1024 * (k % 2):1024 * (k % 2) + 1024], 2, 8) for k in range(4))
            Rb, Rk = carve(2, 8, 64), carve(2, 8, 64)
            pair_m = {n: [] for n in "LABK"}
            for s2 in range(2):
                for key, left, right, dst, mask in (("L", alpha, betaT, Lr, None), ("A", khat, alpha, Ak, "before"),
                                                    ("B", betaT, rhat, Rb, "upto"), ("K", khat, rhat, Rk, "upto")):
                    for e in range(2):
                        b, free = take(WORK8)
                        bv = psum[0:64, b, 0:256].rearrange("p (n s) -> p n s", n=4)
                        rows64 = slice(64 * e, 64 * e + 64)
                        at = lambda n: slice(64 * (2 * s2 + n // 2), 64 * (2 * s2 + n // 2) + 64)
                        m = pe.do([alm, btm, khm, rhm] + free, *[mm(bv[:, n, :], left[rows64, n % 2, at(n)], right[rows64, n % 2, at(n)])
                                                                for n in range(4)])
                        o = dst[0:64, s2].rearrange("p (n e) s -> p e n s", e=2)[:, e]
                        if mask is None:
                            m = act.do([m], lambda o=o, bv=bv: S.copy(o, bv))
                        else:
                            m = V_([m], lambda o=o, bv=bv, mask=mask: V.tensor_tensor(
                                o, bv, C(mask)[0:64, 0:64].unsqueeze(1).to_broadcast([64, 4, 64]), MUL))
                        bank_free[b] = [m]
                        if key == "B":
                            m = pool.do([m], lambda o=o: G.tensor_scalar(o, o, -1.0, None, MUL))
                        pair_m[key].append(m)

            prob = shaped(pc.rearrange("p a b -> p (a b)")[:, 0:1536], 4, 3)
            PTa = carve(4, 3, P)
            ya, yb = carve(NT, 256), eneg
            top, total = carve(4, 2), carve(4, 2)

            def attention_head(h):
                hb, j = 64 * (h % 2), h // 2
                b, free = take(WORK8)
                ops = [mm(psum[:, b, 0:128], qa[hb:hb + 64, j, 0:128], ka[hb:hb + 64, j, 0:128], True, False),
                       mm(psum[:, b, 0:128], C("flip"), reach[:, h, 128:256], False, True),
                       mm(psum[:, b, 128:384], qa[hb:hb + 64, j, 128:256], ka[hb:hb + 64, j, :], True, False),
                       mm(psum[:, b, 128:384], C("flip"), reach[:, h, 0:256], False, True)]
                m = pe.do([marks["q"], marks["k"], small2] + free, *ops)
                yield
                m = V_([m], lambda b=b: V.tensor_tensor(psum[:, b, 64:128], psum[:, b, 64:128], C("barred"), ADD),
                       lambda b=b: V.tensor_tensor(psum[:, b, 320:384], psum[:, b, 320:384], C("barred"), ADD))
                m = V_([m], lambda b=b: V.tensor_reduce(top[:, h, 0:1], psum[:, b, 0:128], AXX, MAX),
                       lambda b=b: V.tensor_reduce(top[:, h, 1:2], psum[:, b, 128:384], AXX, MAX))
                m = V_([m], lambda: V.tensor_scalar(top[:, h], top[:, h], -1.0, None, MUL))
                for t, (lo_, hi_) in enumerate(((0, 128), (128, 384))):
                    m = act.do([m, xm], lambda b=b, t=t, lo_=lo_, hi_=hi_: S.activation(
                        prob[:, h].rearrange("p a b -> p (a b)")[:, lo_:hi_], psum[:, b, lo_:hi_], ACT.Exp,
                        bias=top[:, h, t:t + 1], accum_out=total[:, h, t:t + 1]))
                bank_free[b] = [m]
                mr = V_([m], lambda: V.reciprocal(total[:, h], total[:, h]))
                yield
                b, free = take(WORK8)
                m = pe.do([m] + free, *[tr(psum[:, b, P * k:P * k + P], prob[:, h, k, :]) for k in range(3)])
                m = act.do([m], lambda b=b: S.copy(PTa[:, h], psum[:, b, 0:384].rearrange("p (a b) -> p a b", a=3)))
                bank_free[b] = [m]
                yield
                b, free = take(WORK8)
                m = pe.do([m, marks["v"]] + free, mm(psum[:, b, 0:64], PTa[:, h, 0, :], va[:, 0, 64 * h:64 * h + 64]),
                          *[mm(psum[:, b, 64:128], PTa[:, h, 1 + k, :], va[:, k, 64 * h:64 * h + 64], k == 0, k == 1) for k in range(2)])
                m = V_([m, mr], *[lambda b=b, t=t: V.tensor_scalar(ya[:, t, 64 * h:64 * h + 64], psum[:, b, 64 * t:64 * t + 64],
                                                                  total[:, h, t:t + 1], None, MUL) for t in range(2)])
                bank_free[b] = [m]
                marks[("ya", h)] = m
                yield

            xd, conv = carve(2, TOK + 3), kT0
            gr, gi, yd = (shaped(v, 2) for v in (C("ahead"), C("behind"), C("bwd")[:, 0:512]))

            def lru():
                z0 = pool.do([], lambda: G.memset(xd[:, :, 0:3], 0.0))
                m = kept(colT(U0), xd[:, :, 3:TOK + 3])
                yield
                mg = kept(colT(U0 + 256), yd, ACT.Gelu_apprx_tanh)
                for j in range(2):
                    mc = V_([m, z0, k2m], lambda j=j: V.tensor_scalar(conv[:, j, :], xd[:, j, 0:TOK], vec("lru_conv_w_2", j),
                                                                 vec("lru_conv_b_2", j), MUL, ADD))
                    for n in range(1, 4):
                        mc = V_([mc], lambda j=j, n=n: V.scalar_tensor_tensor(conv[:, j, :], xd[:, j, n:n + TOK],
                                                                              vec("lru_conv_w_2", 2 * n + j), conv[:, j, :], MUL, ADD))
                yield
                for k, dst, name in ((0, gr, "lru_ba_2"), (1, gi, "lru_bx_2")):
                    b, free = take(WORK8)
                    m = pe.do([mc, small2] + free, *[mm(psum[:, b, 256 * j:256 * j + 256], gate_w[:, k, j, :], conv[:, j, :]) for j in range(2)])
                    m = act.do([m], *[lambda j=j, b=b, dst=dst, name=name: S.activation(
                        dst[:, j, :], psum[:, b, 256 * j:256 * j + 256], ACT.Sigmoid, bias=vec(name, j)) for j in range(2)])
                    bank_free[b] = [m]
                yield
                mu_ = V_([m], *[lambda j=j: V.tensor_scalar(gr[:, j, :], gr[:, j, :], sp_l[:, j:j + 1], 8.0, MUL, MUL) for j in range(2)])
                mi = pool.do([m, mc], lambda: G.tensor_tensor(gi, gi, conv, MUL))
                th, aa = conv, xd[:, :, 0:TOK]
                m1 = act.do([mu_, mi], lambda: S.activation(th, gr, ACT.Tanh))
                m2 = act.do([mu_, mc], lambda: S.activation(aa, gr, ACT.Exp, scale=-1.0))
                m3 = pool.do([m2], lambda: G.tensor_tensor(gr, aa, aa, MUL))
                yield
                m3 = V_([m3, m1], lambda: V.scalar_tensor_tensor(th, gr, 1.0, th, ADD, MUL))
                m3 = act.do([m3], lambda: S.activation(th, th, ACT.Sqrt))
                m3 = pool.do([m3], lambda: G.tensor_tensor(gi, gi, th, MUL))
                m3 = V_([m3, m2], *[lambda j=j: V.tensor_tensor_scan(gr[:, j, :], aa[:, j, :], gi[:, j, :], 0.0, MUL, ADD) for j in range(2)])
                marks["yd"] = V_([m3, mg], lambda: V.tensor_tensor(yd, yd, gr, MUL))
                yield

            def aside():
                real_gated, heads = lru(), [attention_head(h) for h in range(4)]
                for h in range(4):
                    yield next(real_gated, None)
                    yield next(heads[h], None)
                    if h == 0:
                        yield recurrence_gate()
                    yield next(heads[h - 1], None) if h else None
                    yield next(heads[h], None)
                for job in [real_gated] + heads:
                    for _ in job:
                        yield

            steps = aside()

            def fill():
                for _ in range(3):
                    next(steps, None)

            LMr, Wr = (shaped(scaled[:, k, :], 2, 8) for k in range(2))
            xts = inverses([(Lr[0:64, s_], Xr[0:64, s_], XTr[0:64, s_], pair_m["L"][2 * s_:2 * s_ + 2]) for s_ in range(2)],
                           64, 8, ["fwd", "fwd"], LEVELS[:6], fill, LMr, Wr, [], WORK8)
            for _ in steps:
                pass

            ST = cosT[:, :].rearrange("p (j n) -> p j n", j=2)
            rhs, sa, yn, av = (v.rearrange("p s n t -> p (s n t)").rearrange("p (c n) -> p c n", c=4) for v in (Lr, Xr, LMr, Wr))
            inverted = xts[0] + xts[1]
            stm = pool.do([], lambda: G.memset(ST, 0.0))

            avm = []
            for c in range(4):
                b, free = take((0, 1))
                m = pe.do(pair_m["A"] + natm + free, *[mm(psum[0:64, b, 64 * h:64 * h + 64], Ak[0:64, c // 2, 4 * (c % 2) + h, :], natv[0:64, c, 64 * h:64 * h + 64]) for h in range(4)])
                m = act.do([m] + inverted, lambda c=c, b=b: S.copy(av[0:64, c, :], psum[0:64, b, 0:256]))
                bank_free[b] = [m]
                avm.append(m)

            rw_m = {"st": stm, "y": []}

            def rwkv_chunk(c):
                s_, n0 = c // 2, 4 * (c % 2)
                b, free = take((0, 1))
                m = pe.do([rw_m["st"], alm] + free, *[mm(psum[0:64, b, P * j:P * j + P], alpha[:, j, 64 * c:64 * c + 64], ST[:, j, :]) for j in range(2)])
                yield
                m = V_([m, avm[c]], lambda c=c, b=b: V.tensor_tensor(rhs[0:64, c, :], psum[0:64, b, 0:256], av[0:64, c, :], ADD))
                bank_free[b] = [m]
                b, free = take((0, 1))
                yield
                m = pe.do([m] + xts[s_] + free, *[mm(psum[0:64, b, 64 * h:64 * h + 64], XTr[0:64, s_, n0 + h, :], rhs[0:64, c, 64 * h:64 * h + 64]) for h in range(4)])
                ms = V_([m], lambda c=c, b=b: V.tensor_copy(sa[0:64, c, :], psum[0:64, b, 0:256]))
                bank_free[b] = [ms]
                yield
                if c < 3:
                    b, free = take((2, 3))
                    m = pe.do([ms] + natm + free, *[op for j in range(2) for op in (
                        mm(psum[:, b, P * j:P * j + P], natb[0:64, c, P * j:P * j + P], sa[0:64, c, P * j:P * j + P], True, False),
                        mm(psum[:, b, P * j:P * j + P], natk[0:64, c, P * j:P * j + P], natv[0:64, c, P * j:P * j + P], False, True))])
                b2, free2 = take((2, 3))
                ops = []
                for j in range(2):
                    ops.append(mm(psum[0:64, b2, P * j:P * j + P], rhat[:, j, 64 * c:64 * c + 64], ST[:, j, :], True, False))
                    for h in (2 * j, 2 * j + 1):
                        ops.append(mm(psum[0:64, b2, 64 * h:64 * h + 64], Rb[0:64, s_, n0 + h, :], sa[0:64, c, 64 * h:64 * h + 64], False, False))
                        ops.append(mm(psum[0:64, b2, 64 * h:64 * h + 64], Rk[0:64, s_, n0 + h, :], natv[0:64, c, 64 * h:64 * h + 64], False, h == 2 * j + 1))
                my = pe.do([ms, rw_m["st"]] + pair_m["B"] + pair_m["K"] + free2, *ops)
                mq = act.do([my], lambda c=c, b2=b2: S.copy(yn[0:64, c, :], psum[0:64, b2, 0:256]))
                bank_free[b2] = [mq]
                rw_m["y"].append(mq)
                yield
                if c < 3:
                    m = V_([m, my], lambda b=b: V.tensor_tensor(ST, psum[:, b, 0:256].rearrange("p (j n) -> p j n", j=2), ST, ADD))
                    bank_free[b] = [m]
                    rw_m["st"] = V_([m], *[lambda j=j, c=c: V.scalar_tensor_tensor(ST[:, j, :], ST[:, j, :], ecum[:, j, 64 * c + 63:64 * c + 64],
                                                                                  C("half"), MUL, MUL) for j in range(2)])
                yield

            scratch = [reach.rearrange("p a b -> p (a b)"), PTa.rearrange("p a b c -> p (a b c)")]
            NB, NZ, LAG = 2, 3, 2
            pair = lambda v, n: [v[:, 512 * k:512 * k + 512] for k in range(n)]
            add_b, st_b, z_b = pair(scratch[0], 2), [scratch[0][:, 1024:1536], flat(aT)], pair(scratch[1], 3)
            attended = [marks[("ya", h)] for h in range(4)] + [btm, k2m]
            z_read = [attended for _ in range(NZ)]
            s_read = [attended for _ in range(NB)]
            a_read = [attended for _ in range(NB)]
            yb_bank = 7
            picks = [sinT[:, 0:128], sinT[:, 128:256]]
            pick_read = [[], []]
            yv = psum[:, yb_bank, :].rearrange("p (t j v h) -> p t j v h", t=2, j=2, h=2)
            yb_free = list(bank_free[yb_bank])
            chunk_steps = (None for c in range(4) for _ in rwkv_chunk(c))
            zm_ = {}
            fz = V_([marks["hf"]], lambda: V.memset(fb[:, :, 0:1], 0.0))
            for v in range(64 + LAG):
                if v < 64:
                    b, free = take((4, 5, 6))
                    pick = picks[v % 2]
                    mp = act.do(pick_read[v % 2], lambda v=v, pick=pick: S.copy(
                        pick.rearrange("p (h k) -> p h k", h=2), ident.rearrange("p (h v) -> p h v", h=2)[:, :, v:v + 1].to_broadcast([P, 2, 64])))
                    mi = pe.do([mp, marks["hi"]] + free, mm(psum[:, b, :], pick, flat(ib)))
                    pick_read[v % 2] = [mi]
                    k, kz = v % NB, v % NZ
                    ma = V_([mi, marks["hf"]] + a_read[k], lambda k=k, b=b: V.tensor_tensor(add_b[k], flat(kb), psum[:, b, :], MUL))
                    ms = V_([ma, fz] + s_read[k], lambda k=k: V.tensor_tensor_scan(st_b[k], flat(fb), add_b[k], 0.0, MUL, ADD))
                    a_read[k] = [ms]
                    mz = pool.do([ms, marks["hq"]] + z_read[kz], lambda k=k, kz=kz: G.tensor_tensor(z_b[kz], st_b[k], flat(qb), MUL))
                    s_read[k] = [mz]
                    zm_[v] = mz
                    bank_free[b] = [ma]
                if v >= LAG:
                    n = v - LAG
                    my = pe.do([zm_[n]] + yb_free, *[mm(yv[:, t, j, n, :], z_b[n % NZ][:, 256 * j + P * t:256 * j + P * t + P], C("headcol"))
                                                     for j in range(2) for t in range(2)])
                    z_read[n % NZ] = [my]
                if v % 2:
                    next(chunk_steps, None)
            for _ in chunk_steps:
                pass
            ybh = yb.rearrange("p t (h v) -> p t h v", h=4)
            sq4, r8 = lw.rearrange("p t (h v) -> p t h v", h=4), carve(NT, 4)
            src = psum[:, yb_bank, :].rearrange("p (t j v h) -> p t j h v", t=2, j=2, h=2)
            m = act.do([my], *[lambda t=t, j=j: S.copy(ybh[:, t, 2 * j:2 * j + 2, :], src[:, t, j]) for t in range(2) for j in range(2)])
            bank_free[yb_bank] = [m]
            m2 = act.do([m], lambda: S.activation(sq4, ybh, ACT.Square))
            m2 = V_([m2], lambda: V.tensor_reduce(r8, sq4, AXX, ADD))
            m2 = inverse_root(r8.rearrange("p t h -> p (t h)"), r8.rearrange("p t h -> p (t h)"), [m2], 1.0 / 64)
            m = V_([m2], lambda: V.tensor_tensor(ybh, ybh, r8.unsqueeze(3).to_broadcast([P, NT, 4, 64]), MUL))
            m = V_([m], lambda: V.tensor_tensor(yb, yb, hgn[:, :].unsqueeze(1).to_broadcast([P, NT, 256]), MUL))
            ybm = V_([m, marks["hg"]], lambda: V.tensor_tensor(yb, yb, gbn, MUL))

            yT = cum
            b, free = take((4, 5, 6))
            m = pe.do(rw_m["y"] + free, *[tr(psum[:, b, 256 * j + 64 * c:256 * j + 64 * c + 64], yn[0:64, c, P * j:P * j + P]) for j in range(2) for c in range(4)])
            m = act.do([m, e1, e2], lambda b=b: S.copy(yT, psum[:, b, :].rearrange("p (j t) -> p j t", j=2)))
            bank_free[b] = [m]
            b, pv, ms = half_sums(flat(yT), [m])
            m = V_([ms, m], lambda pv=pv: V.scalar_tensor_tensor(yT, pv, -1.0 / 64, yT, MUL, ADD))
            bank_free[b] = [m]
            ms = act.do([m], lambda: S.activation(t1, yT, ACT.Square))
            b, pv, ms = half_sums(flat(t1), [ms])
            ms = V_([ms], lambda pv=pv: V.tensor_scalar(t1, pv, 1.0 / 64, 64 * 1e-5, MUL, ADD))
            bank_free[b] = [ms]
            ms = act.do([ms], lambda: S.activation(t1, t1, ACT.Sqrt))
            ms = V_([ms], lambda: V.reciprocal(t1, t1))
            m = V_([m, ms], lambda: V.tensor_tensor(yT, yT, t1, MUL))
            m = V_([m], *[lambda j=j: V.tensor_scalar(yT[:, j, :], yT[:, j, :], vec("rwkv_ln_w_2", j), vec("rwkv_ln_b_2", j), MUL, ADD) for j in range(2)])
            ms = V_([m], *[lambda j=j: V.scalar_tensor_tensor(t1[:, j, :], rT[:, j, :], vec("rwkv_r_k_2", j), k2[:, j, :], MUL, MUL) for j in range(2)])
            b, pv, ms = half_sums(flat(t1), [ms])
            ms = V_([ms], lambda pv=pv: V.tensor_tensor(t1, pv, vT, MUL))
            bank_free[b] = [ms]
            m = V_([ms], lambda: V.tensor_tensor(yT, yT, t1, ADD))
            m = V_([m, gm], lambda: V.tensor_tensor(mixT[:, 4:6, :], yT, gT, MUL))
            m1 = V_([marks["yd"]], lambda: V.tensor_copy(mixT[:, 6:8, :], yd))
            mixed = [m, m1]
            mixed += to_T(ya, mixT, [marks[("ya", h)] for h in range(4)], (0, 1))
            mixed += to_T(yb, mixT, [ybm], (2, 3))
            dump("mix3", mixT[:, :, :], mixed)
            arena_free = everything()
            done = project_out(a["w_out_2"][0], mixT, mixed)
            for k in range(NHL):
                hl_free[k] = arena_free
            following.ahead(3)
            held[:] = everything()
            residual(done, wmark, 1.0, (88, True), arena_free)

        def relu2_mlp(stream):
            stage_start(held)
            stream.ahead(3)
            wmark = load_post(a["norm_mlp_post_2"][0], 0)
            scaled = carve(NT, D)
            n_groups = MLP // 256
            ready = normed[0]
            h32 = carve(2, 2, TOK)
            h_ready, h_read = [None] * n_groups, [[] for _ in range(NH)]
            half_of = lambda g: (lambda h, j: h_hl[:, g % NH, h, j, :])
            for i in range(n_groups):
                b, pv, m = split_project_T(stream, ready)
                hv, g = h32[:, i % 2], i % NH
                m = act.do([m] + (h_ready[i - 2:i - 1] if i > 1 else []), lambda hv=hv, pv=pv: S.activation(hv, pv, ACT.Relu))
                bank_free[b] = [m]
                m = V_([m], lambda hv=hv: V.tensor_tensor(hv, hv, hv, MUL))
                h_ready[i] = split(hv, h_hl[:, g, 0], h_hl[:, g, 1], [m] + h_read[g])
                stream.ahead(3)
                g = i - 1
                if i == n_groups - 1:
                    done = split_out_last(stream, [half_of(g), half_of(i)], [[h_ready[g]], [h_ready[i]]])
                elif i:
                    h_read[g % NH] = [split_out(stream, half_of(g), i == 1, [h_ready[g]])]
                    stream.ahead(3)
            residual(done, wmark, 1.0, None)

        mixer2(mlp_stream)
        dump("x20", x[:, :, :], [])
        relu2_mlp(mlp_stream)

        assert nc.sbuf_base <= arena_base
        out_sem = sem("out_written")
        for t in range(NT):
            wm = sp.dma(x_marks[t], out_sem, 16 * (t + 1), out[0, P * t:P * t + P, :], x[:, t, :])
        sp.wait([wm] + [(s, n) for s, n in load_sems.values()])

        with nc.Block() as block:
            @block.sync
            def _(e):
                sp.play(e)

            @block.tensor
            def _(e):
                pe.play(e)

            @block.vector
            def _(e):
                dve.play(e)

            @block.scalar
            def _(e):
                act.play(e)

            @block.gpsimd
            def _(e):
                pool.play(e)


def kernel(**inputs):
    import concourse.bacc as bacc
    from concourse.bass_utils import run_bass_kernel_spmd

    nc = bacc.Bacc("TRN2", target_bir_lowering=False, num_devices=1)
    arrays = {f"in_{k}": np.ascontiguousarray(v) for k, v in inputs.items()}
    arrays["in_consts"] = shape_constants()[0]
    a = {k[3:]: nc.dram_tensor(k, v.shape, mybir.dt.from_np(v.dtype), kind="ExternalInput").ap()
         for k, v in arrays.items()}
    out = nc.dram_tensor("out_x", (1, TOK, D), F32, kind="ExternalOutput").ap()
    build(nc, a, out)
    return run_bass_kernel_spmd(nc, [arrays], core_ids=[0]).results[0]["out_x"]
```
